# Optimizing a Trainium2 kernel written in Bass

```python
import math
import jax
import jax.numpy as jnp
from jax import lax
import numpy as np

D_MODEL = 1024
BATCH = 1
SEQ = 1024
DEPTH = 1

GRID_W = 64
CTX_LEN = 256
EPS = 1e-6
HY_WIDTH = D_MODEL // 2
HY_ORDER = 2
SHORT_CONV = 3
FILT_BANDS = 8
FILT_EMB = 1 + 2 * FILT_BANDS
FILT_HIDDEN = 64
DECAY_TARGET = 1e-2
FAST_DECAY_PCT = 0.3
SLOW_DECAY_PCT = 1.5
NA_HEADS = 8
NA_HEAD_DIM = 64
NA_WIDTH = NA_HEADS * NA_HEAD_DIM
NA_WIN_H = 8
NA_WIN_W = 16
NA_COL_BLOCK = 16
NA_COL_BAND = 32
N_EXPERTS = 16
EC_CAPACITY = 2
D_FF_EXPERT = 2816
COL_Q = 3 * HY_WIDTH
COL_K = COL_Q + NA_WIDTH
COL_V = COL_K + NA_WIDTH
COL_G_HY = COL_V + NA_WIDTH
COL_G_NA = COL_G_HY + D_MODEL
P_IN = COL_G_NA + D_MODEL

kernel_name = 'hybrid_hyena_natten_ec_dit_block'

def _rmsnorm(x, g):
    x32 = x.astype(jnp.float32)
    y = x32 * lax.rsqrt(jnp.mean(x32 * x32, axis=-1, keepdims=True) + EPS)
    return y.astype(x.dtype) * g

def _modulate(h, shift, scale):
    return h * (1.0 + scale) + shift

def _heads(t):
    return t.reshape(t.shape[0], t.shape[1], NA_HEADS, NA_HEAD_DIM)

def _short_conv(u, w, b):
    L = u.shape[1]
    pad = SHORT_CONV // 2
    up = jnp.pad(u, ((0, 0), (pad, pad), (0, 0)))
    y = b
    for j in range(SHORT_CONV):
        y = y + up[:, j:j + L] * w[j]
    return y

def _hyena_filters(L, w1, b1, w2, b2, w3, freq):
    pos = jnp.arange(L, dtype=jnp.float32)
    t = pos / max(L - 1, 1)
    omega = 2.0 * math.pi * pos / L
    bands = jnp.linspace(1e-4, FILT_BANDS - 1, FILT_BANDS, dtype=jnp.float32)
    ang = omega[:, None] * bands[None, :]
    feats = jnp.concatenate([t[:, None], jnp.cos(ang), -jnp.sin(ang)], axis=-1)
    h = jnp.sin(freq * (feats @ w1 + b1))
    h = jnp.sin(freq * (h @ w2 + b2))
    h = (h @ w3).astype(jnp.float32).reshape(L, 2, HY_ORDER, HY_WIDTH)
    max_decay = math.log(DECAY_TARGET) / FAST_DECAY_PCT
    min_decay = math.log(DECAY_TARGET) / SLOW_DECAY_PCT
    deltas = jnp.linspace(min_decay, max_decay, HY_WIDTH, dtype=jnp.float32)
    decay = jnp.exp(-t[:, None] * jnp.abs(deltas)[None, :])
    return h * decay[:, None, None, :]

def _bidir_long_conv(u, h_past, h_future, skip):
    L = u.shape[1]
    k = jnp.concatenate([h_past, jnp.zeros_like(h_past[:1]), h_future[:0:-1]], axis=0)
    u32 = u.astype(jnp.float32)
    U = jnp.fft.rfft(u32, n=2 * L, axis=1)
    K = jnp.fft.rfft(k, axis=0)
    y = jnp.fft.irfft(U * K[None], n=2 * L, axis=1)[:, :L]
    return (y + u32 * skip.astype(jnp.float32)).astype(u.dtype)

def _hyena_mixer(z, short_w, short_b, skip, w1, b1, w2, b2, w3, freq):
    u = _short_conv(z, short_w, short_b)
    v, x1, x2 = jnp.split(u, 3, axis=-1)
    filt = _hyena_filters(z.shape[1], w1, b1, w2, b2, w3, freq)
    y = x1 * _bidir_long_conv(v, filt[:, 0, 0], filt[:, 1, 0], skip[0])
    y = x2 * _bidir_long_conv(y, filt[:, 0, 1], filt[:, 1, 1], skip[1])
    return y

def _na_latent(q, k, v, kc, vc, rpb):
    B, L = q.shape[0], q.shape[1]
    rows = L // GRID_W
    kh = min(NA_WIN_H, rows)
    n_cb = GRID_W // NA_COL_BLOCK
    n_loc = kh * NA_COL_BAND
    scale = NA_HEAD_DIM ** -0.5
    qg = q.reshape(B, rows, GRID_W, NA_HEADS, NA_HEAD_DIM)
    kg = k.reshape(B, rows, GRID_W, NA_HEADS, NA_HEAD_DIM)
    vg = v.reshape(B, rows, GRID_W, NA_HEADS, NA_HEAD_DIM)
    q_cols = np.arange(GRID_W).reshape(n_cb, NA_COL_BLOCK)
    band_start = np.clip(q_cols[:, 0] - NA_WIN_W // 2, 0, GRID_W - NA_COL_BAND)
    band_cols = band_start[:, None] + np.arange(NA_COL_BAND)[None, :]
    win_start = np.clip(q_cols - NA_WIN_W // 2, 0, GRID_W - NA_WIN_W)
    kcol = band_cols[:, None, :]
    in_win = (kcol >= win_start[:, :, None]) & (kcol < win_start[:, :, None] + NA_WIN_W)
    ci = np.clip(kcol - q_cols[:, :, None] + NA_WIN_W - 1, 0, 2 * NA_WIN_W - 2)

    def row_block(r):
        rs = jnp.clip(r - NA_WIN_H // 2, 0, rows - kh)
        q_r = lax.dynamic_index_in_dim(qg, r, axis=1, keepdims=False)
        q_r = q_r.reshape(B, n_cb, NA_COL_BLOCK, NA_HEADS, NA_HEAD_DIM)
        k_band = lax.dynamic_slice_in_dim(kg, rs, kh, axis=1)[:, :, band_cols]
        v_band = lax.dynamic_slice_in_dim(vg, rs, kh, axis=1)[:, :, band_cols]
        s_loc = jnp.einsum('bnqhd,bknchd->bhnqkc', q_r, k_band).astype(jnp.float32) * scale
        ri = rs + jnp.arange(kh) - r + NA_WIN_H - 1
        bias = rpb[:, ri[None, None, :, None], ci[:, :, None, :]].astype(jnp.float32)
        s_loc = jnp.where(in_win[:, :, None, :], s_loc + bias, -jnp.inf)
        s_ctx = jnp.einsum('bnqhd,bmhd->bhnqm', q_r, kc).astype(jnp.float32) * scale
        s = jnp.concatenate([s_loc.reshape(B, NA_HEADS, n_cb, NA_COL_BLOCK, n_loc), s_ctx], axis=-1)
        p = jax.nn.softmax(s, axis=-1).astype(v.dtype)
        p_loc = p[..., :n_loc].reshape(B, NA_HEADS, n_cb, NA_COL_BLOCK, kh, NA_COL_BAND)
        o = (jnp.einsum('bhnqkc,bknchd->bnqhd', p_loc, v_band)
             + jnp.einsum('bhnqm,bmhd->bnqhd', p[..., n_loc:], vc))
        return o.reshape(B, GRID_W, NA_WIDTH)

    out = lax.map(row_block, jnp.arange(rows))
    return out.transpose(1, 0, 2, 3).reshape(B, L, NA_WIDTH)

def _ctx_attention(q, k, v):
    B, M = q.shape[0], q.shape[1]
    s = jnp.einsum('bqhd,bkhd->bhqk', q, k).astype(jnp.float32) * (NA_HEAD_DIM ** -0.5)
    p = jax.nn.softmax(s, axis=-1).astype(v.dtype)
    return jnp.einsum('bhqk,bkhd->bqhd', p, v).reshape(B, M, NA_WIDTH)

def _merge(z, hy_out, na_out, w_branch_hy, w_branch_na, w_out):
    a = hy_out @ w_branch_hy
    b = na_out @ w_branch_na
    g_hy = jax.nn.sigmoid(z[..., COL_G_HY:COL_G_NA])
    g_na = jax.nn.sigmoid(z[..., COL_G_NA:P_IN])
    return (g_hy * a + g_na * b) @ w_out

def _ec_ffn(h, w_router, w_gate, w_up, w_down):
    B, L, _ = h.shape
    cap = EC_CAPACITY * L // N_EXPERTS
    aff = jax.nn.softmax((h @ w_router).astype(jnp.float32), axis=-1)
    g, idx = lax.top_k(jnp.swapaxes(aff, 1, 2), cap)
    g_e, idx_e = jnp.swapaxes(g, 0, 1), jnp.swapaxes(idx, 0, 1)
    b_ix = jnp.arange(B)[None, :, None]
    x_e = h[b_ix, idx_e]

    def expert(args):
        xe, wg, wu, wd = args
        return (jax.nn.silu(xe @ wg) * (xe @ wu)) @ wd

    y_e = lax.map(expert, (x_e, w_gate, w_up, w_down))
    return jnp.zeros_like(h).at[b_ix, idx_e].add(g_e[..., None].astype(h.dtype) * y_e)

def setup_inputs(seed: int = 0) -> dict:
    key = jax.random.key(seed)
    ks = jax.random.split(key, 28)

    def nrm(k, shape, s):
        return jax.random.normal(k, shape, jnp.float32) * s

    return {
        'x': nrm(ks[0], (BATCH, SEQ, D_MODEL), 1.0),
        'c': nrm(ks[1], (BATCH, D_MODEL), 1.0),
        'ctx': nrm(ks[2], (BATCH, CTX_LEN, D_MODEL), 1.0),
        'c_ctx': nrm(ks[3], (D_MODEL,), 1.0),
        'w_mod': nrm(ks[4], (DEPTH, D_MODEL, 6 * D_MODEL), 0.2 * D_MODEL ** -0.5),
        'b_mod': nrm(ks[5], (DEPTH, 6 * D_MODEL), 0.01),
        'norm1_g': 1.0 + nrm(ks[6], (DEPTH, D_MODEL), 0.05),
        'norm2_g': 1.0 + nrm(ks[7], (DEPTH, D_MODEL), 0.05),
        'w_in': nrm(ks[8], (DEPTH, D_MODEL, P_IN), D_MODEL ** -0.5),
        'b_in': nrm(ks[9], (DEPTH, P_IN), 0.01),
        'hy_short_w': nrm(ks[10], (DEPTH, SHORT_CONV, 3 * HY_WIDTH), 0.5),
        'hy_short_b': nrm(ks[11], (DEPTH, 3 * HY_WIDTH), 0.01),
        'hy_skip': nrm(ks[12], (DEPTH, HY_ORDER, HY_WIDTH), 0.5),
        'filt_w1': nrm(ks[13], (DEPTH, FILT_EMB, FILT_HIDDEN), FILT_EMB ** -0.5),
        'filt_b1': nrm(ks[14], (DEPTH, FILT_HIDDEN), 0.1),
        'filt_w2': nrm(ks[15], (DEPTH, FILT_HIDDEN, FILT_HIDDEN), FILT_HIDDEN ** -0.5),
        'filt_b2': nrm(ks[16], (DEPTH, FILT_HIDDEN), 0.1),
        'filt_w3': nrm(ks[17], (DEPTH, FILT_HIDDEN, 2 * HY_ORDER * HY_WIDTH), 0.005),
        'filt_freq': 1.0 + nrm(ks[18], (DEPTH, FILT_HIDDEN), 0.1),
        'na_rpb': nrm(ks[19], (DEPTH, NA_HEADS, 2 * NA_WIN_H - 1, 2 * NA_WIN_W - 1), 0.1),
        'w_branch_hy': nrm(ks[20], (DEPTH, HY_WIDTH, D_MODEL), HY_WIDTH ** -0.5),
        'w_branch_na': nrm(ks[21], (DEPTH, NA_WIDTH, D_MODEL), NA_WIDTH ** -0.5),
        'w_out': nrm(ks[22], (DEPTH, D_MODEL, D_MODEL), D_MODEL ** -0.5),
        'w_router': nrm(ks[23], (DEPTH, D_MODEL, N_EXPERTS), D_MODEL ** -0.5),
        'w_gate': nrm(ks[24], (DEPTH, N_EXPERTS, D_MODEL, D_FF_EXPERT), D_MODEL ** -0.5),
        'w_up': nrm(ks[25], (DEPTH, N_EXPERTS, D_MODEL, D_FF_EXPERT), D_MODEL ** -0.5),
        'w_down': nrm(ks[26], (DEPTH, N_EXPERTS, D_FF_EXPERT, D_MODEL), D_FF_EXPERT ** -0.5),
        'final_g': 1.0 + nrm(ks[27], (D_MODEL,), 0.05),
    }

def reference(x, c, ctx, c_ctx, w_mod, b_mod, norm1_g, norm2_g, w_in, b_in, hy_short_w, hy_short_b,
              hy_skip, filt_w1, filt_b1, filt_w2, filt_b2, filt_w3, filt_freq, na_rpb, w_branch_hy,
              w_branch_na, w_out, w_router, w_gate, w_up, w_down, final_g):
    for i in range(DEPTH):
        last = i == DEPTH - 1
        hy_params = (hy_short_w[i], hy_short_b[i], hy_skip[i], filt_w1[i], filt_b1[i],
                     filt_w2[i], filt_b2[i], filt_w3[i], filt_freq[i])
        mod_x = jax.nn.silu(c) @ w_mod[i] + b_mod[i]
        mod_c = jax.nn.silu(c_ctx) @ w_mod[i] + b_mod[i]
        sh1, sc1, g1, sh2, sc2, g2 = jnp.split(mod_x[:, None, :], 6, axis=-1)
        csh1, csc1, cg1, csh2, csc2, cg2 = jnp.split(mod_c, 6)

        hx = _modulate(_rmsnorm(x, norm1_g[i]), sh1, sc1)
        hc = _modulate(_rmsnorm(ctx, norm1_g[i]), csh1, csc1)
        zx = hx @ w_in[i] + b_in[i]
        if last:
            kvc = hc @ w_in[i][:, COL_K:COL_G_HY] + b_in[i][COL_K:COL_G_HY]
            kc, vc = (_heads(t) for t in jnp.split(kvc, 2, axis=-1))
        else:
            zc = hc @ w_in[i] + b_in[i]
            kc, vc = _heads(zc[..., COL_K:COL_V]), _heads(zc[..., COL_V:COL_G_HY])

        hy_x = _hyena_mixer(zx[..., :COL_Q], *hy_params)
        na_x = _na_latent(_heads(zx[..., COL_Q:COL_K]), _heads(zx[..., COL_K:COL_V]),
                          _heads(zx[..., COL_V:COL_G_HY]), kc, vc, na_rpb[i])
        mix_x = _merge(zx, hy_x, na_x, w_branch_hy[i], w_branch_na[i], w_out[i])

        if not last:
            hy_c = _hyena_mixer(zc[..., :COL_Q], *hy_params)
            na_c = _ctx_attention(_heads(zc[..., COL_Q:COL_K]), kc, vc)
            mix_c = _merge(zc, hy_c, na_c, w_branch_hy[i], w_branch_na[i], w_out[i])
            ctx = ctx + cg1 * mix_c
            hc2 = _modulate(_rmsnorm(ctx, norm2_g[i]), csh2, csc2)
            ctx = ctx + cg2 * _ec_ffn(hc2, w_router[i], w_gate[i], w_up[i], w_down[i])

        x = x + g1 * mix_x
        hx2 = _modulate(_rmsnorm(x, norm2_g[i]), sh2, sc2)
        x = x + g2 * _ec_ffn(hx2, w_router[i], w_gate[i], w_up[i], w_down[i])
    return _rmsnorm(x, final_g)


_drawn_inputs = setup_inputs


def setup_inputs(seed=0):
    import zlib

    import numpy as np

    out = dict(_drawn_inputs(seed))
    spreads = {}
    factors = {'ctx': 200.0,
     'c_ctx': 200.0,
     'b_mod': 8.0,
     'norm1_g': 8.0,
     'norm2_g': 200.0,
     'w_in': 3.343,
     'b_in': 57.308,
     'hy_short_w': 3.199,
     'hy_short_b': 200.0,
     'hy_skip': 4.681,
     'filt_w1': 5.504,
     'filt_b1': 8.0,
     'filt_w2': 4.722,
     'filt_b2': 8.0,
     'filt_w3': 5.602,
     'filt_freq': 8.0,
     'na_rpb': 64.0,
     'w_branch_hy': 4.155,
     'w_branch_na': 200.0,
     'w_out': 3.47,
     'w_router': 8.0,
     'w_gate': 8.0,
     'w_up': 8.0,
     'w_down': 8.0}
    for name, (base, spread) in spreads.items():
        noise = np.random.default_rng([zlib.crc32(name.encode()), seed]).standard_normal(out[name].shape)
        drawn = base * np.exp(spread * noise) if base else spread * noise
        out[name] = jnp.asarray(drawn.astype(out[name].dtype))
    for name, factor in factors.items():
        out[name] = (out[name] * factor).astype(out[name].dtype)
    return out
```

```python
import math
from contextlib import ExitStack

import numpy as np

import concourse.bass as bass
from concourse import mybir

F32 = mybir.dt.float32
F32R = mybir.dt.float32r
U32 = mybir.dt.uint32
ALU = mybir.AluOpType
ACT = mybir.ActivationFunctionType
AX_X = mybir.AxisListType.X

P = 128
T = 1024
D = 1024
CTX = 256
W = T + CTX
KD = D // P
TT = T // P
NT = W // P
EPS = 1e-6
HY = 512
HEADS, HD = 8, 64
GRID_W = 64
ROWS = T // GRID_W
WIN_H, WIN_W = 8, 16
E_N, CAP, FF = 16, 128, 2816
FC = 64
FEMB = 17
P_IN = 5 * D
NEG = -1.0e30

C_NORM1, C_BIN, C_SW, C_SB, C_SKIP, N_PAR = 0, 8, 48, 84, 96, 104

UNIT = 256
CH_UNIT = UNIT // P


class Tally:

    def __init__(self, eng, sem):
        self.eng, self.sem, self.done, self.turn = eng, sem, 0, 0

    def inc(self, ins):
        ins.then_inc(self.sem, 1)
        self.done += 1

    def wait(self):
        self.eng.wait_ge(self.sem, self.turn + self.done)

    def then_wait(self, ins):
        self.inc(ins)
        self.wait()

    def enter(self, i, per):
        self.start, self.per = self.done, per
        self.turn = i * per

    def leave(self, turns):
        assert self.done - self.start == self.per, (self.done - self.start, self.per)
        self.done, self.turn = self.start + turns * self.per, 0


class Maker:

    def __init__(self, nc, ctx, phase=""):
        self.nc, self.ctx, self.phase = nc, ctx, phase

    def sb(self, name, shape, dt=F32, side="left"):
        return self.ctx.enter_context(self.nc.sbuf_tensor(self.phase + name, shape, dt, side=side))

    def psum(self, name, shape):
        return self.ctx.enter_context(self.nc.psum_tensor(self.phase + name, shape, F32))

    def sem(self, name):
        return self.ctx.enter_context(self.nc.semaphore(name))


def inverse_root(dve, dt, act_sqrt, var, root, inv, tmp):
    act_sqrt()
    dt.then_wait(dve.reciprocal(inv, root))
    dt.then_wait(dve.tensor_tensor(tmp, var, inv, ALU.mult))
    dt.then_wait(dve.tensor_tensor(tmp, tmp, inv, ALU.mult))
    dt.then_wait(dve.tensor_scalar(tmp, tmp, -0.5, 1.5, ALU.mult, ALU.add))
    dt.then_wait(dve.tensor_tensor(inv, inv, tmp, ALU.mult))


def modulate_and_norm(nc, sems, a, keep):
    h_hi, h_lo, par, ident = keep["h_hi"], keep["h_lo"], keep["par"], keep["ident"]
    NC = 6 * D // 512
    with ExitStack() as ctx:
        m = Maker(nc, ctx, "norm_")
        x_raw = m.sb("x_raw", [P, NT, D])
        w_mod = m.sb("w_mod", [P, 2, KD, 512])
        mod_row = m.sb("mod_row", [2, NC, 512])
        par_rows = m.sb("par_rows", [N_PAR, P])
        c_col = m.sb("c_col", [P, 2, KD])
        c_silu = m.sb("c_silu", [P, KD, 2])
        ss = m.sb("ss", [P, NT])
        var = m.sb("var", [P, NT])
        root = m.sb("root", [P, NT])
        inv = m.sb("inv", [P, NT])
        tmp = m.sb("tmp", [P, NT])
        scale_col = m.sb("scale_col", [P, 2, KD])
        shift_col = m.sb("shift_col", [P, 2, KD])
        h_full = m.sb("h_full", [P, 2, 512])
        ps_mod = m.psum("ps_mod", [P, 2, 512])
        ps_col = m.psum("ps_col", [P, 512])
        ps_x = m.psum("ps_x", [P, 4, 512])

        rows_in, c_in, x_in, b_in = (sems(n) for n in ("par_rows_in", "c_in", "x_in", "b_mod_in"))
        w_in = [sems(f"w_mod_in{s}") for s in range(2)]
        silu_ready, mod_done, mod_row_ready = (
            sems(n) for n in ("silu_ready", "mod_done", "mod_row_ready"))
        par_done, col_done, dve_step, sq_done, root_done = (
            sems(n) for n in ("par_done", "col_done", "a_dve_step", "sq_done", "root_done"))
        xn_ready, xt_done, full_ready, lo_done, mod_out = (
            sems(n) for n in ("xn_ready", "xt_done", "full_ready", "h_lo_done", "mod_out"))
        cols_ready, var_ready = sems("cols_ready"), sems("var_ready")

        groups = [(0, 4, 0), (4, 4, 0), (8, 2, 1)]
        fills = [(k, g) for k in range(KD) for g in range(3)]

        with nc.Block() as block:

            @block.sync
            def _(sp):
                for n, (name, lo, hi) in enumerate((("norm1_g", C_NORM1, C_BIN), ("b_in", C_BIN, C_SW),
                                                    ("hy_short_w", C_SW, C_SB), ("hy_short_b", C_SB, C_SKIP),
                                                    ("hy_skip", C_SKIP, N_PAR))):
                    sp.dma_start(par_rows[lo:hi, :], a[name]).then_inc(rows_in, 16)
                sp.dma_start(ident[:], a["ident"]).then_inc(rows_in, 16)
                for j, name in enumerate(("c", "c_ctx")):
                    sp.dma_start(c_col[:, j, :], a[name].rearrange("(p k) -> p k", k=KD)).then_inc(c_in, 16)
                    sp.dma_start(mod_row[j:j + 1, :, :], a["b_mod"].rearrange("(o n c) -> o n c", o=1, c=512)
                                 ).then_inc(b_in, 16)
                w_src = a["w_mod"].rearrange("(p k) (n c) -> n p k c", k=KD, c=512)
                with sp.Fori(0, NC // 2) as i:
                    for s in range(2):
                        sp.wait_ge(mod_done, 2 * i + s + 1)
                        sp.dma_start(w_mod[:, s], w_src[2 * i + s]).then_inc(w_in[s], 16)
                sp.dma_start(x_raw[:, 0:TT, :], a["x"].rearrange("(t p) d -> p t d", p=P)).then_inc(x_in, 16)
                sp.dma_start(x_raw[:, TT:NT, :], a["ctx"].rearrange("(t p) d -> p t d", p=P)).then_inc(x_in, 16)
                sp.wait_ge(mod_row_ready, NC + 2)
                sp.dma_start(a["mod_d"].rearrange("j (n c) -> j n c", c=512), mod_row[:]).then_inc(mod_out, 16)
                sp.wait_ge(mod_out, 16)

            @block.tensor
            def _(pe):
                pe.sem_inc(mod_done, 2)
                pe.wait_ge(rows_in, 6 * 16)
                pe.transpose(ps_col[:, 0:N_PAR], par_rows[:], ident[0:N_PAR, 0:N_PAR]).then_inc(par_done, 1)
                pe.wait_ge(silu_ready, 1)
                with pe.Fori(0, NC // 2) as i:
                    for s in range(2):
                        pe.wait_ge(w_in[s], 16 * i + 16)
                        pe.wait_ge(mod_row_ready, 2 * i + s + 1)
                        for k in range(KD):
                            mm = pe.matmul(ps_mod[0:2, s, :], c_silu[:, k, :], w_mod[:, s, k, :],
                                           start=(k == 0), stop=(k == KD - 1))
                        mm.then_inc(mod_done, 1)
                pe.wait_ge(mod_row_ready, NC + 2)
                pe.wait_ge(cols_ready, 1)
                flat = mod_row[:].rearrange("j n c -> j (n c)")
                for k in range(2 * KD):
                    mm = pe.transpose(ps_col[:, 2 * k:2 * k + 2], flat[:, k * P:(k + 1) * P], ident[0:2, 0:2])
                mm.then_inc(col_done, 1)
                pe.wait_ge(xn_ready, NT)
                for n, (k, g) in enumerate(fills):
                    t0, nt, _ = groups[g]
                    if n >= 4:
                        pe.wait_ge(full_ready, n - 3)
                    for t in range(nt):
                        mm = pe.transpose(ps_x[:, n % 4, t * P:(t + 1) * P],
                                          x_raw[:, t0 + t, k * P:(k + 1) * P], ident[:])
                    mm.then_inc(xt_done, 1)

            @block.scalar
            def _(act):
                act.wait_ge(c_in, 32)
                act.activation(c_silu[:].rearrange("p k j -> p j k"), c_col[:], ACT.Silu).then_inc(silu_ready, 1)
                act.wait_ge(x_in, 32)
                for t in range(NT):
                    if t:
                        act.wait_ge(sq_done, t)
                    act.activation(h_full[:].rearrange("p a b -> p (a b)"), x_raw[:, t, :], ACT.Square, accum_out=ss[:, t:t + 1]).then_inc(sq_done, 1)
                act.wait_ge(var_ready, 1)
                act.activation(root[:], var[:], ACT.Sqrt).then_inc(root_done, 1)
                act.wait_ge(cols_ready, 2)
                for n, (k, g) in enumerate(fills):
                    t0, nt, j = groups[g]
                    cols = slice(t0 * P, (t0 + nt) * P)
                    sc, sh = scale_col[:, j, k:k + 1], shift_col[:, j, k:k + 1]
                    act.wait_ge(xt_done, n + 1)
                    act.activation(h_hi[:, k, cols], ps_x[:, n % 4, 0:nt * P], ACT.Identity, bias=sh, scale=sc)
                    if n >= 2:
                        act.wait_ge(lo_done, n - 1)
                    act.activation(h_full[:, n % 2, 0:nt * P], ps_x[:, n % 4, 0:nt * P], ACT.Identity,
                                   bias=sh, scale=sc).then_inc(full_ready, 1)

            @block.vector
            def _(dve):
                dt = Tally(dve, dve_step)
                dve.sem_inc(mod_row_ready, 2)
                dve.wait_ge(par_done, 1)
                dve.tensor_copy(par[:], ps_col[:, 0:N_PAR]).then_inc(cols_ready, 1)
                dve.wait_ge(b_in, 32)
                with dve.Fori(0, NC // 2) as i:
                    for s in range(2):
                        dve.wait_ge(mod_done, 2 * i + s + 3)
                        dve.tensor_tensor(mod_row[:, 2 * i + s, :], ps_mod[0:2, s, :], mod_row[:, 2 * i + s, :],
                                          ALU.add).then_inc(mod_row_ready, 1)
                dve.wait_ge(col_done, 1)
                dve.wait_ge(cols_ready, 1)
                col = ps_col[:, 0:4 * KD].rearrange("p (w k j) -> p w j k", w=2, j=2)
                dve.tensor_copy(shift_col[:], col[:, 0])
                for j in range(2):
                    ins = dve.scalar_tensor_tensor(out=scale_col[:, j, :], in0=col[:, 1, j, :], scalar=1.0,
                                                   in1=par[:, C_NORM1:C_BIN], op0=ALU.add, op1=ALU.mult)
                ins.then_inc(cols_ready, 1)
                dve.wait_ge(sq_done, NT)
                dve.tensor_scalar(var[:], ss[:], 1.0 / D, EPS, ALU.mult, ALU.add).then_inc(var_ready, 1)
                inverse_root(dve, dt, lambda: dve.wait_ge(root_done, 1), var[:], root[:], inv[:], tmp[:])
                for t in range(NT):
                    dve.tensor_scalar(x_raw[:, t, :], x_raw[:, t, :], inv[:, t:t + 1], None, ALU.mult
                                      ).then_inc(xn_ready, 1)
                for n, (k, g) in enumerate(fills):
                    t0, nt, _ = groups[g]
                    cols = slice(t0 * P, (t0 + nt) * P)
                    dve.wait_ge(full_ready, n + 1)
                    dve.tensor_tensor(h_lo[:, k, cols], h_full[:, n % 2, 0:nt * P], h_hi[:, k, cols].bitcast(F32),
                                      ALU.subtract).then_inc(lo_done, 1)


SEG_HY, SEG_Q, SEG_K, SEG_V, SEG_G = (0, 6), (6, 2), (8, 2), (10, 2), (12, 8)
N_UNITS = P_IN // UNIT


def project(nc, sems, a, keep, v_tok):
    h_hi, h_lo, par = keep["h_hi"], keep["h_lo"], keep["par"]
    with ExitStack() as ctx:
        m = Maker(nc, ctx, "proj_")
        w_raw = m.sb("w_raw", [P, 2, KD, UNIT])
        w_hi = m.sb("w_hi", [P, 2, KD, UNIT], F32R)
        w_lo = m.sb("w_lo", [P, 2, KD, UNIT], F32R)
        z_pad = m.sb("z_pad", [P, 2, T + 2])
        conv = m.sb("conv", [P, 2, T])
        stage = m.sb("stage", [P, 2, W])
        q_bias = m.sb("q_bias", [P, 4])
        bias = m.sb("bias", [P, CH_UNIT])
        bv_row = m.sb("bv_row", [1, 512])
        ones = m.sb("ones", [1, P])
        ps = m.psum("ps", [P, 8, 512])

        w_in = [sems(f"w_in{s}") for s in range(2)]
        hi_ready, lo_ready, z_done, evacuated, conv_ready = (
            sems(n) for n in ("w_hi_ready", "w_lo_ready", "z_done", "evacuated", "conv_ready"))
        stored = [sems(f"stored{s}") for s in range(2)]
        b_dve, bv_in, const_ready, bias_ready = (
            sems(n) for n in ("b_dve_step", "bv_in", "const_ready", "bias_ready"))

        n_q = 4 * SEG_HY[1]
        n_k = n_q + 4 * SEG_Q[1]
        n_v = n_k + 5 * SEG_K[1]
        n_g = n_v + 5 * SEG_V[1]

        with nc.Block() as block:

            @block.sync
            def _(sp):
                src = a["w_in"].rearrange("(k p) (u n) -> u p k n", p=P, n=UNIT)
                u_d = a["u_d"].rearrange("(c p) t -> c p t", p=P)
                qk_d = a["qk_d"].rearrange("(c p) t -> c p t", p=P)
                g_d = a["g_d"].rearrange("(c p) t -> c p t", p=P)

                def load(u, s):
                    sp.wait_ge(lo_ready, u + 1)
                    sp.dma_start(w_raw[:, s], src[u]).then_inc(w_in[s], 16)

                def store_conv(u):
                    for c in range(CH_UNIT):
                        sp.wait_ge(conv_ready, CH_UNIT * u + c + 3)
                        sp.dma_start(u_d[CH_UNIT * u + c], conv[:, c, :]).then_inc(stored[c], 16)

                def store_stage(n, dst, c0, cols):
                    for c in range(CH_UNIT):
                        sp.wait_ge(evacuated, n + (5 if cols == W else 2 * c + 2) + 8)
                        sp.dma_start(dst[c0 + c, :, 0:cols], stage[:, c, 0:cols]).then_inc(stored[c], 16)

                sp.sem_inc(stored[0], 16)
                sp.sem_inc(stored[1], 16)
                sp.dma_start(bv_row[:], a["b_in"].rearrange("(o r) c -> o (r c)", o=1)[:, 5 * 512:6 * 512]
                             ).then_inc(bv_in, 16)
                load(0, 0)
                load(1, 1)
                with sp.Fori(0, SEG_HY[1] // 2) as i:
                    for s in range(2):
                        load(2 * i + s + 2, s)
                        store_conv(2 * i + s)
                for s in range(2):
                    load(SEG_Q[0] + s + 2, s)
                    store_stage(n_q + 4 * s, qk_d, CH_UNIT * s, T)
                for s in range(2):
                    load(SEG_K[0] + s + 2, s)
                    store_stage(n_k + 5 * s, qk_d, 4 + CH_UNIT * s, W)
                for s in range(2):
                    load(SEG_V[0] + s + 2, s)
                with sp.Fori(0, SEG_G[1] // 2 - 1) as i:
                    for s in range(2):
                        load(SEG_G[0] + 2 * i + s + 2, s)
                        store_stage(n_g + 8 * i + 4 * s, g_d, 4 * i + CH_UNIT * s, T)
                for s in range(2):
                    store_stage(n_g + 24 + 4 * s, g_d, 12 + CH_UNIT * s, T)
                for s in range(2):
                    sp.wait_ge(stored[s], 16 * (6 + 2 + 2 + 8 + 1))

            @block.tensor
            def _(pe):
                pe.sem_inc(z_done, 4)

                def begin(u):
                    pe.wait_ge(lo_ready, u + 3)

                def latents(s, n, n8):
                    for c in range(CH_UNIT):
                        banks = [(n8 + 2 * c + th) % 8 for th in range(2)]
                        pe.wait_ge(evacuated, n + 2 * c + 2)
                        for k in range(KD):
                            hi, lo = (w[:, s, k, c * P:(c + 1) * P] for w in (w_hi, w_lo))
                            for w, h, first, last in ((hi, h_hi, True, False), (hi, h_lo, False, False),
                                                      (lo, h_hi, False, True)):
                                for th in range(2):
                                    mm = pe.matmul(ps[:, banks[th], :], w, h[:, k, th * 512:(th + 1) * 512],
                                                   start=(k == 0 and first), stop=(k == KD - 1 and last))
                                    if k == KD - 1 and last:
                                        mm.then_inc(z_done, 1)

                with pe.Fori(0, SEG_HY[1] // 2) as i:
                    for s in range(2):
                        begin(2 * i + s)
                        latents(s, 8 * i + 4 * s, 4 * s)
                for s in range(2):
                    begin(SEG_Q[0] + s)
                    latents(s, n_q + 4 * s, (n_q + 4 * s) % 8)
                for s in range(2):
                    n = n_k + 5 * s
                    begin(SEG_K[0] + s)
                    latents(s, n, n % 8)
                    n += 4
                    pe.wait_ge(evacuated, n + 1)
                    for c in range(CH_UNIT):
                        for k in range(KD):
                            for x, (w, h) in enumerate(((w_hi, h_hi), (w_hi, h_lo), (w_lo, h_hi))):
                                mm = pe.matmul(ps[:, n % 8, c * CTX:(c + 1) * CTX], w[:, s, k, c * P:(c + 1) * P],
                                               h[:, k, T:W], start=(k == 0 and x == 0), stop=(k == KD - 1 and x == 2))
                    mm.then_inc(z_done, 1)
                pe.wait_ge(bv_in, 16)
                pe.wait_ge(const_ready, 1)
                for s in range(2):
                    begin(SEG_V[0] + s)
                    for tp in range(NT // 2):
                        n = n_v + 5 * s + tp
                        pe.wait_ge(evacuated, n + 1)
                        for t in range(2):
                            o = ps[:, n % 8, t * UNIT:(t + 1) * UNIT]
                            tok = slice((2 * tp + t) * P, (2 * tp + t + 1) * P)
                            pe.matmul(o, ones[:], bv_row[:, s * UNIT:(s + 1) * UNIT], start=True, stop=False)
                            for k in range(KD):
                                for x, (w, h) in enumerate(((w_hi, h_hi), (w_lo, h_hi), (w_hi, h_lo))):
                                    mm = pe.matmul(o, h[:, k, tok], w[:, s, k, :], start=False,
                                                   stop=(k == KD - 1 and x == 2))
                        mm.then_inc(z_done, 1)
                with pe.Fori(0, SEG_G[1] // 2) as i:
                    for s in range(2):
                        begin(SEG_G[0] + 2 * i + s)
                        latents(s, n_g + 8 * i + 4 * s, (n_g + 4 * s) % 8)

            @block.scalar
            def _(act):
                act.sem_inc(evacuated, 8)

                def split(s, i, before):
                    act.wait_ge(w_in[s], 16 * i + 16)
                    if before is not None:
                        act.wait_ge(z_done, before + 4)
                    act.activation(w_hi[:, s], w_raw[:, s], ACT.Copy).then_inc(hi_ready, 1)

                def evacuate(n, bank, out, func, bias, scale=1.0):
                    act.wait_ge(z_done, n + 5)
                    act.activation(out, ps[:, bank, :], func, bias=bias, scale=scale).then_inc(evacuated, 1)

                def own_bias(c, ch, count):
                    act.activation(bias[:, c:c + 1], par[:, bass.ds(C_BIN + ch, 1)], ACT.Copy).then_inc(bias_ready, 1)
                    act.wait_ge(bias_ready, count)
                    return bias[:, c:c + 1]

                act.wait_ge(const_ready, 2)
                split(0, 0, None)
                with act.Fori(0, SEG_HY[1] // 2) as i:
                    for s in range(2):
                        split(1 - s, i + s, 8 * i + 4 * s)
                        for c in range(CH_UNIT):
                            ch = 4 * i + 2 * s + c
                            b = own_bias(c, ch, ch + 1)
                            act.wait_ge(conv_ready, ch + 1)
                            for th in range(2):
                                evacuate(8 * i + 4 * s + 2 * c + th, 4 * s + 2 * c + th,
                                         z_pad[:, c, 1 + th * 512:1 + (th + 1) * 512], ACT.Identity, b)
                for s in range(2):
                    n = n_q + 4 * s
                    split(1 - s, (SEG_Q[0] + s + 1) // 2, n)
                    for c in range(CH_UNIT):
                        ch = CH_UNIT * s + c
                        act.wait_ge(stored[c], 16 * (7 + s))
                        for th in range(2):
                            evacuate(n, n % 8, stage[:, c, th * 512:(th + 1) * 512], ACT.Identity,
                                     q_bias[:, ch:ch + 1], HD ** -0.5)
                            n += 1
                for s in range(2):
                    n = n_k + 5 * s
                    split(1 - s, (SEG_K[0] + s + 1) // 2, n)
                    biases = [par[:, b:b + 1] for b in range(C_BIN + 16 + CH_UNIT * s, C_BIN + 18 + CH_UNIT * s)]
                    for c in range(CH_UNIT):
                        act.wait_ge(stored[c], 16 * (9 + s))
                        for th in range(2):
                            evacuate(n, n % 8, stage[:, c, th * 512:(th + 1) * 512], ACT.Identity, biases[c])
                            n += 1
                    act.wait_ge(z_done, n + 5)
                    for c in range(CH_UNIT):
                        ins = act.activation(stage[:, c, T:W], ps[:, n % 8, c * CTX:(c + 1) * CTX],
                                             ACT.Identity, bias=biases[c])
                    ins.then_inc(evacuated, 1)
                for s in range(2):
                    split(1 - s, (SEG_V[0] + s + 1) // 2, n_v + 5 * s)
                    for tp in range(NT // 2):
                        n = n_v + 5 * s + tp
                        act.wait_ge(z_done, n + 5)
                        act.activation(v_tok[:, 2 * tp:2 * tp + 2, s * UNIT:(s + 1) * UNIT],
                                       ps[:, n % 8, :].rearrange("p (t c) -> p t c", t=2), ACT.Copy
                                       ).then_inc(evacuated, 1)

                def gates(i, s, last=False):
                    u = 2 * i + s
                    if not last:
                        split(1 - s, SEG_G[0] // 2 + i + s, n_g + 4 * u)
                    for c in range(CH_UNIT):
                        b = own_bias(c, 24 + 2 * u + c, 12 + 2 * u + c + 1)
                        act.wait_ge(stored[c], 16 * (11 + u))
                        for th in range(2):
                            evacuate(n_g + 4 * u + 2 * c + th, (n_g + 4 * s + 2 * c + th) % 8,
                                     stage[:, c, th * 512:(th + 1) * 512], ACT.Sigmoid, b)

                with act.Fori(0, SEG_G[1] // 2 - 1) as i:
                    for s in range(2):
                        gates(i, s)
                gates(SEG_G[1] // 2 - 1, 0)
                gates(SEG_G[1] // 2 - 1, 1, last=True)

            @block.vector
            def _(dve):
                dt = Tally(dve, b_dve)
                dve.sem_inc(lo_ready, 2)
                dve.sem_inc(conv_ready, 2)
                dt.inc(dve.memset(z_pad[:, :, 0:1], 0.0))
                dt.inc(dve.memset(z_pad[:, :, T + 1:T + 2], 0.0))
                dve.memset(ones[:], 1.0).then_inc(const_ready, 1)
                dve.tensor_scalar(q_bias[:], par[:, C_BIN + 12:C_BIN + 16], HD ** -0.5, None, ALU.mult
                                  ).then_inc(const_ready, 1)
                dt.wait()

                def split(u, s):
                    dve.wait_ge(hi_ready, u + 1)
                    dve.tensor_tensor(w_lo[:, s], w_raw[:, s], w_hi[:, s].bitcast(F32), ALU.subtract
                                      ).then_inc(lo_ready, 1)

                split(0, 0)
                with dve.Fori(0, SEG_HY[1] // 2) as i:
                    dt.enter(i, 8)
                    for s in range(2):
                        split(2 * i + s + 1, 1 - s)
                        for c in range(CH_UNIT):
                            ch = 4 * i + 2 * s + c

                            def w(j):
                                return par[:, bass.ds(C_SW + 12 * j + ch, 1)]

                            dve.wait_ge(evacuated, 2 * ch + 2 + 8)
                            dve.wait_ge(stored[c], 16 * (2 * i + s + 1))
                            dt.then_wait(dve.tensor_scalar(conv[:, c], z_pad[:, c, 1:T + 1], w(1),
                                                           par[:, bass.ds(C_SB + ch, 1)], ALU.mult, ALU.add))
                            dt.then_wait(dve.scalar_tensor_tensor(out=conv[:, c], in0=z_pad[:, c, 0:T], scalar=w(0),
                                                                  in1=conv[:, c], op0=ALU.mult, op1=ALU.add))
                            dve.scalar_tensor_tensor(out=conv[:, c], in0=z_pad[:, c, 2:T + 2], scalar=w(2),
                                                     in1=conv[:, c], op0=ALU.mult, op1=ALU.add
                                                     ).then_inc(conv_ready, 1)
                    dt.leave(SEG_HY[1] // 2)
                for u in range(SEG_Q[0] + 1, SEG_G[0] + 1):
                    split(u, u % 2)
                with dve.Fori(0, SEG_G[1] // 2 - 1) as i:
                    for s in range(2):
                        split(SEG_G[0] + 2 * i + s + 1, 1 - s)
                split(N_UNITS - 1, 1)



def key_rows(i):
    rs = [min(max(r - WIN_H // 2, 0), ROWS - WIN_H) for r in (2 * i, 2 * i + 1)]
    return rs[0], rs[1] + WIN_H - rs[0]


T_ROWS = 14
T_MIN = -6
HALF = P // 2
CTX0 = 5 * P


def attend(nc, sems, a, keep, v_tok, na_t):
    ident = keep["ident"]
    with ExitStack() as ctx:
        m = Maker(nc, ctx, "attn_")
        q_raw = m.sb("q_raw", [P, T])
        k_raw = m.sb("k_raw", [P, W])
        q_hi, q_lo = m.sb("q_hi", [P, T], F32R), m.sb("q_lo", [P, T], F32R)
        k_hi, k_lo = m.sb("k_hi", [P, W], F32R), m.sb("k_lo", [P, W], F32R)
        t_raw = m.sb("t_raw", [P, 2, T_ROWS, GRID_W])
        table = m.sb("table", [P, 2, T_ROWS, GRID_W])
        edged = m.sb("edged", [P, 2, WIN_H + 1, GRID_W])
        mask = m.sb("mask", [P, GRID_W])
        score = m.sb("score", [P, 2, (WIN_H + 1) * GRID_W])
        prob = m.sb("prob", [P, 2, CTX0 + CTX])
        prob_t = m.sb("prob_t", [P, 2, 7, P])
        top = m.sb("top", [P, 2, 3])
        sums = m.sb("sums", [P, 4, 4])
        na = m.sb("na", [P, 2, P])
        ps_s = m.psum("ps_s", [P, 2, 1024])
        ps_t = m.psum("ps_t", [P, 2, 512])
        ps_o = m.psum("ps_o", [P, 2, 512])

        qk_in, t_in, mask_in = (sems(n) for n in ("qk_in", "t_in", "mask_in"))
        qk_hi, qk_lo, tables, scored, max_ready, exps, turned = (
            sems(n) for n in ("qk_hi", "qk_lo", "tables", "scored", "max_ready", "exps", "turned"))
        copied_a, copied_b, filled, used, step, zeros = (
            sems(n) for n in ("copied_a", "copied_b", "filled", "used", "c_dve_step", "zeros"))
        PAIRS, UNITS, STEPS = HEADS // 2, 2 * TT, 2 * TT + 4

        FILLS = UNITS + TT

        def f_unit(n):
            return n + max(n - 1, 0) // 2

        def f_turn(i):
            return min(3 * i + 3, FILLS - 1)

        def blocks(i):
            r0, n = key_rows(i)
            out = [(b, r0 // 2 + b) for b in range(n // 2)]
            if n % 2:
                out.append((4, r0 // 2 + 4))
            return out

        with nc.Block() as block:

            @block.sync
            def _(sp):
                qk = a["qk_d"].rearrange("(w j p) t -> w j p t", w=2, p=P)
                sp.dma_start(mask[:], a["na_mask"]).then_inc(mask_in, 16)
                for j in range(PAIRS):
                    sp.wait_ge(qk_lo, j + 1)
                    sp.dma_start(q_raw[:], qk[0, j][:, 0:T]).then_inc(qk_in, 16)
                    sp.dma_start(k_raw[:], qk[1, j]).then_inc(qk_in, 16)
                    sp.wait_ge(tables, j + 1)
                    rpb = a["rpb"]
                    for hh in range(2):
                        for half in range(2):
                            src = bass.AP(rpb.tensor, ((2 * j + hh) * 15 + 1 - half) * P + 1,
                                          [[1, GRID_W], [P, T_ROWS], [1, GRID_W]])
                            sp.dma_start(t_raw[half * HALF:(half + 1) * HALF, hh], src).then_inc(t_in, 16)

            @block.tensor
            def _(pe):
                pe.sem_inc(scored, 1)
                pe.sem_inc(turned, 2)
                pe.sem_inc(filled, 2)
                with pe.Fori(0, PAIRS) as j:
                    pe.wait_ge(qk_lo, j + 2)
                    for s in range(STEPS):
                        if s < UNITS:
                            i, hh = s // 2, s % 2
                            r0, rows = key_rows(i)
                            part = slice(hh * HALF, (hh + 1) * HALF)
                            cols = [(0, r0 * GRID_W, 512), (512, T, CTX)]
                            if rows > WIN_H:
                                cols = [(0, r0 * GRID_W, 512), (512, r0 * GRID_W + 512, GRID_W), (576, T, CTX)]
                            pe.wait_ge(exps, UNITS * j + s + 1)
                            for o, c, w in cols:
                                for x, (q, k) in enumerate(((q_hi, k_hi), (q_hi, k_lo), (q_lo, k_hi))):
                                    mm = pe.matmul(ps_s[:, s % 2, o:o + w], q[part, i * P:(i + 1) * P],
                                                   k[part, c:c + w], start=(x == 0), stop=(x == 2))
                            mm.then_inc(scored, 1)
                        if 1 <= s <= UNITS:
                            n = s - 1
                            pe.wait_ge(exps, UNITS * j + n + 3)
                            pe.wait_ge(copied_a, UNITS * j + n + 1)
                            pe.wait_ge(copied_b, UNITS * j + n + 1)
                            for b, _ in blocks(n // 2) + [(5, 0), (6, 0)]:
                                mm = pe.transpose(ps_t[:, b // 4, (b % 4) * P:(b % 4 + 1) * P],
                                                  prob[:, n % 2, b * P:(b + 1) * P], ident[:])
                            mm.then_inc(turned, 1)
                        if 2 <= s <= UNITS + 1:
                            n = s - 2
                            pe.wait_ge(copied_a, UNITS * j + n + 2)
                            pe.wait_ge(copied_b, UNITS * j + n + 2)
                            f = f_unit(n)
                            pe.wait_ge(used, FILLS * j + f + 1)
                            todo = blocks(n // 2) + [(5, TT), (6, TT + 1)]
                            for x, (b, tile) in enumerate(todo):
                                mm = pe.matmul(ps_o[:, f % 2, 0:HD], prob_t[:, n % 2, b, :],
                                               v_tok[:, tile, bass.ds(j * P + (n % 2) * HD, HD)],
                                               start=(x == 0), stop=(x == len(todo) - 1))
                            mm.then_inc(filled, 1)
                        if s >= 4 and s % 2 == 0:
                            i = s // 2 - 2
                            f = f_turn(i)
                            pe.wait_ge(used, FILLS * j + max(f_unit(2 * i + 1) + 3, f + 1))
                            pe.transpose(ps_o[:, f % 2, 0:P], na[:, i % 2, :], ident[:]).then_inc(filled, 1)

            @block.scalar
            def _(act):
                act.sem_inc(exps, 2)
                act.sem_inc(copied_b, 1)
                act.wait_ge(zeros, 1)
                with act.Fori(0, PAIRS) as j:
                    act.wait_ge(qk_in, 32 * j + 32)
                    act.wait_ge(scored, UNITS * j + 1)
                    act.activation(q_hi[:], q_raw[:], ACT.Copy)
                    act.activation(k_hi[:], k_raw[:], ACT.Copy).then_inc(qk_hi, 1)
                    for s in range(UNITS + 1):
                        if s >= 1:
                            n = s - 1
                            lo = 4 if key_rows(n // 2)[1] > WIN_H else 5
                            act.wait_ge(turned, UNITS * j + n + 3)
                            act.wait_ge(filled, FILLS * j + (f_unit(n - 2) + 3 if n >= 2 else 2))
                            act.activation(prob_t[:, n % 2, lo:7, :], ps_t[:, 1, (lo - 4) * P:3 * P].rearrange(
                                "p (b q) -> p b q", q=P), ACT.Copy).then_inc(copied_b, 1)
                        if s < UNITS:
                            n, w = s, key_rows(s // 2)[1] * GRID_W
                            act.wait_ge(max_ready, UNITS * j + n + 1)
                            act.wait_ge(turned, UNITS * j + n + 1)
                            act.activation(prob[:, n % 2, 0:w], score[:, n % 2, 0:w], ACT.Exp,
                                           bias=top[:, n % 2, 2:3], accum_out=sums[:, n % 4, 0:1])
                            act.activation(prob[:, n % 2, CTX0:CTX0 + CTX], ps_s[:, n % 2, w:w + CTX], ACT.Exp,
                                           bias=top[:, n % 2, 2:3], accum_out=sums[:, n % 4, 1:2]).then_inc(exps, 1)

            @block.vector
            def _(dve):
                dt = Tally(dve, step)
                dve.sem_inc(qk_lo, 1)
                dve.sem_inc(tables, 1)
                dve.sem_inc(copied_a, 1)
                dve.sem_inc(used, 2)
                dve.memset(prob[:, :, 9 * GRID_W:CTX0], 0.0).then_inc(zeros, 1)
                dve.wait_ge(mask_in, 16)
                with dve.Fori(0, PAIRS) as j:
                    dt.enter(j, 4 + 4 * UNITS)
                    dve.wait_ge(qk_hi, j + 1)
                    dve.tensor_tensor(q_lo[:], q_raw[:], q_hi[:].bitcast(F32), ALU.subtract)
                    dve.tensor_tensor(k_lo[:], k_raw[:], k_hi[:].bitcast(F32), ALU.subtract).then_inc(qk_lo, 1)
                    dve.wait_ge(t_in, 64 * j + 64)
                    for hh in range(2):
                        dt.inc(dve.tensor_tensor(table[:, hh], t_raw[:, hh, :, ::-1], mask[:].unsqueeze(1).broadcast_to(
                            [P, T_ROWS, GRID_W]), ALU.add))
                    dt.wait()
                    dve.tensor_copy(edged[:], table[:, :, -WIN_H // 2 - T_MIN:WIN_H // 2 + 1 - T_MIN]).then_inc(tables, 1)
                    dve.wait_ge(tables, j + 2)
                    dt.inc(dve.memset(edged[0:HALF, :, WIN_H], NEG))
                    dt.inc(dve.memset(edged[HALF:P, :, 0], NEG))
                    dt.wait()
                    for s in range(STEPS + 1):
                        if s < UNITS:
                            n, i, hh = s, s // 2, s % 2
                            r0, rows = key_rows(i)
                            w = rows * GRID_W
                            first = r0 - 2 * i - T_MIN
                            bias = edged[:, hh] if rows > WIN_H else table[:, hh, first:first + WIN_H]
                            dve.wait_ge(scored, UNITS * j + n + 2)
                            dt.inc(dve.reduce_max(top[:, n % 2, 1:2], ps_s[:, n % 2, w:w + CTX], AX_X))
                            dt.then_wait(dve.tensor_tensor_reduce(score[:, n % 2, 0:w], ps_s[:, n % 2, 0:w],
                                                                 bias.rearrange("p r c -> p (r c)"), 1.0, -3.0e38,
                                                                 ALU.add, ALU.max, top[:, n % 2, 0:1]))
                            dve.tensor_scalar(top[:, n % 2, 2:3], top[:, n % 2, 0:1], top[:, n % 2, 1:2], -1.0,
                                              ALU.max, ALU.mult).then_inc(max_ready, 1)
                        if 1 <= s <= UNITS:
                            n = s - 1
                            dve.wait_ge(turned, UNITS * j + n + 3)
                            dve.wait_ge(filled, FILLS * j + (f_unit(n - 2) + 3 if n >= 2 else 2))
                            dve.tensor_copy(prob_t[:, n % 2, 0:4, :], ps_t[:, 0, :].rearrange(
                                "p (b q) -> p b q", q=P)).then_inc(copied_a, 1)
                        if s >= 5 and s % 2 == 1:
                            i = (s - 5) // 2
                            f = f_turn(i)
                            dve.wait_ge(filled, FILLS * j + f + 3)
                            dve.tensor_scalar(na_t[:, j, i * P:(i + 1) * P], ps_o[:, f % 2, 0:P], 1.0, None,
                                              ALU.mult).then_inc(used, 1)
                        if 2 <= s <= UNITS + 1:
                            n, i = s - 2, (s - 2) // 2
                            f = f_unit(n)
                            dt.then_wait(dve.tensor_tensor(sums[:, n % 4, 2:3], sums[:, n % 4, 0:1],
                                                           sums[:, n % 4, 1:2], ALU.add))
                            dt.then_wait(dve.reciprocal(sums[:, n % 4, 3:4], sums[:, n % 4, 2:3]))
                            dve.wait_ge(filled, FILLS * j + f + 3)
                            dve.tensor_scalar(na[:, i % 2, (n % 2) * HD:(n % 2 + 1) * HD], ps_o[:, f % 2, 0:HD],
                                              sums[:, n % 4, 3:4], None, ALU.mult).then_inc(used, 1)
                    dt.leave(PAIRS)


BLK = 256
NB = T // BLK
TWO_PI_HI = 6.28125
TWO_PI_LO = 2.0 * math.pi - TWO_PI_HI
ROUND = 1.5 * 2.0 ** 23


def hyena(nc, sems, a, keep, y_t):
    par, ident = keep["par"], keep["ident"]
    with ExitStack() as ctx:
        m = Maker(nc, ctx, "hyena_")
        feats = m.sb("feats", [FEMB, T])
        w1 = m.sb("w1", [FEMB, FC])
        w2 = m.sb("w2", [FC, FC])
        w3 = m.sb("w3", [P, 4 * HY])
        mlp_col = m.sb("mlp_col", [FC, 5])
        h2 = m.sb("h2", [P, T])
        dft = m.sb("dft", [P, 2, 4, P])
        idft = m.sb("idft", [P, 4, BLK])
        decay = m.sb("decay", [P, 2, HY])
        seg = m.sb("seg", [P, 4, HY])
        win = m.sb("win", [P, 2, NB, 4, HY])
        u_tok = m.sb("u_tok", [P, TT, HY])
        arg, turns, h1 = (u_tok[0:FC, 2 * x:2 * x + 2, :].rearrange("p a b -> p (a b)") for x in range(3))
        uf = m.sb("uf", [P, NB, 4, HY])
        yf = m.sb("yf", [P, 4, HY])
        t1 = m.sb("t1", [P, 4, HY])
        gate = m.sb("gate", [P, 2, 2, BLK])
        ps_a = m.psum("ps_a", [P, 4, 512])
        ps_v = m.psum("ps_v", [P, 4, 512])

        consts_in, mlp_ps, mlp_arg, mlp_sin, v_in = (
            sems(n) for n in ("hy_consts_in", "mlp_ps", "mlp_arg", "mlp_sin", "v_in"))
        a_done, a_used, v_done, v_used, y_ready = (
            sems(n) for n in ("a_done", "a_used", "v_done", "v_used", "y_ready"))
        step, padded = sems("d_dve_step"), sems("padded")
        decay_in = [sems(f"decay_in{s}") for s in range(2)]
        gate_in = [sems(f"gate_in{s}") for s in range(2)]
        y_next = sems("y_next")

        A_TURN, A_SEG, A_U = TT, 8 * NB, 4 * NB
        A_ALL = A_TURN + A_SEG + A_U
        V_FILT, V_OUT = 2 * TT, 2 * NB
        V_ALL = V_FILT + V_OUT

        with nc.Block() as block:

            @block.sync
            def _(sp):
                for dst, name in ((feats[:], "feats"), (w1[:], "filt_w1"), (w2[:], "filt_w2"), (w3[0:FC, :], "filt_w3"),
                                  (mlp_col[:, 0:3], "filt_cols"), (dft[:], "dft"), (idft[:], "idft")):
                    sp.dma_start(dst, a[name]).then_inc(consts_in, 16)
                u_d = a["u_d"].rearrange("(o c p) t -> o p c t", c=4, p=P)
                sp.dma_start(y_t[:], u_d[0]).then_inc(v_in, 16)
                decays = a["decay"].rearrange("(t s p) c -> t s p c", s=2, p=P)
                with sp.Fori(0, 2) as o:
                    for b in range(NB):
                        for s in range(2):
                            sp.wait_ge(v_used, V_ALL * o + (4 * b + 2 * s + 2 if b else 4))
                            sp.dma_start(decay[:, s], decays[b, s]).then_inc(decay_in[s], 16)
                    for b in range(NB):
                        for pair in range(2):
                            if b:
                                sp.wait_ge(v_used, V_ALL * o + V_FILT + 2 * b + pair + 3)
                            sp.dma_start(gate[:, pair], u_d[o + 1][:, 2 * pair:2 * pair + 2, b * BLK:(b + 1) * BLK]
                                         ).then_inc(gate_in[pair], 16)

            @block.tensor
            def _(pe):
                pe.sem_inc(a_done, 4)
                pe.wait_ge(consts_in, 7 * 16)
                for th in range(2):
                    pe.matmul(ps_v[0:FC, th, :], w1[:], feats[:, th * 512:(th + 1) * 512], start=True, stop=True
                              ).then_inc(mlp_ps, 1)
                pe.wait_ge(mlp_sin, 1)
                for th in range(2):
                    pe.matmul(ps_v[0:FC, th, :], w2[:], h1[:, th * 512:(th + 1) * 512], start=True, stop=True
                              ).then_inc(mlp_ps, 1)
                pe.wait_ge(mlp_sin, 2)
                pe.wait_ge(v_in, 16)
                pe.wait_ge(padded, 1)
                with pe.Fori(0, 2) as o:
                    pe.wait_ge(y_next, o + 1)
                    n = 0
                    for t in range(TT):
                        pe.wait_ge(a_used, A_ALL * o + n + 1)
                        for c in range(4):
                            mm = pe.transpose(ps_a[:, n % 4, c * P:(c + 1) * P], y_t[:, c, t * P:(t + 1) * P], ident[:])
                        mm.then_inc(a_done, 1)
                        n += 1
                    v = 0

                    def taps(b):
                        nonlocal v
                        for s in range(2):
                            for d in range(2):
                                pe.wait_ge(v_used, V_ALL * o + v + 1)
                                t = 2 * b + s
                                pe.matmul(ps_v[:, v % 4, :], h2[:, t * P:(t + 1) * P],
                                          w3[:, bass.ds(2 * HY * d + o * HY, HY)], start=True, stop=True
                                          ).then_inc(v_done, 1)
                                v += 1

                    for b in range(NB):
                        taps(b)
                        for d in range(2):
                            pe.wait_ge(v_used, V_ALL * o + 4 * b + 4 + 4)
                            for p in range(4):
                                pe.wait_ge(a_used, A_ALL * o + n + 1)
                                for s in range(2):
                                    mm = pe.matmul(ps_a[:, n % 4, :], dft[:, s, p, :], seg[:, 2 * s + d, :],
                                                   start=(s == 0), stop=(s == 1))
                                mm.then_inc(a_done, 1)
                                n += 1
                    for b in range(NB):
                        for p in range(4):
                            pe.wait_ge(a_used, A_ALL * o + n + 1)
                            for s in range(2):
                                mm = pe.matmul(ps_a[:, n % 4, :], dft[:, s, p, :], u_tok[:, 2 * b + s, :],
                                               start=(s == 0), stop=(s == 1))
                            mm.then_inc(a_done, 1)
                            n += 1
                    for b in range(NB):
                        pe.wait_ge(y_ready, NB * o + b + 1)
                        for pair in range(2):
                            pe.wait_ge(v_used, V_ALL * o + v + 1)
                            for c in range(2):
                                ch = 2 * pair + c
                                for p in range(4):
                                    mm = pe.matmul(ps_v[:, v % 4, c * BLK:(c + 1) * BLK], yf[:, p, ch * P:(ch + 1) * P],
                                                   idft[:, p, :], start=(p == 0), stop=(p == 3))
                            mm.then_inc(v_done, 1)
                            v += 1
                    assert n == A_ALL and v == V_ALL

            @block.scalar
            def _(act):
                for layer, h in enumerate((h1, h2[0:FC, :])):
                    act.wait_ge(mlp_arg, layer + 1)
                    act.activation(h, arg, ACT.Sin).then_inc(mlp_sin, 1)
                act.sem_inc(a_used, 4)
                with act.Fori(0, 2) as o:
                    for n in range(A_ALL):
                        if n < A_TURN:
                            out = u_tok[:, n, :]
                        elif n < A_TURN + A_SEG:
                            b, d, p = (n - A_TURN) // 8, (n - A_TURN) // 4 % 2, n % 4
                            out = win[:, d, b, p, :]
                        else:
                            out = uf[:, (n - A_TURN - A_SEG) // 4, n % 4, :]
                        act.wait_ge(a_done, A_ALL * o + n + 5)
                        if n == 0:
                            act.wait_ge(v_used, V_ALL * o + 4)
                        act.activation(out, ps_a[:, n % 4, :], ACT.Copy).then_inc(a_used, 1)

            @block.vector
            def _(dve):
                dt = Tally(dve, step)
                dve.sem_inc(v_used, 4)
                dve.memset(w3[FC:P, :], 0.0)
                dve.memset(h2[FC:P, :], 0.0).then_inc(padded, 1)
                dve.wait_ge(consts_in, 7 * 16)
                for layer in range(2):
                    dt.then_wait(dve.tensor_tensor(mlp_col[:, 3 + layer:4 + layer], mlp_col[:, 0:1],
                                                   mlp_col[:, 1 + layer:2 + layer], ALU.mult))
                for layer in range(2):
                    for th in range(2):
                        dve.wait_ge(mlp_ps, 2 * layer + th + 1)
                        dt.inc(dve.tensor_scalar(arg[:, th * 512:(th + 1) * 512], ps_v[0:FC, th, :], mlp_col[:, 0:1],
                                                 mlp_col[:, 3 + layer:4 + layer], ALU.mult, ALU.add))
                    dt.wait()
                    dt.then_wait(dve.tensor_scalar(turns, arg, 1.0 / (2.0 * math.pi), ROUND, ALU.mult, ALU.add))
                    dt.then_wait(dve.tensor_scalar(turns, turns, -ROUND, None, ALU.add))
                    dt.then_wait(dve.scalar_tensor_tensor(out=arg, in0=turns, scalar=-TWO_PI_HI, in1=arg,
                                                          op0=ALU.mult, op1=ALU.add))
                    dt.then_wait(dve.scalar_tensor_tensor(out=arg, in0=turns, scalar=-TWO_PI_LO, in1=arg,
                                                          op0=ALU.mult, op1=ALU.add))
                    dve.tensor_scalar(arg, arg, 3.1415925, -3.1415925, ALU.min, ALU.max).then_inc(mlp_arg, 1)
                    dve.wait_ge(mlp_sin, layer + 1)
                dve.sem_inc(y_next, 1)
                PER = 1 + 4 * (NB - 1) + 2 + NB * (5 * NB - 2 + 4)
                with dve.Fori(0, 2) as o:
                    dt.enter(o, PER)
                    v = 0
                    for b in range(NB):
                        for s in range(2):
                            for d in range(2):
                                dve.wait_ge(v_done, V_ALL * o + v + 1)
                                dve.wait_ge(decay_in[s], 16 * NB * o + 16 * b + 16)
                                if b:
                                    dve.wait_ge(a_done, A_ALL * o + A_TURN + 8 * b + 4)
                                dt.inc(dve.tensor_tensor(seg[:, 2 * s + d, :], ps_v[:, v % 4, :], decay[:, s, :],
                                                         ALU.mult)) if (b, s, d) == (0, 0, 1) else \
                                    dve.tensor_tensor(seg[:, 2 * s + d, :], ps_v[:, v % 4, :], decay[:, s, :],
                                                      ALU.mult).then_inc(v_used, 1)
                                if (b, s, d) == (0, 0, 1):
                                    dt.wait()
                                    dve.memset(seg[0:1, 1, :], 0.0).then_inc(v_used, 1)
                                v += 1
                    dve.wait_ge(a_used, A_ALL * o + A_TURN + A_SEG + 4)
                    for b in range(NB - 1, 0, -1):
                        new = win[:, :, b].rearrange("p d (e r) c -> p d e r c", e=2)
                        old = win[:, :, b - 1].rearrange("p d (e r) c -> p d e r c", e=2)
                        for e, (re, im) in enumerate(((ALU.subtract, ALU.add), (ALU.add, ALU.subtract))):
                            dt.inc(dve.tensor_tensor(new[:, :, e, 0], new[:, :, e, 0], old[:, :, e, 1], re))
                            dt.inc(dve.tensor_tensor(new[:, :, e, 1], new[:, :, e, 1], old[:, :, e, 0], im))
                        dt.wait()
                    w0, f0 = (win[:, d, 0].rearrange("p (e r) c -> p e r c", e=2) for d in range(2))
                    dt.inc(dve.tensor_tensor(w0[:, :, 0], w0[:, :, 0], f0[:, :, 0], ALU.add))
                    dt.inc(dve.tensor_tensor(w0[:, :, 1], w0[:, :, 1], f0[:, :, 1], ALU.subtract))
                    dt.wait()
                    dve.wait_ge(a_used, A_ALL * o + A_ALL + 4)
                    for i in range(NB):
                        y = yf[:].rearrange("p (e r) c -> p e r c", e=2)
                        q = t1[:].rearrange("p (e r) c -> p e r c", e=2)
                        for j in range(NB):
                            k = win[:, 0 if i >= j else 1, abs(i - j)].rearrange("p (e r) c -> p e r c", e=2)
                            u = uf[:, j].rearrange("p (e r) c -> p e r c", e=2)
                            kr = [k[:, :, x, :].unsqueeze(2).broadcast_to([P, 2, 2, HY]) for x in range(2)]
                            add, sub = (ALU.add, ALU.subtract) if i >= j else (ALU.subtract, ALU.add)
                            if j == 0:
                                dve.wait_ge(v_done, V_ALL * o + V_FILT + 2 * i)
                                dt.inc(dve.tensor_tensor(y, kr[0], u, ALU.mult))
                            else:
                                dt.then_wait(dve.tensor_tensor(q, kr[0], u, ALU.mult))
                                dt.inc(dve.tensor_tensor(y, y, q, ALU.add))
                            dt.wait()
                            dt.then_wait(dve.tensor_tensor(q, kr[1], u, ALU.mult))
                            dt.inc(dve.tensor_tensor(y[:, :, 0], y[:, :, 0], q[:, :, 1], sub))
                            last = dve.tensor_tensor(y[:, :, 1], y[:, :, 1], q[:, :, 0], add)
                            if j == NB - 1:
                                last.then_inc(y_ready, 1)
                            else:
                                dt.then_wait(last)
                        for pair in range(2):
                            dve.wait_ge(v_done, V_ALL * o + v + 1)
                            dve.wait_ge(gate_in[pair], 16 * NB * o + 16 * i + 16)
                            for c in range(2):
                                ch = 2 * pair + c
                                tok = slice(i * BLK, (i + 1) * BLK)
                                dt.inc(dve.scalar_tensor_tensor(
                                    out=y_t[:, ch, tok], in0=y_t[:, ch, tok],
                                    scalar=par[:, bass.ds(C_SKIP + 4 * o + ch, 1)],
                                    in1=ps_v[:, v % 4, c * BLK:(c + 1) * BLK], op0=ALU.mult, op1=ALU.add))
                            dt.wait()
                            tok_pair = y_t[:, 2 * pair:2 * pair + 2, i * BLK:(i + 1) * BLK]
                            last = dve.tensor_tensor(tok_pair, tok_pair, gate[:, pair], ALU.mult)
                            last.then_inc(v_used, 1)
                            v += 1
                    dve.wait_ge(v_used, V_ALL * o + V_ALL + 4)
                    dve.sem_inc(y_next, 1)
                    dt.leave(2)


def merge(nc, sems, a, y_t, na_t, m_t):
    with ExitStack() as ctx:
        m = Maker(nc, ctx, "merge_")
        in_hi, in_lo = m.sb("in_hi", [P, 2, 4, T], F32R), m.sb("in_lo", [P, 2, 4, T], F32R)
        b_raw = m.sb("b_raw", [P, 2, 2, 4, P])
        b_hi, b_lo = m.sb("b_hi", [P, 2, 2, 4, P], F32R), m.sb("b_lo", [P, 2, 2, 4, P], F32R)
        gate = m.sb("gate", [P, 2, 2, T])
        part = m.sb("part", [P, 2, 2, 512])
        ps = m.psum("ps", [P, 4, 2, 512])

        w_in = [sems(f"branch_in{s}") for s in range(2)]
        g_in = [sems(f"gates_in{s}") for s in range(2)]
        in_hi_ready, in_lo_ready, bh_ready, bl_ready, branched, merged, step = (
            sems(n) for n in ("in_hi_ready", "in_lo_ready", "bh_ready", "bl_ready", "branched", "merged", "e_dve_step"))

        with nc.Block() as block:

            @block.sync
            def _(sp):
                w = [a[n].rearrange("(k p) (d c) -> d p k c", p=P, c=P) for n in ("w_branch_hy", "w_branch_na")]
                g = a["g_d"].rearrange("(b d p) t -> b d p t", b=2, p=P)
                with sp.Fori(0, KD // 2) as i:
                    for s in range(2):
                        d = 2 * i + s
                        sp.wait_ge(bl_ready, d + 1)
                        for b in range(2):
                            sp.dma_start(b_raw[:, s, b], w[b][d]).then_inc(w_in[s], 16)
                        sp.wait_ge(merged, 2 * d + 2)
                        for b in range(2):
                            sp.dma_start(gate[:, s, b], g[b, d]).then_inc(g_in[s], 16)

            @block.tensor
            def _(pe):
                pe.sem_inc(branched, 4)
                pe.wait_ge(in_lo_ready, 8)
                with pe.Fori(0, KD // 2) as i:
                    for s in range(2):
                        pe.wait_ge(bl_ready, 2 * i + s + 3)
                        for th in range(2):
                            n = 2 * s + th
                            pe.wait_ge(merged, 4 * i + n + 1)
                            for b in range(2):
                                for k in range(4):
                                    hi, lo = b_hi[:, s, b, k, :], b_lo[:, s, b, k, :]
                                    cols = slice(th * 512, (th + 1) * 512)
                                    for x, (w, h) in enumerate(((hi, in_hi), (hi, in_lo), (lo, in_hi))):
                                        mm = pe.matmul(ps[:, n, b, :], w, h[:, b, k, cols],
                                                       start=(k == 0 and x == 0), stop=(k == 3 and x == 2))
                            mm.then_inc(branched, 1)

            @block.scalar
            def _(act):
                def split(s, i, d):
                    act.wait_ge(w_in[s], 32 * i + 32)
                    act.wait_ge(branched, 2 * d + 2)
                    act.activation(b_hi[:, s], b_raw[:, s], ACT.Copy).then_inc(bh_ready, 1)

                for b, src in enumerate((y_t, na_t)):
                    for k in range(4):
                        act.activation(in_hi[:, b, k, :], src[:, k, :], ACT.Copy).then_inc(in_hi_ready, 1)
                with act.Fori(0, KD // 2) as i:
                    for s in range(2):
                        split(s, i, 2 * i + s)

            @block.vector
            def _(dve):
                dt = Tally(dve, step)
                dve.sem_inc(bl_ready, 2)
                dve.sem_inc(merged, 4)
                for b, src in enumerate((y_t, na_t)):
                    for k in range(4):
                        dve.wait_ge(in_hi_ready, 4 * b + k + 1)
                        dve.tensor_tensor(in_lo[:, b, k, :], src[:, k, :], in_hi[:, b, k, :].bitcast(F32),
                                          ALU.subtract).then_inc(in_lo_ready, 1)

                def split(d, s):
                    dve.wait_ge(bh_ready, d + 1)
                    dve.tensor_tensor(b_lo[:, s], b_raw[:, s], b_hi[:, s].bitcast(F32), ALU.subtract
                                      ).then_inc(bl_ready, 1)

                def gated(i, s):
                    for th in range(2):
                        n = 2 * s + th
                        cols = slice(th * 512, (th + 1) * 512)
                        dve.wait_ge(branched, 4 * i + n + 5)
                        dve.wait_ge(g_in[s], 32 * i + 32)
                        dve.wait_ge(merged, 4 * i + n + 3)
                        for b in range(2):
                            dt.inc(dve.tensor_tensor(part[:, th, b], ps[:, n, b, :], gate[:, s, b, cols], ALU.mult))
                        dt.wait()
                        dve.tensor_tensor(m_t[:, 2 * i + s, cols], part[:, th, 0], part[:, th, 1], ALU.add
                                          ).then_inc(merged, 1)

                split(0, 0)
                with dve.Fori(0, KD // 2 - 1) as i:
                    dt.enter(i, 8)
                    for s in range(2):
                        split(2 * i + s + 1, 1 - s)
                        gated(i, s)
                    dt.leave(KD // 2 - 1)
                split(KD - 1, 1)
                gated(KD // 2 - 1, 0)
                gated(KD // 2 - 1, 1)


def project_out(nc, sems, a, keep, m_t, logits):
    ident = keep["ident"]
    with ExitStack() as ctx:
        m = Maker(nc, ctx, "out_")
        w_raw = m.sb("w_raw", [P, 2, D])
        w_hi, w_lo = m.sb("w_hi", [P, KD, D], F32R), m.sb("w_lo", [P, KD, D], F32R)
        m_hi, m_lo = m.sb("m_hi", [P, 2, KD, P], F32R), m.sb("m_lo", [P, 2, KD, P], F32R)
        router = m.sb("router", [P, KD, E_N])
        g1_row, scale_row, shift_row, gain_row = (m.sb(n, [P, D]) for n in ("g1_row", "scale_row", "shift_row", "gain_row"))
        x_in = m.sb("x_in", [P, 2, D])
        x1 = m.sb("x1", [P, 2, D])
        h2 = m.sb("h2", [P, 2, D])
        h2_t = m.sb("h2_t", [P, KD, P])
        squares = gain_row
        stat = m.sb("stat", [P, 2, 5])
        ps_o = m.psum("ps_o", [P, 2, D])
        ps_h = m.psum("ps_h", [P, D])

        rows_in = sems("rows_in")
        wo_in = [sems(f"w_out_in{s}") for s in range(2)]
        xt_in = [sems(f"x_tile_in{s}") for s in range(2)]
        stored = [sems(f"f_stored{s}") for s in range(2)]
        wo_hi, wo_lo, m_split, projected, x1_ready, squared, var_ready, rooted, normed, turned, copied, routed = (
            sems(n) for n in ("wo_hi", "wo_lo", "m_split", "projected", "x1_ready", "squared", "f_var_ready", "rooted",
                              "f_normed", "f_turned", "f_copied", "routed"))
        step = sems("f_dve_step")

        with nc.Block() as block:

            @block.sync
            def _(sp):
                w = a["w_out"].rearrange("(k p) n -> k p n", p=P)
                mod = a["mod_d"]
                for k in range(KD):
                    sp.wait_ge(wo_lo, k + 1)
                    sp.dma_start(w_raw[:, k % 2], w[k]).then_inc(wo_in[k % 2], 16)
                    if k == 1:
                        for dst, at in ((g1_row, 2 * D), (shift_row, 3 * D), (scale_row, 4 * D)):
                            sp.dma_start(dst[:], bass.AP(mod.tensor, at, [[0, P], [1, D]])).then_inc(rows_in, 16)
                        sp.dma_start(gain_row[:], bass.AP(a["norm2_g"].tensor, 0, [[0, P], [1, D]])
                                     ).then_inc(rows_in, 16)
                        sp.dma_start(router[:], a["w_router"].rearrange("(k p) e -> p k e", p=P)).then_inc(rows_in, 16)
                x_t, acc_t, h2_t_d = (a[n].rearrange("(t p) d -> t p d", p=P) for n in ("x", "acc_d", "h2_d"))
                sp.sem_inc(stored[0], 32)
                sp.sem_inc(stored[1], 32)

                def load(t, s):
                    sp.wait_ge(x1_ready, t + 1)
                    sp.dma_start(x_in[:, s], x_t[t]).then_inc(xt_in[s], 16)

                def store(t, s):
                    sp.wait_ge(x1_ready, t + 3)
                    sp.dma_start(acc_t[t], x1[:, s]).then_inc(stored[s], 16)
                    sp.wait_ge(normed, t + 3)
                    sp.dma_start(h2_t_d[t], h2[:, s]).then_inc(stored[s], 16)

                load(0, 0)
                load(1, 1)
                with sp.Fori(0, TT // 2 - 1) as i:
                    for s in range(2):
                        store(2 * i + s, s)
                        load(2 * i + s + 2, s)
                store(TT - 2, 0)
                store(TT - 1, 1)
                for s in range(2):
                    sp.wait_ge(stored[s], 32 * (TT // 2 + 1))

            @block.tensor
            def _(pe):
                pe.sem_inc(projected, 2)
                pe.sem_inc(turned, 2)
                pe.sem_inc(routed, 1)
                pe.wait_ge(wo_lo, KD + 2)

                def out(t, s):
                    pe.wait_ge(m_split, t + 3)
                    pe.wait_ge(x1_ready, t + 1)
                    for k in range(KD):
                        for x, (h, w) in enumerate(((m_hi, w_hi), (m_hi, w_lo), (m_lo, w_hi))):
                            for n in range(2):
                                mm = pe.matmul(ps_o[:, s, n * 512:(n + 1) * 512], h[:, s, k, :],
                                               w[:, k, n * 512:(n + 1) * 512], start=(k == 0 and x == 0),
                                               stop=(k == KD - 1 and x == 2))
                    mm.then_inc(projected, 1)

                def route(t, s):
                    pe.wait_ge(normed, t + 3)
                    pe.wait_ge(copied, t + 1)
                    for k in range(KD):
                        mm = pe.transpose(ps_h[:, k * P:(k + 1) * P], h2[:, s, k * P:(k + 1) * P], ident[:])
                    mm.then_inc(turned, 1)
                    pe.wait_ge(copied, t + 2)
                    for k in range(KD):
                        mm = pe.matmul(logits[:, bass.ds(t * E_N, E_N)] if not isinstance(t, int)
                                       else logits[:, t * E_N:(t + 1) * E_N], h2_t[:, k, :], router[:, k, :],
                                       start=(k == 0), stop=(k == KD - 1))
                    mm.then_inc(routed, 1)

                out(0, 0)
                pe.wait_ge(rows_in, 5 * 16)
                with pe.Fori(0, TT // 2 - 1) as i:
                    for s in range(2):
                        out(2 * i + s + 1, 1 - s)
                        route(2 * i + s, s)
                out(TT - 1, 1)
                route(TT - 2, 0)
                route(TT - 1, 1)

            @block.scalar
            def _(act):
                act.sem_inc(copied, 1)
                for k in range(KD):
                    act.wait_ge(wo_in[k % 2], 16 * (k // 2 + 1))
                    act.activation(w_hi[:, k, :], w_raw[:, k % 2, :], ACT.Copy).then_inc(wo_hi, 1)
                act.wait_ge(x1_ready, 2)
                with act.Fori(0, TT // 2) as i:
                    for s in range(2):
                        t = 2 * i + s
                        act.wait_ge(x1_ready, t + 3)
                        act.activation(squares[:], x1[:, s], ACT.Square, accum_out=stat[:, s, 0:1]
                                       ).then_inc(squared, 1)
                        act.wait_ge(var_ready, t + 1)
                        act.activation(stat[:, s, 2:3], stat[:, s, 1:2], ACT.Sqrt).then_inc(rooted, 1)
                        act.wait_ge(turned, t + 3)
                        act.wait_ge(routed, t + 1)
                        act.activation(h2_t[:].rearrange("p k q -> p (k q)"), ps_h[:], ACT.Copy).then_inc(copied, 1)

            @block.vector
            def _(dve):
                dt = Tally(dve, step)
                dve.sem_inc(wo_lo, 2)
                for k in range(KD):
                    dve.wait_ge(wo_hi, k + 1)
                    dve.tensor_tensor(w_lo[:, k, :], w_raw[:, k % 2, :], w_hi[:, k, :].bitcast(F32), ALU.subtract
                                      ).then_inc(wo_lo, 1)
                dve.wait_ge(rows_in, 5 * 16)
                dt.then_wait(dve.scalar_tensor_tensor(out=scale_row[:], in0=scale_row[:], scalar=1.0, in1=gain_row[:],
                                                      op0=ALU.add, op1=ALU.mult))
                dve.sem_inc(m_split, 2)
                dve.sem_inc(x1_ready, 2)
                dve.sem_inc(normed, 2)

                def split(t, s):
                    src = m_t[:, :, bass.ds(t * P, P)] if not isinstance(t, int) else m_t[:, :, t * P:(t + 1) * P]
                    dve.wait_ge(projected, t + 1)
                    dt.then_wait(dve.tensor_scalar(m_hi[:, s], src, 1.0, None, ALU.mult))
                    dve.tensor_tensor(m_lo[:, s], src, m_hi[:, s].bitcast(F32), ALU.subtract).then_inc(m_split, 1)

                def residual(t, s, i):
                    dve.wait_ge(projected, t + 3)
                    dve.wait_ge(stored[s], 32 * i + 32)
                    dt.then_wait(dve.tensor_tensor(x1[:, s], ps_o[:, s], g1_row[:], ALU.mult))
                    dve.wait_ge(xt_in[s], 16 * i + 16)
                    dve.tensor_tensor(x1[:, s], x1[:, s], x_in[:, s], ALU.add).then_inc(x1_ready, 1)
                    dve.wait_ge(squared, t + 1)
                    st = [stat[:, s, x:x + 1] for x in range(5)]
                    dve.tensor_scalar(st[1], st[0], 1.0 / D, EPS, ALU.mult, ALU.add).then_inc(var_ready, 1)
                    inverse_root(dve, dt, lambda: dve.wait_ge(rooted, t + 1), st[1], st[2], st[3], st[4])
                    dve.wait_ge(turned, t + 1)
                    dt.then_wait(dve.scalar_tensor_tensor(out=h2[:, s], in0=x1[:, s], scalar=st[3], in1=scale_row[:],
                                                          op0=ALU.mult, op1=ALU.mult))
                    dve.tensor_tensor(h2[:, s], h2[:, s], shift_row[:], ALU.add).then_inc(normed, 1)

                split(0, 0)
                with dve.Fori(0, TT // 2 - 1) as i:
                    dt.enter(i, 2 * 8)
                    for s in range(2):
                        split(2 * i + s + 1, 1 - s)
                        residual(2 * i + s, s, i)
                    dt.leave(TT // 2 - 1)
                split(TT - 1, 1)
                residual(TT - 2, 0, TT // 2 - 1)
                residual(TT - 1, 1, TT // 2 - 1)


CHUNKS = [(c, min(512, FF - c)) for c in range(0, FF, 512)]
UNITS = []
for _c, (_at, _w) in enumerate(CHUNKS):
    _parts = 2 * _w // 512
    UNITS += [(name, _c, q, _parts) for name in ("gate", "up") for q in range(_parts)]
    if _c:
        UNITS += [("down", _c - 1, q, 2) for q in range(2)]
UNITS += [("down", len(CHUNKS) - 1, q, _parts) for q in range(_parts)]
N_U = len(UNITS)
RAW = 11
PARTS = 3
assert N_U % RAW == 0 and N_U % PARTS == 0
LAST_OF = {(name, c): u for u, (name, c, q, parts) in enumerate(UNITS) if q == parts - 1}


def unit_source(a, e, u):
    name, c, q, parts = UNITS[u]
    at, w = CHUNKS[c]
    if name == "down":
        f = at // P + 2 * q
        return a["w_down"].rearrange("e (f p) n -> e p f n", p=P)[e][:, f:f + 2, :]
    rows = KD // parts
    return a["w_" + name].rearrange("e (k p) n -> e p k n", p=P)[e][:, rows * q:rows * (q + 1), at:at + w]


def unit_view(slot, u):
    name, c, _, parts = UNITS[u]
    return slot.rearrange("p (r n) -> p r n", r=2 if name == "down" else KD // parts)


def choose(nc, sems, a, keep, logits, raw, raw_in, gate_col, idx_col):
    ident = keep["ident"]
    with ExitStack() as ctx:
        m = Maker(nc, ctx, "choose_")
        lg = logits[:, 0:TT * E_N].rearrange("p (t e) -> p t e", e=E_N)
        top, total, inv = (m.sb(n, [P, TT]) for n in ("top", "total", "inv"))
        aff = m.sb("aff", [P, TT, E_N])
        rows = m.sb("rows", [E_N, T])
        best = m.sb("best", [E_N, CAP])
        where = m.sb("where", [E_N, CAP], U32)
        where_f = m.sb("where_f", [E_N, CAP])
        ps_r = m.psum("ps_r", [P, T])
        ps_c = m.psum("ps_c", [P, 2, 512])
        step, shifted, exped, aff_ready, aff_turned, best_ready, best_turned = (
            sems(n) for n in ("g_dve_step", "shifted", "exped", "aff_ready", "aff_turned", "best_ready", "best_turned"))

        with nc.Block() as block:

            @block.sync
            def _(sp):
                for u in range(RAW):
                    sp.dma_start(unit_view(raw[:, u], u), unit_source(a, 0, u)).then_inc(raw_in[u], 16)

            @block.scalar
            def _(act):
                act.wait_ge(shifted, 1)
                act.activation(aff[:], aff[:], ACT.Exp).then_inc(exped, 1)

            @block.tensor
            def _(pe):
                pe.wait_ge(aff_ready, 1)
                for t in range(TT):
                    mm = pe.transpose(ps_r[0:E_N, t * P:(t + 1) * P], aff[:, t, :], ident[:])
                mm.then_inc(aff_turned, 1)
                pe.wait_ge(best_ready, 1)
                pe.transpose(ps_c[:, 0, 0:E_N], best[:], ident[0:E_N, 0:E_N])
                pe.transpose(ps_c[:, 1, 0:E_N], where_f[:], ident[0:E_N, 0:E_N]).then_inc(best_turned, 1)

            @block.vector
            def _(dve):
                dt = Tally(dve, step)

                def wide(v):
                    return v[:].unsqueeze(2).broadcast_to([P, TT, E_N])

                dt.then_wait(dve.reduce_max(top[:], lg, AX_X))
                dve.tensor_tensor(aff[:], lg, wide(top), ALU.subtract).then_inc(shifted, 1)
                dve.wait_ge(exped, 1)
                dt.then_wait(dve.reduce_sum(total[:], aff[:], AX_X))
                dt.then_wait(dve.reciprocal(inv[:], total[:]))
                dve.tensor_tensor(aff[:], aff[:], wide(inv), ALU.mult).then_inc(aff_ready, 1)
                dve.wait_ge(aff_turned, 1)
                dt.then_wait(dve.tensor_copy(rows[:], ps_r[0:E_N, :]))
                for r in range(CAP // 8):
                    eight = slice(8 * r, 8 * r + 8)
                    dt.then_wait(dve.max(best[:, eight], rows[:]))
                    dt.inc(dve.max_index(where[:, eight], best[:, eight], rows[:]))
                    if r + 1 < CAP // 8:
                        dt.inc(dve.match_replace(rows[:], best[:, eight], rows[:], -1.0))
                    dt.wait()
                dve.tensor_copy(where_f[:], where[:]).then_inc(best_ready, 1)
                dve.wait_ge(best_turned, 1)
                dve.tensor_copy(gate_col[:], ps_c[:, 0, 0:E_N])
                dve.tensor_copy(idx_col[:], ps_c[:, 1, 0:E_N])


def experts(nc, sems, a, keep, raw, raw_in, gate_col, idx_col):
    ident = keep["ident"]
    with ExitStack() as ctx:
        m = Maker(nc, ctx, "moe_")
        w_hi, w_lo = m.sb("w_hi", [P, PARTS, 2048], F32R), m.sb("w_lo", [P, PARTS, 2048], F32R)
        xe = m.sb("xe", [P, D])
        xt_hi, xt_lo = m.sb("xt_hi", [P, KD, P], F32R), m.sb("xt_lo", [P, KD, P], F32R)
        sl = m.sb("sl", [P, 2, 512])
        h = m.sb("h", [P, 2, 512])
        ht_hi, ht_lo = m.sb("ht_hi", [P, 2, 4, P], F32R), m.sb("ht_lo", [P, 2, 4, P], F32R)
        y = m.sb("y", [P, D])
        g2_row = m.sb("g2_row", [P, D])
        ps_gate = m.psum("ps_gate", [P, 2, 512])
        ps_up = m.psum("ps_up", [P, 2, 512])
        ps_y = m.psum("ps_y", [P, D])
        ps_h = m.psum("ps_h", [P, 512])
        ps_x = m.psum("ps_x", [P, 512])

        hi_ready, lo_ready, used, silu_done, multiplied, turned_h, h_high, h_parts = (
            sems(n) for n in ("m_hi_ready", "m_lo_ready", "used_units", "silu_done", "multiplied", "turned_h", "h_high",
                              "h_parts"))
        turned_x, x_high, x_parts, gathered, y_ready, y_free, scattered, g2_in = (
            sems(n) for n in ("turned_x", "x_high", "x_parts", "gathered", "moe_y_ready", "y_free", "scattered", "g2_in"))
        N_C = len(CHUNKS)

        def after(u):
            out = []
            for c in range(N_C):
                if min(LAST_OF["gate", c] + 2, N_U - 1) == u:
                    out.append(("silu", c))
                if min(LAST_OF["up", c] + 2, N_U - 1) == u:
                    out.append(("multiply", c))
            for c in range(N_C - 1):
                if LAST_OF["gate", c + 1] + 2 == u:
                    out.append(("turned", c))
            if LAST_OF["up", N_C - 1] + 2 == u:
                out.append(("turned_x", 0))
            if u == N_U - 1:
                out += [("turned", N_C - 1), ("turned_x", 1)]
            return out

        with nc.Block() as block:

            @block.sync
            def _(sp):
                sp.dma_start(g2_row[:], bass.AP(a["mod_d"].tensor, 5 * D, [[0, P], [1, D]])).then_inc(g2_in, 16)

                def load(e, e_of, u):
                    sp.wait_ge(lo_ready, N_U * e_of + u + 1)
                    sp.dma_start(unit_view(raw[:, u % RAW], u), unit_source(a, e_of, u)).then_inc(raw_in[u % RAW], 16)

                with sp.Fori(0, E_N - 1) as e:
                    for u in range(RAW, N_U):
                        load(e, e, u)
                    for u in range(RAW):
                        load(e, e + 1, u)
                for u in range(RAW, N_U):
                    load(E_N - 1, E_N - 1, u)

            @block.gpsimd
            def _(pool):
                h2, acc = a["h2_d"], a["acc_d"]

                def gather(e):
                    if e:
                        pool.wait_ge(turned_x, 2 * e)
                    pool.indirect_dma_start(xe[:], None, h2, bass.IndirectOffsetOnAxis(ap=idx_col[:, min(e, E_N - 1):min(e, E_N - 1) + 1], axis=0)
                                            ).then_inc(gathered, 16)

                pool.sem_inc(y_free, 1)
                gather(0)
                for e in range(E_N):
                    gather(e + 1)
                    pool.wait_ge(y_ready, e + 2)
                    pool.indirect_dma_start(acc, bass.IndirectOffsetOnAxis(ap=idx_col[:, e:e + 1], axis=0), y[:], None,
                                            compute_op=ALU.add).then_inc(scattered, 16)
                    pool.wait_ge(scattered, 16 * e + 16)
                    pool.sem_inc(y_free, 1)

            @block.tensor
            def _(pe):
                pe.sem_inc(used, 3)
                pe.sem_inc(turned_h, 1)

                def turn_x(half, count):
                    pe.wait_ge(x_parts, count + 1)
                    for k in range(4):
                        at = (4 * half + k) * P
                        mm = pe.transpose(ps_x[:, k * P:(k + 1) * P], xe[:, at:at + P], ident[:])
                    mm.then_inc(turned_x, 1)

                def turn_h(e, c):
                    pe.wait_ge(multiplied, N_C * e + c + 3)
                    pe.wait_ge(h_parts, N_C * e + c + 1)
                    for b in range(CHUNKS[c][1] // P):
                        mm = pe.transpose(ps_h[:, b * P:(b + 1) * P], h[:, c % 2, b * P:(b + 1) * P], ident[:])
                    mm.then_inc(turned_h, 1)

                def unit(e, u):
                    name, c, q, parts = UNITS[u]
                    w = CHUNKS[c][1]
                    hi, lo = (unit_view(x[:, u % PARTS], u) for x in (w_hi, w_lo))
                    pe.wait_ge(lo_ready, N_U * e + u + 1 + RAW)
                    if name == "down":
                        if q == 0:
                            pe.wait_ge(h_parts, N_C * e + c + 2)
                        if q == 0 and c == 0:
                            pe.wait_ge(y_ready, e + 1)
                        for r in range(2):
                            f = 2 * q + r
                            ht = [x[:, c % 2, f, :] for x in (ht_hi, ht_lo)]
                            first, last = c == 0 and f == 0, c == N_C - 1 and f == w // P - 1
                            for x, (hp, wp) in enumerate(((ht[0], hi), (ht[0], lo), (ht[1], hi))):
                                for n in range(2):
                                    mm = pe.matmul(ps_y[:, n * 512:(n + 1) * 512], hp, wp[:, r, n * 512:(n + 1) * 512],
                                                   start=(first and x == 0), stop=(last and x == 2))
                    else:
                        ps = (ps_gate if name == "gate" else ps_up)[:, c % 2, 0:w]
                        if q == 0:
                            pe.wait_ge(multiplied, N_C * e + c + 1)
                        rows = KD // parts
                        for r in range(rows):
                            k = rows * q + r
                            for x, (hp, wp) in enumerate(((xt_hi, hi), (xt_hi, lo), (xt_lo, hi))):
                                mm = pe.matmul(ps, hp[:, k, :], wp[:, r, :], start=(k == 0 and x == 0),
                                               stop=(k == KD - 1 and x == 2))
                    mm.then_inc(used, 1)

                pe.wait_ge(gathered, 16)
                turn_x(0, 0)
                turn_x(1, 1)
                with pe.Fori(0, E_N) as e:
                    pe.wait_ge(x_parts, 2 * e + 3)
                    for u in range(N_U):
                        unit(e, u)
                        for c in range(N_C - 1):
                            if LAST_OF["gate", c + 1] == u:
                                turn_h(e, c)
                        if LAST_OF["up", N_C - 1] == u:
                            pe.wait_ge(gathered, 16 * e + 32)
                            turn_x(0, 2 * e + 2)
                        if LAST_OF["down", N_C - 2] == u:
                            turn_h(e, N_C - 1)
                            turn_x(1, 2 * e + 3)

            @block.scalar
            def _(act):
                act.sem_inc(silu_done, 2)

                def high_x(count):
                    half = count[1]
                    act.wait_ge(turned_x, count[0] + 1)
                    act.activation(xt_hi[:, 4 * half:4 * half + 4, :], ps_x[:].rearrange("p (k q) -> p k q", q=P),
                                   ACT.Copy).then_inc(x_high, 1)

                high_x((0, 0))
                high_x((1, 1))
                with act.Fori(0, E_N) as e:
                    for u in range(N_U):
                        act.wait_ge(raw_in[u % RAW], 48 * e + 16 * (u // RAW) + 16)
                        act.wait_ge(used, N_U * e + u + 1)
                        act.activation(w_hi[:, u % PARTS], raw[:, u % RAW], ACT.Copy).then_inc(hi_ready, 1)
                        for what, c in after(u):
                            if what == "silu":
                                w = CHUNKS[c][1]
                                act.wait_ge(used, N_U * e + LAST_OF["gate", c] + 1 + 3)
                                act.activation(sl[:, c % 2, 0:w], ps_gate[:, c % 2, 0:w], ACT.Silu
                                               ).then_inc(silu_done, 1)
                            elif what == "turned":
                                n = CHUNKS[c][1] // P
                                act.wait_ge(turned_h, N_C * e + c + 2)
                                act.activation(ht_hi[:, c % 2, 0:n], ps_h[:, 0:n * P].rearrange(
                                    "p (k q) -> p k q", q=P), ACT.Copy).then_inc(h_high, 1)
                            elif what == "turned_x":
                                high_x((2 * e + 2 + c, c))

            @block.vector
            def _(dve):
                dve.sem_inc(lo_ready, RAW)
                dve.sem_inc(h_parts, 1)
                dve.sem_inc(x_parts, 1)
                dve.sem_inc(multiplied, 2)
                dve.sem_inc(y_ready, 1)

                def low_x(count, half):
                    dve.wait_ge(x_high, count + 1)
                    view = xt_lo[:, 4 * half:4 * half + 4, :]
                    dve.tensor_tensor(view, ps_x[:].rearrange("p (k q) -> p k q", q=P),
                                      xt_hi[:, 4 * half:4 * half + 4, :].bitcast(F32), ALU.subtract
                                      ).then_inc(x_parts, 1)

                low_x(0, 0)
                low_x(1, 1)
                dve.wait_ge(g2_in, 16)
                with dve.Fori(0, E_N) as e:
                    for u in range(N_U):
                        dve.wait_ge(hi_ready, N_U * e + u + 1)
                        dve.tensor_tensor(w_lo[:, u % PARTS], raw[:, u % RAW], w_hi[:, u % PARTS].bitcast(F32),
                                          ALU.subtract).then_inc(lo_ready, 1)
                        for what, c in after(u):
                            if what == "multiply":
                                w = CHUNKS[c][1]
                                dve.wait_ge(silu_done, N_C * e + c + 3)
                                dve.wait_ge(used, N_U * e + LAST_OF["up", c] + 1 + 3)
                                dve.tensor_tensor(h[:, c % 2, 0:w], sl[:, c % 2, 0:w], ps_up[:, c % 2, 0:w], ALU.mult
                                                  ).then_inc(multiplied, 1)
                            elif what == "turned":
                                n = CHUNKS[c][1] // P
                                dve.wait_ge(h_high, N_C * e + c + 1)
                                dve.tensor_tensor(ht_lo[:, c % 2, 0:n], ps_h[:, 0:n * P].rearrange(
                                    "p (k q) -> p k q", q=P), ht_hi[:, c % 2, 0:n].bitcast(F32), ALU.subtract
                                    ).then_inc(h_parts, 1)
                            elif what == "turned_x":
                                low_x(2 * e + 2 + c, c)
                    dve.wait_ge(used, N_U * e + N_U + 3)
                    dve.wait_ge(y_free, e + 1)
                    dve.scalar_tensor_tensor(out=y[:], in0=ps_y[:], scalar=gate_col[:, bass.ds(e, 1)], in1=g2_row[:],
                                             op0=ALU.mult, op1=ALU.mult).then_inc(y_ready, 1)


def last_norm(nc, sems, a, out):
    with ExitStack() as ctx:
        m = Maker(nc, ctx, "last_")
        x = m.sb("x", [P, TT, D])
        o = m.sb("o", [P, TT, D])
        gain = m.sb("gain", [P, D])
        squares = m.sb("squares", [P, D])
        stat = m.sb("stat", [P, TT, 5])
        x_in = [sems(f"acc_in{t}") for t in range(TT)]
        gain_in, squared, var_ready, rooted, step, out_ready, stored = (
            sems(n) for n in ("gain_in", "h_squared", "h_var_ready", "h_rooted", "h_dve_step", "out_ready", "out_stored"))

        with nc.Block() as block:

            @block.sync
            def _(sp):
                src, dst = a["acc_d"].rearrange("(t p) d -> t p d", p=P), out[0].rearrange("(t p) d -> t p d", p=P)
                for t in range(TT):
                    sp.dma_start(x[:, t], src[t]).then_inc(x_in[t], 16)
                sp.dma_start(gain[:], bass.AP(a["final_g"].tensor, 0, [[0, P], [1, D]])).then_inc(gain_in, 16)
                for t in range(TT):
                    sp.wait_ge(out_ready, t + 1)
                    sp.dma_start(dst[t], o[:, t]).then_inc(stored, 16)
                sp.wait_ge(stored, 16 * TT)

            @block.scalar
            def _(act):
                for t in range(TT):
                    act.wait_ge(x_in[t], 16)
                    if t:
                        act.wait_ge(squared, t)
                    act.activation(squares[:], x[:, t], ACT.Square, accum_out=stat[:, t, 0:1]).then_inc(squared, 1)
                    act.wait_ge(var_ready, t + 1)
                    act.activation(stat[:, t, 2:3], stat[:, t, 1:2], ACT.Sqrt).then_inc(rooted, 1)

            @block.vector
            def _(dve):
                dt = Tally(dve, step)
                dve.wait_ge(gain_in, 16)
                for t in range(TT):
                    st = [stat[:, t, i:i + 1] for i in range(5)]
                    dve.wait_ge(squared, t + 1)
                    dve.tensor_scalar(st[1], st[0], 1.0 / D, EPS, ALU.mult, ALU.add).then_inc(var_ready, 1)
                    inverse_root(dve, dt, lambda: dve.wait_ge(rooted, t + 1), st[1], st[2], st[3], st[4])
                    dve.scalar_tensor_tensor(out=o[:, t], in0=x[:, t], scalar=st[3], in1=gain[:], op0=ALU.mult,
                                             op1=ALU.mult).then_inc(out_ready, 1)


def program(nc, a, out):
    with ExitStack() as ctx:
        m = Maker(nc, ctx)
        sems = m.sem
        for name, shape in (("mod_d", (2, 6 * D)), ("u_d", (3 * HY, T)), ("qk_d", (2 * HY, W)), ("g_d", (2 * D, T)),
                            ("acc_d", (T, D)), ("h2_d", (T, D))):
            a[name] = nc.dram_tensor(name, shape, F32, kind="Internal").ap()
        keep = {"ident": m.sb("identity", [P, P]), "par": m.sb("par", [P, N_PAR])}
        with ExitStack() as mixer:
            with ExitStack() as values:
                with ExitStack() as projection:
                    n = Maker(nc, projection)
                    keep["h_hi"] = n.sb("h_hi", [P, KD, W], F32R)
                    keep["h_lo"] = n.sb("h_lo", [P, KD, W], F32R)
                    modulate_and_norm(nc, sems, a, keep)
                    v_tok = Maker(nc, values).sb("v_tok", [P, NT, 512], side="right")
                    project(nc, sems, a, keep, v_tok)
                n = Maker(nc, mixer)
                na_t = n.sb("na_t", [P, 4, T])
                attend(nc, sems, a, keep, v_tok, na_t)
            y_t = n.sb("y_t", [P, 4, T])
            hyena(nc, sems, a, keep, y_t)
            merged = ExitStack()
            m_t = Maker(nc, merged).sb("m_t", [P, KD, T], side="right")
            merge(nc, sems, a, y_t, na_t, m_t)
        with ExitStack() as routing:
            logits = Maker(nc, routing).psum("logits", [P, 512])
            with merged:
                project_out(nc, sems, a, keep, m_t, logits)
            n = Maker(nc, ctx)
            gate_col = n.sb("gate_col", [P, E_N])
            idx_col = n.sb("idx_col", [P, E_N], U32)
            raw = n.sb("raw", [P, RAW, 2048])
            raw_in = [sems(f"raw_in{s}") for s in range(RAW)]
            choose(nc, sems, a, keep, logits, raw, raw_in, gate_col, idx_col)
        experts(nc, sems, a, keep, raw, raw_in, gate_col, idx_col)
        last_norm(nc, sems, a, out)


def laid_out(inputs):
    x = {k: np.asarray(v) for k, v in inputs.items()}
    arrays = {
        "x": x["x"][0], "ctx": x["ctx"][0], "c": x["c"][0], "c_ctx": x["c_ctx"],
        "w_mod": x["w_mod"][0], "b_mod": x["b_mod"][0], "norm1_g": x["norm1_g"].reshape(-1, P),
        "w_in": x["w_in"][0], "b_in": x["b_in"].reshape(-1, P),
        "hy_short_w": x["hy_short_w"].reshape(-1, P), "hy_short_b": x["hy_short_b"].reshape(-1, P),
        "hy_skip": x["hy_skip"].reshape(-1, P),
    }
    rpb = np.pad(x["na_rpb"][0], ((0, 0), (0, 0), (48, P - 48 - (2 * WIN_W - 1))))
    arrays["rpb"] = rpb[:, :, ::-1]
    col = np.arange(GRID_W)
    start = np.clip(col - WIN_W // 2, 0, GRID_W - WIN_W)[:, None]
    seen = (col[None, :] >= start) & (col[None, :] < start + WIN_W)
    arrays["na_mask"] = np.tile(np.where(seen, 0.0, NEG).astype(np.float32), (2, 1))
    arrays["filt_w1"], arrays["filt_w2"], arrays["filt_w3"] = (x["filt_w" + n][0] for n in "123")
    arrays["filt_cols"] = np.stack([x[n][0] for n in ("filt_freq", "filt_b1", "filt_b2")], axis=1)
    pos = np.arange(T, dtype=np.float32)
    t = pos / np.float32(T - 1)
    bands = np.linspace(1e-4, (FEMB - 1) // 2 - 1, (FEMB - 1) // 2, dtype=np.float32)
    ang = (np.float32(2.0 * math.pi) * pos / np.float32(T))[:, None] * bands[None, :]
    arrays["feats"] = np.concatenate([t[:, None], np.cos(ang), -np.sin(ang)], axis=1).astype(np.float32).T
    deltas = np.linspace(math.log(1e-2) / 1.5, math.log(1e-2) / 0.3, HY, dtype=np.float32)
    arrays["decay"] = np.exp(-t[:, None] * np.abs(deltas)[None, :]).astype(np.float32)
    f = 2 * np.arange(P)[None, :] + np.arange(2)[:, None]
    turn = np.arange(BLK)[:, None, None] * (f[None] + 0.5) * (2.0 * math.pi / (2 * BLK))
    planes = np.stack([np.cos(turn), -np.sin(turn)], axis=2)
    arrays["dft"] = planes.reshape(2, P, 4, P).transpose(1, 0, 2, 3).astype(np.float32)
    arrays["idft"] = (planes.reshape(BLK, 4, P).transpose(2, 1, 0) / BLK).astype(np.float32)
    arrays.update({k: x[k][0] for k in ("w_branch_hy", "w_branch_na", "w_out", "w_router", "w_gate", "w_up", "w_down")})
    arrays["norm2_g"], arrays["final_g"] = x["norm2_g"], x["final_g"].reshape(1, -1)
    arrays["ident"] = np.eye(P, dtype=np.float32)
    return {k: np.ascontiguousarray(v) for k, v in arrays.items()}


def kernel(**inputs):
    import concourse.bacc as bacc
    from concourse.bass_utils import run_bass_kernel_spmd as run

    nc = bacc.Bacc("TRN2", target_bir_lowering=False, num_devices=1)
    arrays = {"in_" + k: v for k, v in laid_out(inputs).items()}
    a = {k[3:]: nc.dram_tensor(k, v.shape, mybir.dt.from_np(v.dtype), kind="ExternalInput").ap()
         for k, v in arrays.items()}
    out = nc.dram_tensor("out", (1, T, D), F32, kind="ExternalOutput").ap()
    program(nc, a, out)
    return run(nc, [arrays], core_ids=[0]).results[0]["out"]
```

```python
import math
from contextlib import ExitStack

import numpy as np

import concourse.bass as bass
from concourse import mybir

F32 = mybir.dt.float32
F32R = mybir.dt.float32r
U32 = mybir.dt.uint32
ALU = mybir.AluOpType
ACT = mybir.ActivationFunctionType
AX_X = mybir.AxisListType.X

P = 128
T = 1024
D = 1024
CTX = 256
W = T + CTX
KD = D // P
TT = T // P
NT = W // P
EPS = 1e-6
HY = 512
HEADS, HD = 8, 64
GRID_W = 64
ROWS = T // GRID_W
WIN_H, WIN_W = 8, 16
E_N, CAP, FF = 16, 128, 2816
FC = 64
FEMB = 17
P_IN = 5 * D
NEG = -1.0e30

C_NORM1, C_BIN, C_SW, C_SB, C_SKIP, N_PAR = 0, 8, 48, 84, 96, 104

UNIT = 256
CH_UNIT = UNIT // P


class Tally:

    def __init__(self, eng, sem):
        self.eng, self.sem, self.done, self.turn = eng, sem, 0, 0

    def inc(self, ins):
        ins.then_inc(self.sem, 1)
        self.done += 1

    def wait(self, but=0):
        self.eng.wait_ge(self.sem, self.turn + self.done - but)

    def then_wait(self, ins):
        self.inc(ins)
        self.wait()

    def enter(self, i, per):
        self.start, self.per = self.done, per
        self.turn = i * per

    def leave(self, turns):
        assert self.done - self.start == self.per, (self.done - self.start, self.per)
        self.done, self.turn = self.start + turns * self.per, 0


class Maker:

    def __init__(self, nc, ctx, phase=""):
        self.nc, self.ctx, self.phase = nc, ctx, phase

    def sb(self, name, shape, dt=F32, side="left"):
        return self.ctx.enter_context(self.nc.sbuf_tensor(self.phase + name, shape, dt, side=side))

    def psum(self, name, shape):
        return self.ctx.enter_context(self.nc.psum_tensor(self.phase + name, shape, F32))

    def sem(self, name):
        return self.ctx.enter_context(self.nc.semaphore(name))


def inverse_root(dve, dt, act_sqrt, var, root, inv, tmp):
    act_sqrt()
    dt.then_wait(dve.reciprocal(inv, root))
    dt.then_wait(dve.tensor_tensor(tmp, var, inv, ALU.mult))
    dt.then_wait(dve.tensor_tensor(tmp, tmp, inv, ALU.mult))
    dt.then_wait(dve.tensor_scalar(tmp, tmp, -0.5, 1.5, ALU.mult, ALU.add))
    dt.then_wait(dve.tensor_tensor(inv, inv, tmp, ALU.mult))


def modulate_and_norm(nc, sems, a, keep):
    h_hi, h_lo, par, ident = keep["h_hi"], keep["h_lo"], keep["par"], keep["ident"]
    NC = 6 * D // 512
    with ExitStack() as ctx:
        m = Maker(nc, ctx, "norm_")
        x_raw = m.sb("x_raw", [P, NT, D])
        w_mod = m.sb("w_mod", [P, 2, KD, 512])
        mod_row = m.sb("mod_row", [2, NC, 512])
        par_rows = m.sb("par_rows", [N_PAR, P])
        c_col = m.sb("c_col", [P, 2, KD])
        c_silu = m.sb("c_silu", [P, KD, 2])
        ss = m.sb("ss", [P, NT])
        var = m.sb("var", [P, NT])
        root = m.sb("root", [P, NT])
        inv = m.sb("inv", [P, NT])
        tmp = m.sb("tmp", [P, NT])
        scale_col = m.sb("scale_col", [P, 2, KD])
        shift_col = m.sb("shift_col", [P, 2, KD])
        h_full = m.sb("h_full", [P, 2, 512])
        ps_mod = m.psum("ps_mod", [P, 2, 512])
        ps_col = m.psum("ps_col", [P, 512])
        ps_x = m.psum("ps_x", [P, 4, 512])

        rows_in, c_in, x_in, b_in = (sems(n) for n in ("par_rows_in", "c_in", "x_in", "b_mod_in"))
        w_in = [sems(f"w_mod_in{s}") for s in range(2)]
        silu_ready, mod_done, mod_row_ready = (
            sems(n) for n in ("silu_ready", "mod_done", "mod_row_ready"))
        par_done, col_done, dve_step, sq_done, root_done = (
            sems(n) for n in ("par_done", "col_done", "a_dve_step", "sq_done", "root_done"))
        xn_ready, xt_done, full_ready, lo_done, mod_out = (
            sems(n) for n in ("xn_ready", "xt_done", "full_ready", "h_lo_done", "mod_out"))
        cols_ready, var_ready = sems("cols_ready"), sems("var_ready")

        groups = [(0, 4, 0), (4, 4, 0), (8, 2, 1)]
        fills = [(k, g) for k in range(KD) for g in range(3)]

        with nc.Block() as block:

            @block.sync
            def _(sp):
                for n, (name, lo, hi) in enumerate((("norm1_g", C_NORM1, C_BIN), ("b_in", C_BIN, C_SW),
                                                    ("hy_short_w", C_SW, C_SB), ("hy_short_b", C_SB, C_SKIP),
                                                    ("hy_skip", C_SKIP, N_PAR))):
                    sp.dma_start(par_rows[lo:hi, :], a[name]).then_inc(rows_in, 16)
                sp.dma_start(ident[:], a["ident"]).then_inc(rows_in, 16)
                for j, name in enumerate(("c", "c_ctx")):
                    sp.dma_start(c_col[:, j, :], a[name].rearrange("(p k) -> p k", k=KD)).then_inc(c_in, 16)
                    sp.dma_start(mod_row[j:j + 1, :, :], a["b_mod"].rearrange("(o n c) -> o n c", o=1, c=512)
                                 ).then_inc(b_in, 16)
                w_src = a["w_mod"].rearrange("(p k) (n c) -> n p k c", k=KD, c=512)
                with sp.Fori(0, NC // 2) as i:
                    for s in range(2):
                        sp.wait_ge(mod_done, 2 * i + s + 1)
                        sp.dma_start(w_mod[:, s], w_src[2 * i + s]).then_inc(w_in[s], 16)
                sp.dma_start(x_raw[:, 0:TT, :], a["x"].rearrange("(t p) d -> p t d", p=P)).then_inc(x_in, 16)
                sp.dma_start(x_raw[:, TT:NT, :], a["ctx"].rearrange("(t p) d -> p t d", p=P)).then_inc(x_in, 16)
                sp.wait_ge(mod_row_ready, NC + 2)
                sp.dma_start(a["mod_d"].rearrange("j (n c) -> j n c", c=512), mod_row[:]).then_inc(mod_out, 16)
                sp.wait_ge(mod_out, 16)

            @block.tensor
            def _(pe):
                pe.sem_inc(mod_done, 2)
                pe.wait_ge(rows_in, 6 * 16)
                pe.transpose(ps_col[:, 0:N_PAR], par_rows[:], ident[0:N_PAR, 0:N_PAR]).then_inc(par_done, 1)
                pe.wait_ge(silu_ready, 1)
                with pe.Fori(0, NC // 2) as i:
                    for s in range(2):
                        pe.wait_ge(w_in[s], 16 * i + 16)
                        pe.wait_ge(mod_row_ready, 2 * i + s + 1)
                        for k in range(KD):
                            mm = pe.matmul(ps_mod[0:2, s, :], c_silu[:, k, :], w_mod[:, s, k, :],
                                           start=(k == 0), stop=(k == KD - 1))
                        mm.then_inc(mod_done, 1)
                pe.wait_ge(mod_row_ready, NC + 2)
                pe.wait_ge(cols_ready, 1)
                flat = mod_row[:].rearrange("j n c -> j (n c)")
                for k in range(2 * KD):
                    mm = pe.transpose(ps_col[:, 2 * k:2 * k + 2], flat[:, k * P:(k + 1) * P], ident[0:2, 0:2])
                mm.then_inc(col_done, 1)
                pe.wait_ge(xn_ready, NT)
                for n, (k, g) in enumerate(fills):
                    t0, nt, _ = groups[g]
                    if n >= 4:
                        pe.wait_ge(full_ready, n - 3)
                    for t in range(nt):
                        mm = pe.transpose(ps_x[:, n % 4, t * P:(t + 1) * P],
                                          x_raw[:, t0 + t, k * P:(k + 1) * P], ident[:])
                    mm.then_inc(xt_done, 1)

            @block.scalar
            def _(act):
                act.wait_ge(c_in, 32)
                act.activation(c_silu[:].rearrange("p k j -> p j k"), c_col[:], ACT.Silu).then_inc(silu_ready, 1)
                act.wait_ge(x_in, 32)
                for t in range(NT):
                    if t:
                        act.wait_ge(sq_done, t)
                    act.activation(h_full[:].rearrange("p a b -> p (a b)"), x_raw[:, t, :], ACT.Square, accum_out=ss[:, t:t + 1]).then_inc(sq_done, 1)
                act.wait_ge(var_ready, 1)
                act.activation(root[:], var[:], ACT.Sqrt).then_inc(root_done, 1)
                act.wait_ge(cols_ready, 2)
                for n, (k, g) in enumerate(fills):
                    t0, nt, j = groups[g]
                    cols = slice(t0 * P, (t0 + nt) * P)
                    sc, sh = scale_col[:, j, k:k + 1], shift_col[:, j, k:k + 1]
                    act.wait_ge(xt_done, n + 1)
                    act.activation(h_hi[:, k, cols], ps_x[:, n % 4, 0:nt * P], ACT.Identity, bias=sh, scale=sc)
                    if n >= 2:
                        act.wait_ge(lo_done, n - 1)
                    act.activation(h_full[:, n % 2, 0:nt * P], ps_x[:, n % 4, 0:nt * P], ACT.Identity,
                                   bias=sh, scale=sc).then_inc(full_ready, 1)

            @block.vector
            def _(dve):
                dt = Tally(dve, dve_step)
                dve.sem_inc(mod_row_ready, 2)
                dve.wait_ge(par_done, 1)
                dve.tensor_copy(par[:], ps_col[:, 0:N_PAR]).then_inc(cols_ready, 1)
                dve.wait_ge(b_in, 32)
                with dve.Fori(0, NC // 2) as i:
                    for s in range(2):
                        dve.wait_ge(mod_done, 2 * i + s + 3)
                        dve.tensor_tensor(mod_row[:, 2 * i + s, :], ps_mod[0:2, s, :], mod_row[:, 2 * i + s, :],
                                          ALU.add).then_inc(mod_row_ready, 1)
                dve.wait_ge(col_done, 1)
                dve.wait_ge(cols_ready, 1)
                col = ps_col[:, 0:4 * KD].rearrange("p (w k j) -> p w j k", w=2, j=2)
                dve.tensor_copy(shift_col[:], col[:, 0])
                for j in range(2):
                    ins = dve.scalar_tensor_tensor(out=scale_col[:, j, :], in0=col[:, 1, j, :], scalar=1.0,
                                                   in1=par[:, C_NORM1:C_BIN], op0=ALU.add, op1=ALU.mult)
                ins.then_inc(cols_ready, 1)
                dve.wait_ge(sq_done, NT)
                dve.tensor_scalar(var[:], ss[:], 1.0 / D, EPS, ALU.mult, ALU.add).then_inc(var_ready, 1)
                inverse_root(dve, dt, lambda: dve.wait_ge(root_done, 1), var[:], root[:], inv[:], tmp[:])
                for t in range(NT):
                    dve.tensor_scalar(x_raw[:, t, :], x_raw[:, t, :], inv[:, t:t + 1], None, ALU.mult
                                      ).then_inc(xn_ready, 1)
                for n, (k, g) in enumerate(fills):
                    t0, nt, _ = groups[g]
                    cols = slice(t0 * P, (t0 + nt) * P)
                    dve.wait_ge(full_ready, n + 1)
                    dve.tensor_tensor(h_lo[:, k, cols], h_full[:, n % 2, 0:nt * P], h_hi[:, k, cols].bitcast(F32),
                                      ALU.subtract).then_inc(lo_done, 1)


SEG_HY, SEG_Q, SEG_K, SEG_V, SEG_G = (0, 6), (6, 2), (8, 2), (10, 2), (12, 8)
N_UNITS = P_IN // UNIT


def project(nc, sems, a, keep, v_tok):
    h_hi, h_lo, par = keep["h_hi"], keep["h_lo"], keep["par"]
    with ExitStack() as ctx:
        m = Maker(nc, ctx, "proj_")
        w_raw = m.sb("w_raw", [P, 2, KD, UNIT])
        w_hi = m.sb("w_hi", [P, 2, KD, UNIT], F32R)
        w_lo = m.sb("w_lo", [P, 2, KD, UNIT], F32R)
        z_pad = m.sb("z_pad", [P, 2, T + 2])
        conv = m.sb("conv", [P, 2, T])
        stage = m.sb("stage", [P, 2, W])
        q_bias = m.sb("q_bias", [P, 4])
        bias = m.sb("bias", [P, CH_UNIT])
        bv_row = m.sb("bv_row", [1, 512])
        ones = m.sb("ones", [1, P])
        ps = m.psum("ps", [P, 8, 512])

        w_in = [sems(f"w_in{s}") for s in range(2)]
        hi_ready, lo_ready, z_done, evacuated, conv_ready = (
            sems(n) for n in ("w_hi_ready", "w_lo_ready", "z_done", "evacuated", "conv_ready"))
        stored = [sems(f"stored{s}") for s in range(2)]
        b_dve, bv_in, const_ready, bias_ready = (
            sems(n) for n in ("b_dve_step", "bv_in", "const_ready", "bias_ready"))

        n_q = 4 * SEG_HY[1]
        n_k = n_q + 4 * SEG_Q[1]
        n_v = n_k + 5 * SEG_K[1]
        n_g = n_v + 5 * SEG_V[1]

        with nc.Block() as block:

            @block.sync
            def _(sp):
                src = a["w_in"].rearrange("(k p) (u n) -> u p k n", p=P, n=UNIT)
                u_d = a["u_d"].rearrange("(c p) t -> c p t", p=P)
                qk_d = a["qk_d"].rearrange("(c p) t -> c p t", p=P)
                g_d = a["g_d"].rearrange("(c p) t -> c p t", p=P)

                def load(u, s):
                    sp.wait_ge(lo_ready, u + 1)
                    sp.dma_start(w_raw[:, s], src[u]).then_inc(w_in[s], 16)

                def store_conv(u):
                    for c in range(CH_UNIT):
                        sp.wait_ge(conv_ready, CH_UNIT * u + c + 3)
                        sp.dma_start(u_d[CH_UNIT * u + c], conv[:, c, :]).then_inc(stored[c], 16)

                def store_stage(n, dst, c0, cols):
                    for c in range(CH_UNIT):
                        sp.wait_ge(evacuated, n + (5 if cols == W else 2 * c + 2) + 8)
                        sp.dma_start(dst[c0 + c, :, 0:cols], stage[:, c, 0:cols]).then_inc(stored[c], 16)

                sp.sem_inc(stored[0], 16)
                sp.sem_inc(stored[1], 16)
                sp.dma_start(bv_row[:], a["b_in"].rearrange("(o r) c -> o (r c)", o=1)[:, 5 * 512:6 * 512]
                             ).then_inc(bv_in, 16)
                load(0, 0)
                load(1, 1)
                with sp.Fori(0, SEG_HY[1] // 2) as i:
                    for s in range(2):
                        load(2 * i + s + 2, s)
                        store_conv(2 * i + s)
                for s in range(2):
                    load(SEG_Q[0] + s + 2, s)
                    store_stage(n_q + 4 * s, qk_d, CH_UNIT * s, T)
                for s in range(2):
                    load(SEG_K[0] + s + 2, s)
                    store_stage(n_k + 5 * s, qk_d, 4 + CH_UNIT * s, W)
                for s in range(2):
                    load(SEG_V[0] + s + 2, s)
                with sp.Fori(0, SEG_G[1] // 2 - 1) as i:
                    for s in range(2):
                        load(SEG_G[0] + 2 * i + s + 2, s)
                        store_stage(n_g + 8 * i + 4 * s, g_d, 4 * i + CH_UNIT * s, T)
                for s in range(2):
                    store_stage(n_g + 24 + 4 * s, g_d, 12 + CH_UNIT * s, T)
                for s in range(2):
                    sp.wait_ge(stored[s], 16 * (6 + 2 + 2 + 8 + 1))

            @block.tensor
            def _(pe):
                pe.sem_inc(z_done, 4)

                def begin(u):
                    pe.wait_ge(lo_ready, u + 3)

                def latents(s, n, n8):
                    for c in range(CH_UNIT):
                        banks = [(n8 + 2 * c + th) % 8 for th in range(2)]
                        pe.wait_ge(evacuated, n + 2 * c + 2)
                        for k in range(KD):
                            hi, lo = (w[:, s, k, c * P:(c + 1) * P] for w in (w_hi, w_lo))
                            for w, h, first, last in ((hi, h_hi, True, False), (hi, h_lo, False, False),
                                                      (lo, h_hi, False, True)):
                                for th in range(2):
                                    mm = pe.matmul(ps[:, banks[th], :], w, h[:, k, th * 512:(th + 1) * 512],
                                                   start=(k == 0 and first), stop=(k == KD - 1 and last))
                                    if k == KD - 1 and last:
                                        mm.then_inc(z_done, 1)

                with pe.Fori(0, SEG_HY[1] // 2) as i:
                    for s in range(2):
                        begin(2 * i + s)
                        latents(s, 8 * i + 4 * s, 4 * s)
                for s in range(2):
                    begin(SEG_Q[0] + s)
                    latents(s, n_q + 4 * s, (n_q + 4 * s) % 8)
                for s in range(2):
                    n = n_k + 5 * s
                    begin(SEG_K[0] + s)
                    latents(s, n, n % 8)
                    n += 4
                    pe.wait_ge(evacuated, n + 1)
                    for c in range(CH_UNIT):
                        for k in range(KD):
                            for x, (w, h) in enumerate(((w_hi, h_hi), (w_hi, h_lo), (w_lo, h_hi))):
                                mm = pe.matmul(ps[:, n % 8, c * CTX:(c + 1) * CTX], w[:, s, k, c * P:(c + 1) * P],
                                               h[:, k, T:W], start=(k == 0 and x == 0), stop=(k == KD - 1 and x == 2))
                    mm.then_inc(z_done, 1)
                pe.wait_ge(bv_in, 16)
                pe.wait_ge(const_ready, 1)
                for s in range(2):
                    begin(SEG_V[0] + s)
                    for tp in range(NT // 2):
                        n = n_v + 5 * s + tp
                        pe.wait_ge(evacuated, n + 1)
                        for t in range(2):
                            o = ps[:, n % 8, t * UNIT:(t + 1) * UNIT]
                            tok = slice((2 * tp + t) * P, (2 * tp + t + 1) * P)
                            pe.matmul(o, ones[:], bv_row[:, s * UNIT:(s + 1) * UNIT], start=True, stop=False)
                            for k in range(KD):
                                for x, (w, h) in enumerate(((w_hi, h_hi), (w_lo, h_hi), (w_hi, h_lo))):
                                    mm = pe.matmul(o, h[:, k, tok], w[:, s, k, :], start=False,
                                                   stop=(k == KD - 1 and x == 2))
                        mm.then_inc(z_done, 1)
                with pe.Fori(0, SEG_G[1] // 2) as i:
                    for s in range(2):
                        begin(SEG_G[0] + 2 * i + s)
                        latents(s, n_g + 8 * i + 4 * s, (n_g + 4 * s) % 8)

            @block.scalar
            def _(act):
                act.sem_inc(evacuated, 8)

                def split(s, i, before):
                    act.wait_ge(w_in[s], 16 * i + 16)
                    if before is not None:
                        act.wait_ge(z_done, before + 4)
                    act.activation(w_hi[:, s], w_raw[:, s], ACT.Copy).then_inc(hi_ready, 1)

                def evacuate(n, bank, out, func, bias, scale=1.0):
                    act.wait_ge(z_done, n + 5)
                    act.activation(out, ps[:, bank, :], func, bias=bias, scale=scale).then_inc(evacuated, 1)

                def own_bias(c, ch, count):
                    act.activation(bias[:, c:c + 1], par[:, bass.ds(C_BIN + ch, 1)], ACT.Copy).then_inc(bias_ready, 1)
                    act.wait_ge(bias_ready, count)
                    return bias[:, c:c + 1]

                act.wait_ge(const_ready, 2)
                split(0, 0, None)
                with act.Fori(0, SEG_HY[1] // 2) as i:
                    for s in range(2):
                        split(1 - s, i + s, 8 * i + 4 * s)
                        for c in range(CH_UNIT):
                            ch = 4 * i + 2 * s + c
                            b = own_bias(c, ch, ch + 1)
                            act.wait_ge(conv_ready, ch + 1)
                            for th in range(2):
                                evacuate(8 * i + 4 * s + 2 * c + th, 4 * s + 2 * c + th,
                                         z_pad[:, c, 1 + th * 512:1 + (th + 1) * 512], ACT.Identity, b)
                for s in range(2):
                    n = n_q + 4 * s
                    split(1 - s, (SEG_Q[0] + s + 1) // 2, n)
                    for c in range(CH_UNIT):
                        ch = CH_UNIT * s + c
                        act.wait_ge(stored[c], 16 * (7 + s))
                        for th in range(2):
                            evacuate(n, n % 8, stage[:, c, th * 512:(th + 1) * 512], ACT.Identity,
                                     q_bias[:, ch:ch + 1], HD ** -0.5)
                            n += 1
                for s in range(2):
                    n = n_k + 5 * s
                    split(1 - s, (SEG_K[0] + s + 1) // 2, n)
                    biases = [par[:, b:b + 1] for b in range(C_BIN + 16 + CH_UNIT * s, C_BIN + 18 + CH_UNIT * s)]
                    for c in range(CH_UNIT):
                        act.wait_ge(stored[c], 16 * (9 + s))
                        for th in range(2):
                            evacuate(n, n % 8, stage[:, c, th * 512:(th + 1) * 512], ACT.Identity, biases[c])
                            n += 1
                    act.wait_ge(z_done, n + 5)
                    for c in range(CH_UNIT):
                        ins = act.activation(stage[:, c, T:W], ps[:, n % 8, c * CTX:(c + 1) * CTX],
                                             ACT.Identity, bias=biases[c])
                    ins.then_inc(evacuated, 1)
                for s in range(2):
                    split(1 - s, (SEG_V[0] + s + 1) // 2, n_v + 5 * s)
                    for tp in range(NT // 2):
                        n = n_v + 5 * s + tp
                        act.wait_ge(z_done, n + 5)
                        act.activation(v_tok[:, 2 * tp:2 * tp + 2, s * UNIT:(s + 1) * UNIT],
                                       ps[:, n % 8, :].rearrange("p (t c) -> p t c", t=2), ACT.Copy
                                       ).then_inc(evacuated, 1)

                def gates(i, s, last=False):
                    u = 2 * i + s
                    if not last:
                        split(1 - s, SEG_G[0] // 2 + i + s, n_g + 4 * u)
                    for c in range(CH_UNIT):
                        b = own_bias(c, 24 + 2 * u + c, 12 + 2 * u + c + 1)
                        act.wait_ge(stored[c], 16 * (11 + u))
                        for th in range(2):
                            evacuate(n_g + 4 * u + 2 * c + th, (n_g + 4 * s + 2 * c + th) % 8,
                                     stage[:, c, th * 512:(th + 1) * 512], ACT.Sigmoid, b)

                with act.Fori(0, SEG_G[1] // 2 - 1) as i:
                    for s in range(2):
                        gates(i, s)
                gates(SEG_G[1] // 2 - 1, 0)
                gates(SEG_G[1] // 2 - 1, 1, last=True)

            @block.vector
            def _(dve):
                dt = Tally(dve, b_dve)
                dve.sem_inc(lo_ready, 2)
                dve.sem_inc(conv_ready, 2)
                dt.inc(dve.memset(z_pad[:, :, 0:1], 0.0))
                dt.inc(dve.memset(z_pad[:, :, T + 1:T + 2], 0.0))
                dve.memset(ones[:], 1.0).then_inc(const_ready, 1)
                dve.tensor_scalar(q_bias[:], par[:, C_BIN + 12:C_BIN + 16], HD ** -0.5, None, ALU.mult
                                  ).then_inc(const_ready, 1)
                dt.wait()

                def split(u, s):
                    dve.wait_ge(hi_ready, u + 1)
                    dve.tensor_tensor(w_lo[:, s], w_raw[:, s], w_hi[:, s].bitcast(F32), ALU.subtract
                                      ).then_inc(lo_ready, 1)

                split(0, 0)
                with dve.Fori(0, SEG_HY[1] // 2) as i:
                    dt.enter(i, 8)
                    for s in range(2):
                        split(2 * i + s + 1, 1 - s)
                        for c in range(CH_UNIT):
                            ch = 4 * i + 2 * s + c

                            def w(j):
                                return par[:, bass.ds(C_SW + 12 * j + ch, 1)]

                            dve.wait_ge(evacuated, 2 * ch + 2 + 8)
                            dve.wait_ge(stored[c], 16 * (2 * i + s + 1))
                            dt.then_wait(dve.tensor_scalar(conv[:, c], z_pad[:, c, 1:T + 1], w(1),
                                                           par[:, bass.ds(C_SB + ch, 1)], ALU.mult, ALU.add))
                            dt.then_wait(dve.scalar_tensor_tensor(out=conv[:, c], in0=z_pad[:, c, 0:T], scalar=w(0),
                                                                  in1=conv[:, c], op0=ALU.mult, op1=ALU.add))
                            dve.scalar_tensor_tensor(out=conv[:, c], in0=z_pad[:, c, 2:T + 2], scalar=w(2),
                                                     in1=conv[:, c], op0=ALU.mult, op1=ALU.add
                                                     ).then_inc(conv_ready, 1)
                    dt.leave(SEG_HY[1] // 2)
                for u in range(SEG_Q[0] + 1, SEG_G[0] + 1):
                    split(u, u % 2)
                with dve.Fori(0, SEG_G[1] // 2 - 1) as i:
                    for s in range(2):
                        split(SEG_G[0] + 2 * i + s + 1, 1 - s)
                split(N_UNITS - 1, 1)



def key_rows(i):
    rs = [min(max(r - WIN_H // 2, 0), ROWS - WIN_H) for r in (2 * i, 2 * i + 1)]
    return rs[0], rs[1] + WIN_H - rs[0]


T_ROWS = 14
T_MIN = -6
HALF = P // 2
CTX0 = 5 * P


def attend(nc, sems, a, keep, v_tok, na_t):
    ident = keep["ident"]
    with ExitStack() as ctx:
        m = Maker(nc, ctx, "attn_")
        q_raw = m.sb("q_raw", [P, 2, T])
        k_raw = m.sb("k_raw", [P, 2, W])
        q_two = m.sb("q_two", [P, 2, T], F32R)
        k_hi, k_lo = m.sb("k_hi", [P, 2, W], F32R), m.sb("k_lo", [P, 2, W], F32R)
        t_raw = m.sb("t_raw", [P, 2, T_ROWS, GRID_W])
        table = m.sb("table", [P, 2, T_ROWS, GRID_W])
        edged = m.sb("edged", [P, 2, WIN_H + 1, GRID_W])
        mask = m.sb("mask", [P, GRID_W])
        score = m.sb("score", [P, 2, (WIN_H + 1) * GRID_W])
        prob = m.sb("prob", [P, 2, CTX0 + CTX])
        prob_t = m.sb("prob_t", [P, 2, 7, P])
        top = m.sb("top", [P, 2, 3])
        sums = m.sb("sums", [P, 4, 4])
        na = m.sb("na", [P, TT, P])
        ps_s = m.psum("ps_s", [P, 2, 1024])
        ps_t = m.psum("ps_t", [P, 2, 512])
        ps_o = m.psum("ps_o", [P, 2, 512])

        qk_in, t_in = ([sems(f"{n}{s}") for s in range(2)] for n in ("qk_in", "t_in"))
        mask_in = sems("mask_in")
        q_high, k_high, q_split, k_split, tables, scored, max_ready, exps, turned = (
            sems(n) for n in ("q_high", "k_high", "q_split", "k_split", "tables", "scored", "max_ready", "exps", "turned"))
        copied_a, copied_b, filled, used, step, zeros = (
            sems(n) for n in ("copied_a", "copied_b", "filled", "used", "c_dve_step", "zeros"))
        PAIRS, UNITS, STEPS = HEADS // 2, 2 * TT, 2 * TT + 4

        FILLS = UNITS + TT

        def f_unit(n):
            return n + max(n - TT - 2, 0)

        def f_turn(i):
            return min(UNITS, i + TT + 3) + i

        def blocks(i):
            r0, n = key_rows(i)
            out = [(b, r0 // 2 + b) for b in range(n // 2)]
            if n % 2:
                out.append((4, r0 // 2 + 4))
            return out

        with nc.Block() as block:

            @block.sync
            def _(sp):
                qk = a["qk_d"].rearrange("(w g p) t -> w g p t", w=2, p=HD)
                sp.dma_start(mask[:], a["na_mask"]).then_inc(mask_in, 16)
                rpb = a["rpb"]
                for g in range(HEADS):
                    hh = g % 2
                    if g >= 2:
                        sp.wait_ge(k_split, g - 1)
                        sp.wait_ge(q_split, g - 1)
                    for half in range(2):
                        rows = slice(half * HALF, (half + 1) * HALF)
                        sp.dma_start(q_raw[rows, hh], qk[0, g][:, 0:T]).then_inc(qk_in[hh], 16)
                        sp.dma_start(k_raw[rows, hh], qk[1, g]).then_inc(qk_in[hh], 16)
                    if g >= 2:
                        sp.wait_ge(tables, g - 1)
                    for half in range(2):
                        src = bass.AP(rpb.tensor, (g * 15 + 1 - half) * P + 1, [[1, GRID_W], [P, T_ROWS], [1, GRID_W]])
                        sp.dma_start(t_raw[half * HALF:(half + 1) * HALF, hh], src).then_inc(t_in[hh], 16)
                sp.wait_ge(qk_in[0], 64 * PAIRS)
                sp.wait_ge(t_in[0], 32 * PAIRS)
                sp.sem_inc(qk_in[0], 64)
                sp.sem_inc(t_in[0], 32)

            @block.tensor
            def _(pe):
                pe.sem_inc(scored, 1)
                pe.sem_inc(turned, 2)
                pe.sem_inc(filled, 2)
                with pe.Fori(0, PAIRS) as j:
                    for s in range(STEPS):
                        if s < UNITS:
                            i, hh = s % TT, s // TT
                            r0, rows = key_rows(i)
                            if i == 0:
                                pe.wait_ge(k_split, 2 * j + hh + 1)
                                pe.wait_ge(q_split, 2 * j + hh + 1)
                            cols = [(0, r0 * GRID_W, 512), (512, T, CTX)]
                            if rows > WIN_H:
                                cols = [(0, r0 * GRID_W, 512), (512, r0 * GRID_W + 512, GRID_W), (576, T, CTX)]
                            pe.wait_ge(exps, UNITS * j + s + 1)
                            for o, c, w in cols:
                                for x, k in enumerate((k_hi, k_lo)):
                                    mm = pe.matmul(ps_s[:, s % 2, o:o + w], q_two[:, hh, i * P:(i + 1) * P],
                                                   k[:, hh, c:c + w], start=(x == 0), stop=(x == 1))
                            mm.then_inc(scored, 1)
                        if 1 <= s <= UNITS:
                            n = s - 1
                            pe.wait_ge(exps, UNITS * j + n + 3)
                            pe.wait_ge(copied_a, UNITS * j + n + 1)
                            pe.wait_ge(copied_b, UNITS * j + n + 1)
                            for b, _ in blocks(n % TT) + [(5, 0), (6, 0)]:
                                mm = pe.transpose(ps_t[:, b // 4, (b % 4) * P:(b % 4 + 1) * P],
                                                  prob[:, n % 2, b * P:(b + 1) * P], ident[:])
                            mm.then_inc(turned, 1)
                        if 2 <= s <= UNITS + 1:
                            n = s - 2
                            pe.wait_ge(copied_a, UNITS * j + n + 2)
                            pe.wait_ge(copied_b, UNITS * j + n + 2)
                            f = f_unit(n)
                            pe.wait_ge(used, FILLS * j + f + 1)
                            todo = blocks(n % TT) + [(5, TT), (6, TT + 1)]
                            for x, (b, tile) in enumerate(todo):
                                mm = pe.matmul(ps_o[:, f % 2, 0:HD], prob_t[:, n % 2, b, :],
                                               v_tok[:, tile, bass.ds(j * P + n // TT * HD, HD)],
                                               start=(x == 0), stop=(x == len(todo) - 1))
                            mm.then_inc(filled, 1)
                        if s >= TT + 4:
                            i = s - TT - 4
                            f = f_turn(i)
                            pe.wait_ge(used, FILLS * j + max(f_unit(TT + i) + 3, f + 1))
                            pe.transpose(ps_o[:, f % 2, 0:P], na[:, i, :], ident[:]).then_inc(filled, 1)

            @block.scalar
            def _(act):
                act.sem_inc(exps, 2)
                act.sem_inc(copied_b, 1)
                act.wait_ge(zeros, 1)

                def high(hh, which):
                    dst, src, done = ((q_two, q_raw, q_high), (k_hi, k_raw, k_high))[which]
                    act.activation(dst[:, hh], src[:, hh], ACT.Copy).then_inc(done, 1)

                act.wait_ge(qk_in[0], 64)
                high(0, 0)
                high(0, 1)
                with act.Fori(0, PAIRS) as j:
                    for s in range(UNITS + 1):
                        if s in (1, TT + 1):
                            nh = s // TT
                            act.wait_ge(qk_in[1 - nh], 64 * (j + nh) + 64)
                            act.wait_ge(scored, UNITS * j + TT * nh + 1)
                            high(1 - nh, 0)
                        if s in (3, TT + 3):
                            high(1 - s // TT, 1)
                        if s >= 1:
                            n = s - 1
                            lo = 4 if key_rows(n % TT)[1] > WIN_H else 5
                            act.wait_ge(turned, UNITS * j + n + 3)
                            act.wait_ge(filled, FILLS * j + (f_unit(n - 2) + 3 if n >= 2 else 2))
                            act.activation(prob_t[:, n % 2, lo:7, :], ps_t[:, 1, (lo - 4) * P:3 * P].rearrange(
                                "p (b q) -> p b q", q=P), ACT.Copy).then_inc(copied_b, 1)
                        if s < UNITS:
                            n, w = s, key_rows(s % TT)[1] * GRID_W
                            act.wait_ge(max_ready, UNITS * j + n + 1)
                            act.wait_ge(turned, UNITS * j + n + 1)
                            act.activation(prob[:, n % 2, 0:w], score[:, n % 2, 0:w], ACT.Exp,
                                           bias=top[:, n % 2, 2:3], accum_out=sums[:, n % 4, 0:1])
                            act.activation(prob[:, n % 2, CTX0:CTX0 + CTX], ps_s[:, n % 2, w:w + CTX], ACT.Exp,
                                           bias=top[:, n % 2, 2:3], accum_out=sums[:, n % 4, 1:2]).then_inc(exps, 1)

            @block.vector
            def _(dve):
                dt = Tally(dve, step)
                dve.sem_inc(copied_a, 1)
                dve.sem_inc(used, 2)
                dve.memset(prob[:, :, 9 * GRID_W:CTX0], 0.0).then_inc(zeros, 1)
                dve.memset(edged[0:HALF, :, WIN_H], NEG)
                dve.memset(edged[HALF:P, :, 0], NEG)
                dve.wait_ge(mask_in, 16)

                def low_q(turn, hh):
                    dve.wait_ge(q_high, 2 * turn + hh + 1)
                    dve.tensor_tensor(q_two[HALF:P, hh], q_raw[HALF:P, hh], q_two[HALF:P, hh].bitcast(F32),
                                      ALU.subtract).then_inc(q_split, 1)

                def low_k(turn, hh):
                    dve.wait_ge(k_high, 2 * turn + hh + 1)
                    dve.tensor_tensor(k_lo[:, hh], k_raw[:, hh], k_hi[:, hh].bitcast(F32), ALU.subtract
                                      ).then_inc(k_split, 1)

                def make_table(turn, hh):
                    dve.wait_ge(t_in[hh], 32 * turn + 32)
                    dt.then_wait(dve.tensor_tensor(table[:, hh], t_raw[:, hh, :, ::-1], mask[:].unsqueeze(1).broadcast_to(
                        [P, T_ROWS, GRID_W]), ALU.add))
                    for part, first in ((slice(0, HALF), 0), (slice(HALF, P), 1)):
                        src = table[part, hh, first - WIN_H // 2 - T_MIN:first + WIN_H // 2 - T_MIN]
                        dt.inc(dve.tensor_scalar(edged[part, hh, first:first + WIN_H], src, 1.0, None, ALU.mult))
                    dt.wait()
                    dve.sem_inc(tables, 1)

                low_q(0, 0)
                low_k(0, 0)
                make_table(0, 0)
                with dve.Fori(0, PAIRS) as j:
                    dt.enter(j, 6 + 4 * UNITS)
                    for s in range(STEPS + 1):
                        if s < UNITS:
                            n, i, hh = s, s % TT, s // TT
                            r0, rows = key_rows(i)
                            w = rows * GRID_W
                            first = r0 - 2 * i - T_MIN
                            bias = edged[:, hh] if rows > WIN_H else table[:, hh, first:first + WIN_H]
                            dve.wait_ge(scored, UNITS * j + n + 2)
                            dt.inc(dve.reduce_max(top[:, n % 2, 1:2], ps_s[:, n % 2, w:w + CTX], AX_X))
                            dt.then_wait(dve.tensor_tensor_reduce(score[:, n % 2, 0:w], ps_s[:, n % 2, 0:w],
                                                                 bias.rearrange("p r c -> p (r c)"), 1.0, -3.0e38,
                                                                 ALU.add, ALU.max, top[:, n % 2, 0:1]))
                            dve.tensor_scalar(top[:, n % 2, 2:3], top[:, n % 2, 0:1], top[:, n % 2, 1:2], -1.0,
                                              ALU.max, ALU.mult).then_inc(max_ready, 1)
                        if 1 <= s <= UNITS:
                            n = s - 1
                            dve.wait_ge(turned, UNITS * j + n + 3)
                            dve.wait_ge(filled, FILLS * j + (f_unit(n - 2) + 3 if n >= 2 else 2))
                            dve.tensor_copy(prob_t[:, n % 2, 0:4, :], ps_t[:, 0, :].rearrange(
                                "p (b q) -> p b q", q=P)).then_inc(copied_a, 1)
                        if s % TT in (2, 4, 5) and s < UNITS:
                            make = {2: low_q, 4: low_k, 5: make_table}[s % TT]
                            make(j + s // TT, 1 - s // TT)
                        if s >= TT + 5:
                            i = s - TT - 5
                            f = f_turn(i)
                            dve.wait_ge(filled, FILLS * j + f + 3)
                            dve.tensor_scalar(na_t[:, j, i * P:(i + 1) * P], ps_o[:, f % 2, 0:P], 1.0, None,
                                              ALU.mult).then_inc(used, 1)
                        if 2 <= s <= UNITS + 1:
                            n, i = s - 2, (s - 2) % TT
                            f = f_unit(n)
                            dt.then_wait(dve.tensor_tensor(sums[:, n % 4, 2:3], sums[:, n % 4, 0:1],
                                                           sums[:, n % 4, 1:2], ALU.add))
                            dt.then_wait(dve.reciprocal(sums[:, n % 4, 3:4], sums[:, n % 4, 2:3]))
                            dve.wait_ge(filled, FILLS * j + f + 3)
                            dve.tensor_scalar(na[:, i, n // TT * HD:(n // TT + 1) * HD], ps_o[:, f % 2, 0:HD],
                                              sums[:, n % 4, 3:4], None, ALU.mult).then_inc(used, 1)
                    dt.leave(PAIRS)


BLK = 256
NB = T // BLK
TWO_PI_HI = 6.28125
TWO_PI_LO = 2.0 * math.pi - TWO_PI_HI
ROUND = 1.5 * 2.0 ** 23


HALF_C = HY // 2
PASSES = 4


def hyena(nc, sems, a, keep, y_t):
    par, ident = keep["par"], keep["ident"]
    with ExitStack() as ctx:
        m = Maker(nc, ctx, "hyena_")
        feats = m.sb("feats", [FEMB, T])
        w1 = m.sb("w1", [FEMB, FC])
        w2 = m.sb("w2", [FC, FC])
        w3 = m.sb("w3", [P, 4 * HY])
        mlp_col = m.sb("mlp_col", [FC, 5])
        h2 = m.sb("h2", [P, T])
        dft = m.sb("dft", [P, 2, 4, P])
        idft = m.sb("idft", [P, 4, BLK])
        decay = m.sb("decay", [P, 2, 2, HALF_C])
        seg = m.sb("seg", [P, 2, 2, 2, HALF_C])
        win = m.sb("win", [P, 2, 2, NB, 4, HALF_C])
        u_tok = m.sb("u_tok", [P, TT, HALF_C])
        uf = m.sb("uf", [P, 2, NB, 4, HALF_C])
        arg, turns, h1 = (uf[0:FC, 1, x].rearrange("p a b -> p (a b)") for x in range(3))
        yf = m.sb("yf", [P, 2, 4, HALF_C])
        cross = m.sb("cross", [P, 4, HALF_C])
        t1, t2 = m.sb("t1", [P, 4, HALF_C]), m.sb("t2", [P, 4, HALF_C])
        gate = m.sb("gate", [P, 2, 2, BLK])
        ps_a = m.psum("ps_a", [P, 4, 512])
        ps_tap = m.psum("ps_tap", [P, 2, 512])
        ps_out = m.psum("ps_out", [P, 2, 512])

        consts_in, mlp_ps, mlp_arg, mlp_sin, v_in = (
            sems(n) for n in ("hy_consts_in", "mlp_ps", "mlp_arg", "mlp_sin", "v_in"))
        a_done, a_used, tap_done, tap_used, out_done, out_used, y_ready = (
            sems(n) for n in ("a_done", "a_used", "tap_done", "tap_used", "out_done", "out_used", "yf_ready"))
        step, padded = sems("d_dve_step"), sems("padded")
        decay_in = [sems(f"decay_in{s}") for s in range(2)]
        gate_in = [sems(f"gate_in{s}") for s in range(2)]

        a_order = []
        for q in range(PASSES):
            for i in range(NB):
                a_order += [("seg", q, i, pl) for pl in range(4)] + [("turn", q, i)]
                if i % 2:
                    a_order += [("input", q, i // 2, pl) for pl in range(4)]
        a_at = {what: n for n, what in enumerate(a_order)}
        PER_A = len(a_order) // PASSES

        def split(p):
            return p // 2, p % 2

        with nc.Block() as block:

            @block.sync
            def _(sp):
                for dst, name in ((feats[:], "feats"), (w1[:], "filt_w1"), (w2[:], "filt_w2"), (w3[0:FC, :], "filt_w3"),
                                  (mlp_col[:, 0:3], "filt_cols"), (dft[:], "dft"), (idft[:], "idft")):
                    sp.dma_start(dst, a[name]).then_inc(consts_in, 16)
                u_d = a["u_d"].rearrange("(o c p) t -> o p c t", c=4, p=P)
                sp.dma_start(y_t[:], u_d[0]).then_inc(v_in, 16)
                decays = a["decay"].rearrange("(b s p) c -> b p s c", s=2, p=P)
                for p in range(-1, PASSES):
                    q = p + 1
                    for i in range(NB):
                        if q < PASSES:
                            h = q % 2
                            if NB * q + i >= 2:
                                sp.wait_ge(tap_used, 2 * (NB * q + i) - 2)
                            sp.dma_start(decay[:, i % 2], decays[i][:, :, h * HALF_C:(h + 1) * HALF_C]
                                         ).then_inc(decay_in[i % 2], 16)
                        if p >= 0:
                            o, h = split(p)
                            if NB * p + i >= 2:
                                sp.wait_ge(out_used, NB * p + i - 1)
                            sp.dma_start(gate[:, i % 2], u_d[o + 1][:, 2 * h:2 * h + 2, i * BLK:(i + 1) * BLK]
                                         ).then_inc(gate_in[i % 2], 16)

            @block.tensor
            def _(pe):
                pe.wait_ge(consts_in, 7 * 16)
                for th in range(2):
                    pe.matmul(ps_tap[0:FC, th, :], w1[:], feats[:, th * 512:(th + 1) * 512], start=True, stop=True
                              ).then_inc(mlp_ps, 1)
                pe.wait_ge(mlp_sin, 1)
                for th in range(2):
                    pe.matmul(ps_tap[0:FC, th, :], w2[:], h1[:, th * 512:(th + 1) * 512], start=True, stop=True
                              ).then_inc(mlp_ps, 1)
                pe.wait_ge(v_in, 16)

                def bank(what):
                    n = a_at[what]
                    if n >= 4:
                        pe.wait_ge(a_used, n - 3)
                    return ps_a[:, n % 4, :]

                def taps(q, i):
                    o, h = split(q)
                    for s in range(2):
                        n = 2 * (NB * q + i) + s
                        if n >= 2:
                            pe.wait_ge(tap_used, n - 1)
                        for d in range(2):
                            at = (2 * d + o) * HY + h * HALF_C
                            mm = pe.matmul(ps_tap[:, s, d * HALF_C:(d + 1) * HALF_C],
                                           h2[:, (2 * i + s) * P:(2 * i + s + 1) * P],
                                           w3[:, at:at + HALF_C], start=True, stop=True)
                        mm.then_inc(tap_done, 1)

                pe.wait_ge(mlp_sin, 2)
                pe.wait_ge(padded, 1)
                taps(0, 0)
                for p in range(-1, PASSES):
                    q = p + 1
                    for i in range(NB):
                        if q < PASSES:
                            pe.wait_ge(tap_used, 2 * (NB * q + i) + 2)
                            for pl in range(4):
                                to = bank(("seg", q, i, pl))
                                for s in range(2):
                                    mm = pe.matmul(to, dft[:, s, pl, :], seg[:, i % 2, s].rearrange("p d c -> p (d c)"),
                                                   start=(s == 0), stop=(s == 1))
                                mm.then_inc(a_done, 1)
                            if NB * q + i + 1 < NB * PASSES:
                                taps((NB * q + i + 1) // NB, (i + 1) % NB)
                            o, h = split(q)
                            if o and i == 0:
                                pe.wait_ge(out_used, NB * (q - 2) + NB)
                            to = bank(("turn", q, i))
                            for t in range(2):
                                for c in range(2):
                                    mm = pe.transpose(to[:, (2 * t + c) * P:(2 * t + c + 1) * P],
                                                      y_t[:, 2 * h + c, (2 * i + t) * P:(2 * i + t + 1) * P], ident[:])
                            mm.then_inc(a_done, 1)
                            if i % 2:
                                pe.wait_ge(a_used, a_at["turn", q, i] + 1)
                                for pl in range(4):
                                    to = bank(("input", q, i // 2, pl)).rearrange("p (b c) -> p b c", b=2)
                                    for s in range(2):
                                        mm = pe.matmul(to, dft[:, s, pl, :], u_tok[:, 2 * i - 2 + s:2 * i + 2:2, :],
                                                       start=(s == 0), stop=(s == 1))
                                    mm.then_inc(a_done, 1)
                        if p >= 0:
                            n = NB * p + i
                            pe.wait_ge(y_ready, n + 1)
                            if n >= 2:
                                pe.wait_ge(out_used, n - 1)
                            for c in range(2):
                                for pl in range(4):
                                    mm = pe.matmul(ps_out[:, i % 2, c * BLK:(c + 1) * BLK],
                                                   yf[:, i % 2, pl, c * P:(c + 1) * P], idft[:, pl, :],
                                                   start=(pl == 0), stop=(pl == 3))
                            mm.then_inc(out_done, 1)

            @block.scalar
            def _(act):
                for layer, h in enumerate((h1, h2[0:FC, :])):
                    act.wait_ge(mlp_arg, layer + 1)
                    act.activation(h, arg, ACT.Sin).then_inc(mlp_sin, 1)
                for n, what in enumerate(a_order):
                    kind, q, i = what[0:3]
                    h, src = q % 2, ps_a[:, n % 4, :].rearrange("p (x c) -> p x c", x=2)
                    if kind == "turn":
                        out = u_tok[:, 2 * i:2 * i + 2, :]
                    elif kind == "seg":
                        if q >= 2 and i == 0:
                            act.wait_ge(y_ready, NB * (q - 2) + NB)
                        out = win[:, h, :, i, what[3], :]
                    else:
                        out = uf[:, h, 2 * i:2 * i + 2, what[3], :]
                    act.wait_ge(a_done, n + 1)
                    act.activation(out, src, ACT.Copy).then_inc(a_used, 1)

            @block.vector
            def _(dve):
                dt = Tally(dve, step)
                dve.memset(w3[FC:P, :], 0.0)
                dve.memset(h2[FC:P, :], 0.0).then_inc(padded, 1)
                dve.wait_ge(consts_in, 7 * 16)
                for layer in range(2):
                    dt.then_wait(dve.tensor_tensor(mlp_col[:, 3 + layer:4 + layer], mlp_col[:, 0:1],
                                                   mlp_col[:, 1 + layer:2 + layer], ALU.mult))
                for layer in range(2):
                    for th in range(2):
                        dve.wait_ge(mlp_ps, 2 * layer + th + 1)
                        dt.inc(dve.tensor_scalar(arg[:, th * 512:(th + 1) * 512], ps_tap[0:FC, th, :], mlp_col[:, 0:1],
                                                 mlp_col[:, 3 + layer:4 + layer], ALU.mult, ALU.add))
                    dt.wait()
                    dt.then_wait(dve.tensor_scalar(turns, arg, 1.0 / (2.0 * math.pi), ROUND, ALU.mult, ALU.add))
                    dt.then_wait(dve.tensor_scalar(turns, turns, -ROUND, None, ALU.add))
                    dt.then_wait(dve.scalar_tensor_tensor(out=arg, in0=turns, scalar=-TWO_PI_HI, in1=arg,
                                                          op0=ALU.mult, op1=ALU.add))
                    dt.then_wait(dve.scalar_tensor_tensor(out=arg, in0=turns, scalar=-TWO_PI_LO, in1=arg,
                                                          op0=ALU.mult, op1=ALU.add))
                    dve.tensor_scalar(arg, arg, 3.1415925, -3.1415925, ALU.min, ALU.max).then_inc(mlp_arg, 1)
                    dve.wait_ge(mlp_sin, layer + 1)

                def decayed(q, i):
                    dve.wait_ge(decay_in[i % 2], 16 * (NB // 2 * q + i // 2 + 1))
                    if NB * q + i >= 2:
                        before = NB * q + i - 2
                        dve.wait_ge(a_done, a_at["seg", before // NB, before % NB, 3] + 1)
                    for s in range(2):
                        dve.wait_ge(tap_done, 2 * (NB * q + i) + s + 1)
                        ins = dve.tensor_tensor(
                            seg[:, i % 2, s], ps_tap[:, s, :].rearrange("p (d c) -> p d c", d=2),
                            decay[:, i % 2, s, :].unsqueeze(1).broadcast_to([P, 2, HALF_C]), ALU.mult)
                        if i == 0 and s == 0:
                            dt.then_wait(ins)
                            ins = dve.memset(seg[0:1, 0, 0, 1, :], 0.0)
                        ins.then_inc(tap_used, 1)

                def products(p, i):
                    h, y = p % 2, yf[:, i % 2]
                    planes = "p (e r) c -> p e r c"
                    if NB * p + i >= 2:
                        dve.wait_ge(out_done, NB * p + i - 1)
                    for j in range(NB):
                        k = win[:, h, 0 if i >= j else 1, abs(i - j)].rearrange(planes, e=2)
                        re, im = (k[:, :, x, :].unsqueeze(2).broadcast_to([P, 2, 2, HALF_C]) for x in range(2))
                        u = uf[:, h, j].rearrange(planes, e=2)
                        if j == 0:
                            dt.inc(dve.tensor_tensor(y.rearrange(planes, e=2), re, u, ALU.mult))
                            dt.inc(dve.tensor_tensor(cross[:].rearrange(planes, e=2), im, u, ALU.mult))
                        else:
                            dt.wait(1)
                            dt.inc(dve.tensor_tensor(t1[:].rearrange(planes, e=2), re, u, ALU.mult))
                            dt.wait(1)
                            dt.inc(dve.tensor_tensor(t2[:].rearrange(planes, e=2), im, u, ALU.mult))
                            dt.wait(1)
                            dt.inc(dve.tensor_tensor(y, y, t1[:], ALU.add))
                            dt.wait(1)
                            dt.inc(dve.tensor_tensor(cross[:], cross[:], t2[:], ALU.add if i >= j else ALU.subtract))
                    dt.wait()
                    yv, cv = (x.rearrange(planes, e=2) for x in (y, cross[:]))
                    dt.inc(dve.tensor_tensor(yv[:, :, 0], yv[:, :, 0], cv[:, :, 1], ALU.subtract))
                    dt.inc(dve.tensor_tensor(yv[:, :, 1], yv[:, :, 1], cv[:, :, 0], ALU.add))
                    dt.wait()
                    dve.sem_inc(y_ready, 1)

                def gated(p, i):
                    o, h = split(p)
                    dve.wait_ge(out_done, NB * p + i + 1)
                    dve.wait_ge(gate_in[i % 2], 16 * (NB // 2 * p + i // 2 + 1))
                    for c in range(2):
                        ch, tok = 2 * h + c, slice(i * BLK, (i + 1) * BLK)
                        dt.inc(dve.scalar_tensor_tensor(
                            out=y_t[:, ch, tok], in0=y_t[:, ch, tok], scalar=par[:, C_SKIP + 4 * o + ch:C_SKIP + 4 * o + ch + 1],
                            in1=ps_out[:, i % 2, c * BLK:(c + 1) * BLK], op0=ALU.mult, op1=ALU.add))
                    dt.wait()
                    pair = y_t[:, 2 * h:2 * h + 2, i * BLK:(i + 1) * BLK]
                    dve.tensor_tensor(pair, pair, gate[:, i % 2], ALU.mult).then_inc(out_used, 1)

                for p in range(-1, PASSES):
                    q = p + 1
                    for i in range(NB):
                        if q < PASSES:
                            decayed(q, i)
                        if p >= 0:
                            products(p, i)
                            if i:
                                gated(p, i - 1)
                    if q < PASSES:
                        h = q % 2
                        dve.wait_ge(a_used, PER_A * (q + 1))
                        for b in range(NB - 1, 0, -1):
                            new, old = (win[:, h, :, x].rearrange("p d (e r) c -> p d e r c", e=2) for x in (b, b - 1))
                            for e, (re, im) in enumerate(((ALU.subtract, ALU.add), (ALU.add, ALU.subtract))):
                                dt.inc(dve.tensor_tensor(new[:, :, e, 0], new[:, :, e, 0], old[:, :, e, 1], re))
                                dt.inc(dve.tensor_tensor(new[:, :, e, 1], new[:, :, e, 1], old[:, :, e, 0], im))
                            dt.wait()
                        w0, f0 = (win[:, h, d, 0].rearrange("p (e r) c -> p e r c", e=2) for d in range(2))
                        dt.inc(dve.tensor_tensor(w0[:, :, 0], w0[:, :, 0], f0[:, :, 0], ALU.add))
                        dt.inc(dve.tensor_tensor(w0[:, :, 1], w0[:, :, 1], f0[:, :, 1], ALU.subtract))
                        dt.wait()
                    if p >= 0:
                        gated(p, NB - 1)


def merge(nc, sems, a, y_t, na_t, m_t):
    with ExitStack() as ctx:
        m = Maker(nc, ctx, "merge_")
        in_hi, in_lo = m.sb("in_hi", [P, 2, 4, T], F32R), m.sb("in_lo", [P, 2, 4, T], F32R)
        b_raw = m.sb("b_raw", [P, 2, 2, 4, P])
        b_hi, b_lo = m.sb("b_hi", [P, 2, 2, 4, P], F32R), m.sb("b_lo", [P, 2, 2, 4, P], F32R)
        gate = m.sb("gate", [P, 2, 2, T])
        part = m.sb("part", [P, 2, 2, 512])
        ps = m.psum("ps", [P, 4, 2, 512])

        w_in = [sems(f"branch_in{s}") for s in range(2)]
        g_in = [sems(f"gates_in{s}") for s in range(2)]
        in_hi_ready, in_lo_ready, bh_ready, bl_ready, branched, merged, step = (
            sems(n) for n in ("in_hi_ready", "in_lo_ready", "bh_ready", "bl_ready", "branched", "merged", "e_dve_step"))

        with nc.Block() as block:

            @block.sync
            def _(sp):
                w = [a[n].rearrange("(k p) (d c) -> d p k c", p=P, c=P) for n in ("w_branch_hy", "w_branch_na")]
                g = a["g_d"].rearrange("(b d p) t -> b d p t", b=2, p=P)
                with sp.Fori(0, KD // 2) as i:
                    for s in range(2):
                        d = 2 * i + s
                        sp.wait_ge(bl_ready, d + 1)
                        for b in range(2):
                            sp.dma_start(b_raw[:, s, b], w[b][d]).then_inc(w_in[s], 16)
                        sp.wait_ge(merged, 2 * d + 2)
                        for b in range(2):
                            sp.dma_start(gate[:, s, b], g[b, d]).then_inc(g_in[s], 16)

            @block.tensor
            def _(pe):
                pe.sem_inc(branched, 4)
                pe.wait_ge(in_lo_ready, 8)
                with pe.Fori(0, KD // 2) as i:
                    for s in range(2):
                        pe.wait_ge(bl_ready, 2 * i + s + 3)
                        for th in range(2):
                            n = 2 * s + th
                            pe.wait_ge(merged, 4 * i + n + 1)
                            for b in range(2):
                                for k in range(4):
                                    hi, lo = b_hi[:, s, b, k, :], b_lo[:, s, b, k, :]
                                    cols = slice(th * 512, (th + 1) * 512)
                                    for x, (w, h) in enumerate(((hi, in_hi), (hi, in_lo), (lo, in_hi))):
                                        mm = pe.matmul(ps[:, n, b, :], w, h[:, b, k, cols],
                                                       start=(k == 0 and x == 0), stop=(k == 3 and x == 2))
                            mm.then_inc(branched, 1)

            @block.scalar
            def _(act):
                def split(s, i, d):
                    act.wait_ge(w_in[s], 32 * i + 32)
                    act.wait_ge(branched, 2 * d + 2)
                    act.activation(b_hi[:, s], b_raw[:, s], ACT.Copy).then_inc(bh_ready, 1)

                for b, src in enumerate((y_t, na_t)):
                    for k in range(4):
                        act.activation(in_hi[:, b, k, :], src[:, k, :], ACT.Copy).then_inc(in_hi_ready, 1)
                with act.Fori(0, KD // 2) as i:
                    for s in range(2):
                        split(s, i, 2 * i + s)

            @block.vector
            def _(dve):
                dt = Tally(dve, step)
                dve.sem_inc(bl_ready, 2)
                dve.sem_inc(merged, 4)
                for b, src in enumerate((y_t, na_t)):
                    for k in range(4):
                        dve.wait_ge(in_hi_ready, 4 * b + k + 1)
                        dve.tensor_tensor(in_lo[:, b, k, :], src[:, k, :], in_hi[:, b, k, :].bitcast(F32),
                                          ALU.subtract).then_inc(in_lo_ready, 1)

                def split(d, s):
                    dve.wait_ge(bh_ready, d + 1)
                    dve.tensor_tensor(b_lo[:, s], b_raw[:, s], b_hi[:, s].bitcast(F32), ALU.subtract
                                      ).then_inc(bl_ready, 1)

                def gated(i, s):
                    for th in range(2):
                        n = 2 * s + th
                        cols = slice(th * 512, (th + 1) * 512)
                        dve.wait_ge(branched, 4 * i + n + 5)
                        dve.wait_ge(g_in[s], 32 * i + 32)
                        dve.wait_ge(merged, 4 * i + n + 3)
                        for b in range(2):
                            dt.inc(dve.tensor_tensor(part[:, th, b], ps[:, n, b, :], gate[:, s, b, cols], ALU.mult))
                        dt.wait()
                        dve.tensor_tensor(m_t[:, 2 * i + s, cols], part[:, th, 0], part[:, th, 1], ALU.add
                                          ).then_inc(merged, 1)

                split(0, 0)
                with dve.Fori(0, KD // 2 - 1) as i:
                    dt.enter(i, 8)
                    for s in range(2):
                        split(2 * i + s + 1, 1 - s)
                        gated(i, s)
                    dt.leave(KD // 2 - 1)
                split(KD - 1, 1)
                gated(KD // 2 - 1, 0)
                gated(KD // 2 - 1, 1)


def project_out(nc, sems, a, keep, m_t, logits):
    ident = keep["ident"]
    with ExitStack() as ctx:
        m = Maker(nc, ctx, "out_")
        w_raw = m.sb("w_raw", [P, 2, D])
        w_hi, w_lo = m.sb("w_hi", [P, KD, D], F32R), m.sb("w_lo", [P, KD, D], F32R)
        m_hi, m_lo = m.sb("m_hi", [P, 2, KD, P], F32R), m.sb("m_lo", [P, 2, KD, P], F32R)
        router = m.sb("router", [P, KD, E_N])
        g1_row, scale_row, shift_row, gain_row = (m.sb(n, [P, D]) for n in ("g1_row", "scale_row", "shift_row", "gain_row"))
        x_in = m.sb("x_in", [P, 2, D])
        x1 = m.sb("x1", [P, 2, D])
        h2 = m.sb("h2", [P, 2, D])
        h2_t = m.sb("h2_t", [P, KD, P])
        squares = gain_row
        stat = m.sb("stat", [P, 2, 5])
        ps_o = m.psum("ps_o", [P, 2, D])
        ps_h = m.psum("ps_h", [P, D])

        rows_in = sems("rows_in")
        wo_in = [sems(f"w_out_in{s}") for s in range(2)]
        xt_in = [sems(f"x_tile_in{s}") for s in range(2)]
        stored = [sems(f"f_stored{s}") for s in range(2)]
        wo_hi, wo_lo, m_split, projected, x1_ready, squared, var_ready, rooted, normed, turned, copied, routed = (
            sems(n) for n in ("wo_hi", "wo_lo", "m_split", "projected", "x1_ready", "squared", "f_var_ready", "rooted",
                              "f_normed", "f_turned", "f_copied", "routed"))
        step = sems("f_dve_step")

        with nc.Block() as block:

            @block.sync
            def _(sp):
                w = a["w_out"].rearrange("(k p) n -> k p n", p=P)
                mod = a["mod_d"]
                for k in range(KD):
                    sp.wait_ge(wo_lo, k + 1)
                    sp.dma_start(w_raw[:, k % 2], w[k]).then_inc(wo_in[k % 2], 16)
                    if k == 1:
                        for dst, at in ((g1_row, 2 * D), (shift_row, 3 * D), (scale_row, 4 * D)):
                            sp.dma_start(dst[:], bass.AP(mod.tensor, at, [[0, P], [1, D]])).then_inc(rows_in, 16)
                        sp.dma_start(gain_row[:], bass.AP(a["norm2_g"].tensor, 0, [[0, P], [1, D]])
                                     ).then_inc(rows_in, 16)
                        sp.dma_start(router[:], a["w_router"].rearrange("(k p) e -> p k e", p=P)).then_inc(rows_in, 16)
                x_t, acc_t, h2_t_d = (a[n].rearrange("(t p) d -> t p d", p=P) for n in ("x", "acc_d", "h2_d"))
                sp.sem_inc(stored[0], 32)
                sp.sem_inc(stored[1], 32)

                def load(t, s):
                    sp.wait_ge(x1_ready, t + 1)
                    sp.dma_start(x_in[:, s], x_t[t]).then_inc(xt_in[s], 16)

                def store(t, s):
                    sp.wait_ge(x1_ready, t + 3)
                    sp.dma_start(acc_t[t], x1[:, s]).then_inc(stored[s], 16)
                    sp.wait_ge(normed, t + 3)
                    sp.dma_start(h2_t_d[t], h2[:, s]).then_inc(stored[s], 16)

                load(0, 0)
                load(1, 1)
                with sp.Fori(0, TT // 2 - 1) as i:
                    for s in range(2):
                        store(2 * i + s, s)
                        load(2 * i + s + 2, s)
                store(TT - 2, 0)
                store(TT - 1, 1)
                for s in range(2):
                    sp.wait_ge(stored[s], 32 * (TT // 2 + 1))

            @block.tensor
            def _(pe):
                pe.sem_inc(projected, 2)
                pe.sem_inc(turned, 2)
                pe.sem_inc(routed, 1)
                pe.wait_ge(wo_lo, KD + 2)

                def out(t, s):
                    pe.wait_ge(m_split, t + 3)
                    pe.wait_ge(x1_ready, t + 1)
                    for k in range(KD):
                        for x, (h, w) in enumerate(((m_hi, w_hi), (m_hi, w_lo), (m_lo, w_hi))):
                            for n in range(2):
                                mm = pe.matmul(ps_o[:, s, n * 512:(n + 1) * 512], h[:, s, k, :],
                                               w[:, k, n * 512:(n + 1) * 512], start=(k == 0 and x == 0),
                                               stop=(k == KD - 1 and x == 2))
                    mm.then_inc(projected, 1)

                def route(t, s):
                    pe.wait_ge(normed, t + 3)
                    pe.wait_ge(copied, t + 1)
                    for k in range(KD):
                        mm = pe.transpose(ps_h[:, k * P:(k + 1) * P], h2[:, s, k * P:(k + 1) * P], ident[:])
                    mm.then_inc(turned, 1)
                    pe.wait_ge(copied, t + 2)
                    for k in range(KD):
                        mm = pe.matmul(logits[:, bass.ds(t * E_N, E_N)] if not isinstance(t, int)
                                       else logits[:, t * E_N:(t + 1) * E_N], h2_t[:, k, :], router[:, k, :],
                                       start=(k == 0), stop=(k == KD - 1))
                    mm.then_inc(routed, 1)

                out(0, 0)
                pe.wait_ge(rows_in, 5 * 16)
                with pe.Fori(0, TT // 2 - 1) as i:
                    for s in range(2):
                        out(2 * i + s + 1, 1 - s)
                        route(2 * i + s, s)
                out(TT - 1, 1)
                route(TT - 2, 0)
                route(TT - 1, 1)

            @block.scalar
            def _(act):
                act.sem_inc(copied, 1)
                for k in range(KD):
                    act.wait_ge(wo_in[k % 2], 16 * (k // 2 + 1))
                    act.activation(w_hi[:, k, :], w_raw[:, k % 2, :], ACT.Copy).then_inc(wo_hi, 1)
                act.wait_ge(x1_ready, 2)
                with act.Fori(0, TT // 2) as i:
                    for s in range(2):
                        t = 2 * i + s
                        act.wait_ge(x1_ready, t + 3)
                        act.activation(squares[:], x1[:, s], ACT.Square, accum_out=stat[:, s, 0:1]
                                       ).then_inc(squared, 1)
                        act.wait_ge(var_ready, t + 1)
                        act.activation(stat[:, s, 2:3], stat[:, s, 1:2], ACT.Sqrt).then_inc(rooted, 1)
                        act.wait_ge(turned, t + 3)
                        act.wait_ge(routed, t + 1)
                        act.activation(h2_t[:].rearrange("p k q -> p (k q)"), ps_h[:], ACT.Copy).then_inc(copied, 1)

            @block.vector
            def _(dve):
                dt = Tally(dve, step)
                dve.sem_inc(wo_lo, 2)
                for k in range(KD):
                    dve.wait_ge(wo_hi, k + 1)
                    dve.tensor_tensor(w_lo[:, k, :], w_raw[:, k % 2, :], w_hi[:, k, :].bitcast(F32), ALU.subtract
                                      ).then_inc(wo_lo, 1)
                dve.wait_ge(rows_in, 5 * 16)
                dt.then_wait(dve.scalar_tensor_tensor(out=scale_row[:], in0=scale_row[:], scalar=1.0, in1=gain_row[:],
                                                      op0=ALU.add, op1=ALU.mult))
                dve.sem_inc(m_split, 2)
                dve.sem_inc(x1_ready, 2)
                dve.sem_inc(normed, 2)

                def split(t, s):
                    src = m_t[:, :, bass.ds(t * P, P)] if not isinstance(t, int) else m_t[:, :, t * P:(t + 1) * P]
                    dve.wait_ge(projected, t + 1)
                    dt.then_wait(dve.tensor_scalar(m_hi[:, s], src, 1.0, None, ALU.mult))
                    dve.tensor_tensor(m_lo[:, s], src, m_hi[:, s].bitcast(F32), ALU.subtract).then_inc(m_split, 1)

                def residual(t, s, i):
                    dve.wait_ge(projected, t + 3)
                    dve.wait_ge(stored[s], 32 * i + 32)
                    dt.then_wait(dve.tensor_tensor(x1[:, s], ps_o[:, s], g1_row[:], ALU.mult))
                    dve.wait_ge(xt_in[s], 16 * i + 16)
                    dve.tensor_tensor(x1[:, s], x1[:, s], x_in[:, s], ALU.add).then_inc(x1_ready, 1)
                    dve.wait_ge(squared, t + 1)
                    st = [stat[:, s, x:x + 1] for x in range(5)]
                    dve.tensor_scalar(st[1], st[0], 1.0 / D, EPS, ALU.mult, ALU.add).then_inc(var_ready, 1)
                    inverse_root(dve, dt, lambda: dve.wait_ge(rooted, t + 1), st[1], st[2], st[3], st[4])
                    dve.wait_ge(turned, t + 1)
                    dt.then_wait(dve.scalar_tensor_tensor(out=h2[:, s], in0=x1[:, s], scalar=st[3], in1=scale_row[:],
                                                          op0=ALU.mult, op1=ALU.mult))
                    dve.tensor_tensor(h2[:, s], h2[:, s], shift_row[:], ALU.add).then_inc(normed, 1)

                split(0, 0)
                with dve.Fori(0, TT // 2 - 1) as i:
                    dt.enter(i, 2 * 8)
                    for s in range(2):
                        split(2 * i + s + 1, 1 - s)
                        residual(2 * i + s, s, i)
                    dt.leave(TT // 2 - 1)
                split(TT - 1, 1)
                residual(TT - 2, 0, TT // 2 - 1)
                residual(TT - 1, 1, TT // 2 - 1)


CHUNKS = [(c, min(512, FF - c)) for c in range(0, FF, 512)]
UNITS = []
for _c, (_at, _w) in enumerate(CHUNKS):
    _parts = 2 * _w // 512
    UNITS += [(name, _c, q, _parts) for name in ("gate", "up") for q in range(_parts)]
    if _c:
        UNITS += [("down", _c - 1, q, 2) for q in range(2)]
UNITS += [("down", len(CHUNKS) - 1, q, _parts) for q in range(_parts)]
N_U = len(UNITS)
RAW = 11
PARTS = 3
assert N_U % RAW == 0 and N_U % PARTS == 0
LAST_OF = {(name, c): u for u, (name, c, q, parts) in enumerate(UNITS) if q == parts - 1}


def unit_source(a, e, u):
    name, c, q, parts = UNITS[u]
    at, w = CHUNKS[c]
    if name == "down":
        f = at // P + 2 * q
        return a["w_down"].rearrange("e (f p) n -> e p f n", p=P)[e][:, f:f + 2, :]
    rows = KD // parts
    return a["w_" + name].rearrange("e (k p) n -> e p k n", p=P)[e][:, rows * q:rows * (q + 1), at:at + w]


def unit_view(slot, u):
    name, c, _, parts = UNITS[u]
    return slot.rearrange("p (r n) -> p r n", r=2 if name == "down" else KD // parts)


def choose(nc, sems, a, keep, logits, raw, raw_in, gate_col, idx_col):
    ident = keep["ident"]
    with ExitStack() as ctx:
        m = Maker(nc, ctx, "choose_")
        lg = logits[:, 0:TT * E_N].rearrange("p (t e) -> p t e", e=E_N)
        top, total, inv = (m.sb(n, [P, TT]) for n in ("top", "total", "inv"))
        aff = m.sb("aff", [P, TT, E_N])
        rows = m.sb("rows", [E_N, T])
        best = m.sb("best", [E_N, CAP])
        where = m.sb("where", [E_N, CAP], U32)
        where_f = m.sb("where_f", [E_N, CAP])
        ps_r = m.psum("ps_r", [P, T])
        ps_c = m.psum("ps_c", [P, 2, 512])
        step, shifted, exped, aff_ready, aff_turned, best_ready, best_turned = (
            sems(n) for n in ("g_dve_step", "shifted", "exped", "aff_ready", "aff_turned", "best_ready", "best_turned"))

        with nc.Block() as block:

            @block.sync
            def _(sp):
                for u in range(RAW):
                    sp.dma_start(unit_view(raw[:, u], u), unit_source(a, 0, u)).then_inc(raw_in[u], 16)

            @block.scalar
            def _(act):
                act.wait_ge(shifted, 1)
                act.activation(aff[:], aff[:], ACT.Exp).then_inc(exped, 1)

            @block.tensor
            def _(pe):
                pe.wait_ge(aff_ready, 1)
                for t in range(TT):
                    mm = pe.transpose(ps_r[0:E_N, t * P:(t + 1) * P], aff[:, t, :], ident[:])
                mm.then_inc(aff_turned, 1)
                pe.wait_ge(best_ready, 1)
                pe.transpose(ps_c[:, 0, 0:E_N], best[:], ident[0:E_N, 0:E_N])
                pe.transpose(ps_c[:, 1, 0:E_N], where_f[:], ident[0:E_N, 0:E_N]).then_inc(best_turned, 1)

            @block.vector
            def _(dve):
                dt = Tally(dve, step)

                def wide(v):
                    return v[:].unsqueeze(2).broadcast_to([P, TT, E_N])

                dt.then_wait(dve.reduce_max(top[:], lg, AX_X))
                dve.tensor_tensor(aff[:], lg, wide(top), ALU.subtract).then_inc(shifted, 1)
                dve.wait_ge(exped, 1)
                dt.then_wait(dve.reduce_sum(total[:], aff[:], AX_X))
                dt.then_wait(dve.reciprocal(inv[:], total[:]))
                dve.tensor_tensor(aff[:], aff[:], wide(inv), ALU.mult).then_inc(aff_ready, 1)
                dve.wait_ge(aff_turned, 1)
                dt.then_wait(dve.tensor_copy(rows[:], ps_r[0:E_N, :]))
                for r in range(CAP // 8):
                    eight = slice(8 * r, 8 * r + 8)
                    dt.then_wait(dve.max(best[:, eight], rows[:]))
                    dt.inc(dve.max_index(where[:, eight], best[:, eight], rows[:]))
                    if r + 1 < CAP // 8:
                        dt.inc(dve.match_replace(rows[:], best[:, eight], rows[:], -1.0))
                    dt.wait()
                dve.tensor_copy(where_f[:], where[:]).then_inc(best_ready, 1)
                dve.wait_ge(best_turned, 1)
                dve.tensor_copy(gate_col[:], ps_c[:, 0, 0:E_N])
                dve.tensor_copy(idx_col[:], ps_c[:, 1, 0:E_N])


def experts(nc, sems, a, keep, raw, raw_in, gate_col, idx_col):
    ident = keep["ident"]
    with ExitStack() as ctx:
        m = Maker(nc, ctx, "moe_")
        w_hi, w_lo = m.sb("w_hi", [P, PARTS, 2048], F32R), m.sb("w_lo", [P, PARTS, 2048], F32R)
        xe = m.sb("xe", [P, D])
        xt_hi, xt_lo = m.sb("xt_hi", [P, KD, P], F32R), m.sb("xt_lo", [P, KD, P], F32R)
        sl = m.sb("sl", [P, 2, 512])
        h = m.sb("h", [P, 2, 512])
        ht_hi, ht_lo = m.sb("ht_hi", [P, 2, 4, P], F32R), m.sb("ht_lo", [P, 2, 4, P], F32R)
        y = m.sb("y", [P, D])
        g2_row = m.sb("g2_row", [P, D])
        ps_gate = m.psum("ps_gate", [P, 2, 512])
        ps_up = m.psum("ps_up", [P, 2, 512])
        ps_y = m.psum("ps_y", [P, D])
        ps_h = m.psum("ps_h", [P, 512])
        ps_x = m.psum("ps_x", [P, 512])

        hi_ready, lo_ready, used, silu_done, multiplied, turned_h, h_high, h_parts = (
            sems(n) for n in ("m_hi_ready", "m_lo_ready", "used_units", "silu_done", "multiplied", "turned_h", "h_high",
                              "h_parts"))
        turned_x, x_high, x_parts, gathered, y_ready, y_free, scattered, g2_in = (
            sems(n) for n in ("turned_x", "x_high", "x_parts", "gathered", "moe_y_ready", "y_free", "scattered", "g2_in"))
        N_C = len(CHUNKS)

        def after(u):
            out = []
            for c in range(N_C):
                if min(LAST_OF["gate", c] + 2, N_U - 1) == u:
                    out.append(("silu", c))
                if min(LAST_OF["up", c] + 2, N_U - 1) == u:
                    out.append(("multiply", c))
            for c in range(N_C - 1):
                if LAST_OF["gate", c + 1] + 2 == u:
                    out.append(("turned", c))
            if LAST_OF["up", N_C - 1] + 2 == u:
                out.append(("turned_x", 0))
            if u == N_U - 1:
                out += [("turned", N_C - 1), ("turned_x", 1)]
            return out

        with nc.Block() as block:

            @block.sync
            def _(sp):
                sp.dma_start(g2_row[:], bass.AP(a["mod_d"].tensor, 5 * D, [[0, P], [1, D]])).then_inc(g2_in, 16)

                def load(e, e_of, u):
                    sp.wait_ge(lo_ready, N_U * e_of + u + 1)
                    sp.dma_start(unit_view(raw[:, u % RAW], u), unit_source(a, e_of, u)).then_inc(raw_in[u % RAW], 16)

                with sp.Fori(0, E_N - 1) as e:
                    for u in range(RAW, N_U):
                        load(e, e, u)
                    for u in range(RAW):
                        load(e, e + 1, u)
                for u in range(RAW, N_U):
                    load(E_N - 1, E_N - 1, u)

            @block.gpsimd
            def _(pool):
                h2, acc = a["h2_d"], a["acc_d"]

                def gather(e):
                    if e:
                        pool.wait_ge(turned_x, 2 * e)
                    pool.indirect_dma_start(xe[:], None, h2, bass.IndirectOffsetOnAxis(ap=idx_col[:, min(e, E_N - 1):min(e, E_N - 1) + 1], axis=0)
                                            ).then_inc(gathered, 16)

                pool.sem_inc(y_free, 1)
                gather(0)
                for e in range(E_N):
                    gather(e + 1)
                    pool.wait_ge(y_ready, e + 2)
                    pool.indirect_dma_start(acc, bass.IndirectOffsetOnAxis(ap=idx_col[:, e:e + 1], axis=0), y[:], None,
                                            compute_op=ALU.add).then_inc(scattered, 16)
                    pool.wait_ge(scattered, 16 * e + 16)
                    pool.sem_inc(y_free, 1)

            @block.tensor
            def _(pe):
                pe.sem_inc(used, 3)
                pe.sem_inc(turned_h, 1)

                def turn_x(half, count):
                    pe.wait_ge(x_parts, count + 1)
                    for k in range(4):
                        at = (4 * half + k) * P
                        mm = pe.transpose(ps_x[:, k * P:(k + 1) * P], xe[:, at:at + P], ident[:])
                    mm.then_inc(turned_x, 1)

                def turn_h(e, c):
                    pe.wait_ge(multiplied, N_C * e + c + 3)
                    pe.wait_ge(h_parts, N_C * e + c + 1)
                    for b in range(CHUNKS[c][1] // P):
                        mm = pe.transpose(ps_h[:, b * P:(b + 1) * P], h[:, c % 2, b * P:(b + 1) * P], ident[:])
                    mm.then_inc(turned_h, 1)

                def unit(e, u):
                    name, c, q, parts = UNITS[u]
                    w = CHUNKS[c][1]
                    hi, lo = (unit_view(x[:, u % PARTS], u) for x in (w_hi, w_lo))
                    pe.wait_ge(lo_ready, N_U * e + u + 1 + RAW)
                    if name == "down":
                        if q == 0:
                            pe.wait_ge(h_parts, N_C * e + c + 2)
                        if q == 0 and c == 0:
                            pe.wait_ge(y_ready, e + 1)
                        for r in range(2):
                            f = 2 * q + r
                            ht = [x[:, c % 2, f, :] for x in (ht_hi, ht_lo)]
                            first, last = c == 0 and f == 0, c == N_C - 1 and f == w // P - 1
                            for x, (hp, wp) in enumerate(((ht[0], hi), (ht[0], lo), (ht[1], hi))):
                                for n in range(2):
                                    mm = pe.matmul(ps_y[:, n * 512:(n + 1) * 512], hp, wp[:, r, n * 512:(n + 1) * 512],
                                                   start=(first and x == 0), stop=(last and x == 2))
                    else:
                        ps = (ps_gate if name == "gate" else ps_up)[:, c % 2, 0:w]
                        if q == 0:
                            pe.wait_ge(multiplied, N_C * e + c + 1)
                        rows = KD // parts
                        for r in range(rows):
                            k = rows * q + r
                            for x, (hp, wp) in enumerate(((xt_hi, hi), (xt_hi, lo), (xt_lo, hi))):
                                mm = pe.matmul(ps, hp[:, k, :], wp[:, r, :], start=(k == 0 and x == 0),
                                               stop=(k == KD - 1 and x == 2))
                    mm.then_inc(used, 1)

                pe.wait_ge(gathered, 16)
                turn_x(0, 0)
                turn_x(1, 1)
                with pe.Fori(0, E_N) as e:
                    pe.wait_ge(x_parts, 2 * e + 3)
                    for u in range(N_U):
                        unit(e, u)
                        for c in range(N_C - 1):
                            if LAST_OF["gate", c + 1] == u:
                                turn_h(e, c)
                        if LAST_OF["up", N_C - 1] == u:
                            pe.wait_ge(gathered, 16 * e + 32)
                            turn_x(0, 2 * e + 2)
                        if LAST_OF["down", N_C - 2] == u:
                            turn_h(e, N_C - 1)
                            turn_x(1, 2 * e + 3)

            @block.scalar
            def _(act):
                act.sem_inc(silu_done, 2)

                def high_x(count):
                    half = count[1]
                    act.wait_ge(turned_x, count[0] + 1)
                    act.activation(xt_hi[:, 4 * half:4 * half + 4, :], ps_x[:].rearrange("p (k q) -> p k q", q=P),
                                   ACT.Copy).then_inc(x_high, 1)

                high_x((0, 0))
                high_x((1, 1))
                with act.Fori(0, E_N) as e:
                    for u in range(N_U):
                        act.wait_ge(raw_in[u % RAW], 48 * e + 16 * (u // RAW) + 16)
                        act.wait_ge(used, N_U * e + u + 1)
                        act.activation(w_hi[:, u % PARTS], raw[:, u % RAW], ACT.Copy).then_inc(hi_ready, 1)
                        for what, c in after(u):
                            if what == "silu":
                                w = CHUNKS[c][1]
                                act.wait_ge(used, N_U * e + LAST_OF["gate", c] + 1 + 3)
                                act.activation(sl[:, c % 2, 0:w], ps_gate[:, c % 2, 0:w], ACT.Silu
                                               ).then_inc(silu_done, 1)
                            elif what == "turned":
                                n = CHUNKS[c][1] // P
                                act.wait_ge(turned_h, N_C * e + c + 2)
                                act.activation(ht_hi[:, c % 2, 0:n], ps_h[:, 0:n * P].rearrange(
                                    "p (k q) -> p k q", q=P), ACT.Copy).then_inc(h_high, 1)
                            elif what == "turned_x":
                                high_x((2 * e + 2 + c, c))

            @block.vector
            def _(dve):
                dve.sem_inc(lo_ready, RAW)
                dve.sem_inc(h_parts, 1)
                dve.sem_inc(x_parts, 1)
                dve.sem_inc(multiplied, 2)
                dve.sem_inc(y_ready, 1)

                def low_x(count, half):
                    dve.wait_ge(x_high, count + 1)
                    view = xt_lo[:, 4 * half:4 * half + 4, :]
                    dve.tensor_tensor(view, ps_x[:].rearrange("p (k q) -> p k q", q=P),
                                      xt_hi[:, 4 * half:4 * half + 4, :].bitcast(F32), ALU.subtract
                                      ).then_inc(x_parts, 1)

                low_x(0, 0)
                low_x(1, 1)
                dve.wait_ge(g2_in, 16)
                with dve.Fori(0, E_N) as e:
                    for u in range(N_U):
                        dve.wait_ge(hi_ready, N_U * e + u + 1)
                        dve.tensor_tensor(w_lo[:, u % PARTS], raw[:, u % RAW], w_hi[:, u % PARTS].bitcast(F32),
                                          ALU.subtract).then_inc(lo_ready, 1)
                        for what, c in after(u):
                            if what == "multiply":
                                w = CHUNKS[c][1]
                                dve.wait_ge(silu_done, N_C * e + c + 3)
                                dve.wait_ge(used, N_U * e + LAST_OF["up", c] + 1 + 3)
                                dve.tensor_tensor(h[:, c % 2, 0:w], sl[:, c % 2, 0:w], ps_up[:, c % 2, 0:w], ALU.mult
                                                  ).then_inc(multiplied, 1)
                            elif what == "turned":
                                n = CHUNKS[c][1] // P
                                dve.wait_ge(h_high, N_C * e + c + 1)
                                dve.tensor_tensor(ht_lo[:, c % 2, 0:n], ps_h[:, 0:n * P].rearrange(
                                    "p (k q) -> p k q", q=P), ht_hi[:, c % 2, 0:n].bitcast(F32), ALU.subtract
                                    ).then_inc(h_parts, 1)
                            elif what == "turned_x":
                                low_x(2 * e + 2 + c, c)
                    dve.wait_ge(used, N_U * e + N_U + 3)
                    dve.wait_ge(y_free, e + 1)
                    dve.scalar_tensor_tensor(out=y[:], in0=ps_y[:], scalar=gate_col[:, bass.ds(e, 1)], in1=g2_row[:],
                                             op0=ALU.mult, op1=ALU.mult).then_inc(y_ready, 1)


def last_norm(nc, sems, a, out):
    with ExitStack() as ctx:
        m = Maker(nc, ctx, "last_")
        x = m.sb("x", [P, TT, D])
        o = m.sb("o", [P, TT, D])
        gain = m.sb("gain", [P, D])
        squares = m.sb("squares", [P, D])
        stat = m.sb("stat", [P, TT, 5])
        x_in = [sems(f"acc_in{t}") for t in range(TT)]
        gain_in, squared, var_ready, rooted, step, out_ready, stored = (
            sems(n) for n in ("gain_in", "h_squared", "h_var_ready", "h_rooted", "h_dve_step", "out_ready", "out_stored"))

        with nc.Block() as block:

            @block.sync
            def _(sp):
                src, dst = a["acc_d"].rearrange("(t p) d -> t p d", p=P), out[0].rearrange("(t p) d -> t p d", p=P)
                for t in range(TT):
                    sp.dma_start(x[:, t], src[t]).then_inc(x_in[t], 16)
                sp.dma_start(gain[:], bass.AP(a["final_g"].tensor, 0, [[0, P], [1, D]])).then_inc(gain_in, 16)
                for t in range(TT):
                    sp.wait_ge(out_ready, t + 1)
                    sp.dma_start(dst[t], o[:, t]).then_inc(stored, 16)
                sp.wait_ge(stored, 16 * TT)

            @block.scalar
            def _(act):
                for t in range(TT):
                    act.wait_ge(x_in[t], 16)
                    if t:
                        act.wait_ge(squared, t)
                    act.activation(squares[:], x[:, t], ACT.Square, accum_out=stat[:, t, 0:1]).then_inc(squared, 1)
                    act.wait_ge(var_ready, t + 1)
                    act.activation(stat[:, t, 2:3], stat[:, t, 1:2], ACT.Sqrt).then_inc(rooted, 1)

            @block.vector
            def _(dve):
                dt = Tally(dve, step)
                dve.wait_ge(gain_in, 16)
                for t in range(TT):
                    st = [stat[:, t, i:i + 1] for i in range(5)]
                    dve.wait_ge(squared, t + 1)
                    dve.tensor_scalar(st[1], st[0], 1.0 / D, EPS, ALU.mult, ALU.add).then_inc(var_ready, 1)
                    inverse_root(dve, dt, lambda: dve.wait_ge(rooted, t + 1), st[1], st[2], st[3], st[4])
                    dve.scalar_tensor_tensor(out=o[:, t], in0=x[:, t], scalar=st[3], in1=gain[:], op0=ALU.mult,
                                             op1=ALU.mult).then_inc(out_ready, 1)


def program(nc, a, out):
    with ExitStack() as ctx:
        m = Maker(nc, ctx)
        sems = m.sem
        for name, shape in (("mod_d", (2, 6 * D)), ("u_d", (3 * HY, T)), ("qk_d", (2 * HY, W)), ("g_d", (2 * D, T)),
                            ("acc_d", (T, D)), ("h2_d", (T, D))):
            a[name] = nc.dram_tensor(name, shape, F32, kind="Internal").ap()
        keep = {"ident": m.sb("identity", [P, P]), "par": m.sb("par", [P, N_PAR])}
        with ExitStack() as mixer:
            with ExitStack() as values:
                with ExitStack() as projection:
                    n = Maker(nc, projection)
                    keep["h_hi"] = n.sb("h_hi", [P, KD, W], F32R)
                    keep["h_lo"] = n.sb("h_lo", [P, KD, W], F32R)
                    modulate_and_norm(nc, sems, a, keep)
                    v_tok = Maker(nc, values).sb("v_tok", [P, NT, 512], side="right")
                    project(nc, sems, a, keep, v_tok)
                n = Maker(nc, mixer)
                na_t = n.sb("na_t", [P, 4, T])
                attend(nc, sems, a, keep, v_tok, na_t)
            y_t = n.sb("y_t", [P, 4, T])
            hyena(nc, sems, a, keep, y_t)
            merged = ExitStack()
            m_t = Maker(nc, merged).sb("m_t", [P, KD, T], side="right")
            merge(nc, sems, a, y_t, na_t, m_t)
        with ExitStack() as routing:
            logits = Maker(nc, routing).psum("logits", [P, 512])
            with merged:
                project_out(nc, sems, a, keep, m_t, logits)
            n = Maker(nc, ctx)
            gate_col = n.sb("gate_col", [P, E_N])
            idx_col = n.sb("idx_col", [P, E_N], U32)
            raw = n.sb("raw", [P, RAW, 2048])
            raw_in = [sems(f"raw_in{s}") for s in range(RAW)]
            choose(nc, sems, a, keep, logits, raw, raw_in, gate_col, idx_col)
        experts(nc, sems, a, keep, raw, raw_in, gate_col, idx_col)
        last_norm(nc, sems, a, out)


def laid_out(inputs):
    x = {k: np.asarray(v) for k, v in inputs.items()}
    arrays = {
        "x": x["x"][0], "ctx": x["ctx"][0], "c": x["c"][0], "c_ctx": x["c_ctx"],
        "w_mod": x["w_mod"][0], "b_mod": x["b_mod"][0], "norm1_g": x["norm1_g"].reshape(-1, P),
        "w_in": x["w_in"][0], "b_in": x["b_in"].reshape(-1, P),
        "hy_short_w": x["hy_short_w"].reshape(-1, P), "hy_short_b": x["hy_short_b"].reshape(-1, P),
        "hy_skip": x["hy_skip"].reshape(-1, P),
    }
    rpb = np.pad(x["na_rpb"][0], ((0, 0), (0, 0), (48, P - 48 - (2 * WIN_W - 1))))
    arrays["rpb"] = rpb[:, :, ::-1]
    col = np.arange(GRID_W)
    start = np.clip(col - WIN_W // 2, 0, GRID_W - WIN_W)[:, None]
    seen = (col[None, :] >= start) & (col[None, :] < start + WIN_W)
    arrays["na_mask"] = np.tile(np.where(seen, 0.0, NEG).astype(np.float32), (2, 1))
    arrays["filt_w1"], arrays["filt_w2"], arrays["filt_w3"] = (x["filt_w" + n][0] for n in "123")
    arrays["filt_cols"] = np.stack([x[n][0] for n in ("filt_freq", "filt_b1", "filt_b2")], axis=1)
    pos = np.arange(T, dtype=np.float32)
    t = pos / np.float32(T - 1)
    bands = np.linspace(1e-4, (FEMB - 1) // 2 - 1, (FEMB - 1) // 2, dtype=np.float32)
    ang = (np.float32(2.0 * math.pi) * pos / np.float32(T))[:, None] * bands[None, :]
    arrays["feats"] = np.concatenate([t[:, None], np.cos(ang), -np.sin(ang)], axis=1).astype(np.float32).T
    deltas = np.linspace(math.log(1e-2) / 1.5, math.log(1e-2) / 0.3, HY, dtype=np.float32)
    arrays["decay"] = np.exp(-t[:, None] * np.abs(deltas)[None, :]).astype(np.float32)
    f = 2 * np.arange(P)[None, :] + np.arange(2)[:, None]
    turn = np.arange(BLK)[:, None, None] * (f[None] + 0.5) * (2.0 * math.pi / (2 * BLK))
    planes = np.stack([np.cos(turn), -np.sin(turn)], axis=2)
    arrays["dft"] = planes.reshape(2, P, 4, P).transpose(1, 0, 2, 3).astype(np.float32)
    arrays["idft"] = (planes.reshape(BLK, 4, P).transpose(2, 1, 0) / BLK).astype(np.float32)
    arrays.update({k: x[k][0] for k in ("w_branch_hy", "w_branch_na", "w_out", "w_router", "w_gate", "w_up", "w_down")})
    arrays["norm2_g"], arrays["final_g"] = x["norm2_g"], x["final_g"].reshape(1, -1)
    arrays["ident"] = np.eye(P, dtype=np.float32)
    return {k: np.ascontiguousarray(v) for k, v in arrays.items()}


def kernel(**inputs):
    import concourse.bacc as bacc
    from concourse.bass_utils import run_bass_kernel_spmd as run

    nc = bacc.Bacc("TRN2", target_bir_lowering=False, num_devices=1)
    arrays = {"in_" + k: v for k, v in laid_out(inputs).items()}
    a = {k[3:]: nc.dram_tensor(k, v.shape, mybir.dt.from_np(v.dtype), kind="ExternalInput").ap()
         for k, v in arrays.items()}
    out = nc.dram_tensor("out", (1, T, D), F32, kind="ExternalOutput").ap()
    program(nc, a, out)
    return run(nc, [arrays], core_ids=[0]).results[0]["out"]
```

```python
import math
from contextlib import ExitStack

import numpy as np

import concourse.bass as bass
from concourse import mybir

F32 = mybir.dt.float32
F32R = mybir.dt.float32r
U32 = mybir.dt.uint32
ALU = mybir.AluOpType
ACT = mybir.ActivationFunctionType
AX_X = mybir.AxisListType.X

P = 128
T = 1024
D = 1024
CTX = 256
W = T + CTX
KD = D // P
TT = T // P
NT = W // P
EPS = 1e-6
HY = 512
HEADS, HD = 8, 64
GRID_W = 64
ROWS = T // GRID_W
WIN_H, WIN_W = 8, 16
E_N, CAP, FF = 16, 128, 2816
FC = 64
FEMB = 17
P_IN = 5 * D
NEG = -1.0e30

C_NORM1, C_BIN, C_SW, C_SB, C_SKIP, N_PAR = 0, 8, 48, 84, 96, 104

TWO_PI_HI = 6.28125
TWO_PI_LO = 2.0 * math.pi - TWO_PI_HI
ROUND = 1.5 * 2.0 ** 23
MOD_CHUNKS = 6 * D // 512
MOD_EARLY = 2 * D // 512

UNIT = 256
CH_UNIT = UNIT // P


class Tally:

    def __init__(self, eng, sem):
        self.eng, self.sem, self.done, self.turn = eng, sem, 0, 0

    def inc(self, ins):
        ins.then_inc(self.sem, 1)
        self.done += 1

    def wait(self, but=0):
        self.eng.wait_ge(self.sem, self.turn + self.done - but)

    def then_wait(self, ins):
        self.inc(ins)
        self.wait()

    def enter(self, i, per):
        self.start, self.per = self.done, per
        self.turn = i * per

    def leave(self, turns):
        assert self.done - self.start == self.per, (self.done - self.start, self.per)
        self.done, self.turn = self.start + turns * self.per, 0


class Maker:

    def __init__(self, nc, ctx, phase=""):
        self.nc, self.ctx, self.phase = nc, ctx, phase

    def sb(self, name, shape, dt=F32, side="left"):
        return self.ctx.enter_context(self.nc.sbuf_tensor(self.phase + name, shape, dt, side=side))

    def psum(self, name, shape):
        return self.ctx.enter_context(self.nc.psum_tensor(self.phase + name, shape, F32))

    def sem(self, name):
        return self.ctx.enter_context(self.nc.semaphore(name))


def inverse_root(dve, dt, act_sqrt, var, root, inv, tmp):
    act_sqrt()
    dt.then_wait(dve.reciprocal(inv, root))
    dt.then_wait(dve.tensor_tensor(tmp, var, inv, ALU.mult))
    dt.then_wait(dve.tensor_tensor(tmp, tmp, inv, ALU.mult))
    dt.then_wait(dve.tensor_scalar(tmp, tmp, -0.5, 1.5, ALU.mult, ALU.add))
    dt.then_wait(dve.tensor_tensor(inv, inv, tmp, ALU.mult))


def modulate_and_norm(nc, sems, a, keep):
    h_hi, h_lo, par, ident, c_silu = keep["h_hi"], keep["h_lo"], keep["par"], keep["ident"], keep["c_silu"]
    NC = MOD_EARLY
    with ExitStack() as ctx:
        m = Maker(nc, ctx, "norm_")
        x_raw = m.sb("x_raw", [P, NT, D])
        w_mod = m.sb("w_mod", [P, 2, KD, 512])
        mod_row = m.sb("mod_row", [2, NC, 512])
        par_rows = m.sb("par_rows", [N_PAR, P])
        c_col = m.sb("c_col", [P, 2, KD])
        feats = m.sb("feats", [FEMB, T])
        w1 = m.sb("w1", [FEMB, FC])
        w2 = m.sb("w2", [FC, FC])
        mlp_col = m.sb("mlp_col", [FC, 5])
        arg, turns, hidden = (m.sb(n, [FC, T]) for n in ("arg", "turns", "hidden"))
        ss = m.sb("ss", [P, NT])
        var = m.sb("var", [P, NT])
        root = m.sb("root", [P, NT])
        inv = m.sb("inv", [P, NT])
        tmp = m.sb("tmp", [P, NT])
        scale_col = m.sb("scale_col", [P, 2, KD])
        shift_col = m.sb("shift_col", [P, 2, KD])
        h_full = m.sb("h_full", [P, 2, 512])
        ps_mod = m.psum("ps_mod", [P, 2, 512])
        ps_col = m.psum("ps_col", [P, 512])
        ps_x = m.psum("ps_x", [P, 4, 512])

        rows_in, c_in, mlp_in = (sems(n) for n in ("par_rows_in", "c_in", "mlp_in"))
        x_in = [sems(f"x_in{n}") for n in range(3)]
        mlp_ps, mlp_arg, mlp_sin = (sems(n) for n in ("mlp_ps", "mlp_arg", "mlp_sin"))
        w_in = [sems(f"w_mod_in{s}") for s in range(2)]
        silu_ready, mod_done, mod_row_ready = (
            sems(n) for n in ("silu_ready", "mod_done", "mod_row_ready"))
        par_done, col_done, dve_step, sq_done, root_done = (
            sems(n) for n in ("par_done", "col_done", "a_dve_step", "sq_done", "root_done"))
        xn_ready, xt_done, full_ready, lo_done, hidden_out = (
            sems(n) for n in ("xn_ready", "xt_done", "full_ready", "h_lo_done", "hidden_out"))
        cols_ready, var_ready = sems("cols_ready"), sems("var_ready")

        groups = [(0, 4, 0), (4, 4, 0), (8, 2, 1)]
        fills = [(k, g) for k in range(KD) for g in range(3)]

        with nc.Block() as block:

            @block.sync
            def _(sp):
                for n, (name, lo, hi) in enumerate((("norm1_g", C_NORM1, C_BIN), ("b_in", C_BIN, C_SW),
                                                    ("hy_short_w", C_SW, C_SB), ("hy_short_b", C_SB, C_SKIP),
                                                    ("hy_skip", C_SKIP, N_PAR))):
                    sp.dma_start(par_rows[lo:hi, :], a[name]).then_inc(rows_in, 16)
                sp.dma_start(ident[:], a["ident"]).then_inc(rows_in, 16)
                for j, name in enumerate(("c", "c_ctx")):
                    sp.dma_start(c_col[:, j, :], a[name].rearrange("(p k) -> p k", k=KD)).then_inc(c_in, 16)
                    sp.dma_start(mod_row[j:j + 1, :, :], a["b_mod"].rearrange("(o n c) -> o n c", o=1, c=512)[:, 0:NC]
                                 ).then_inc(c_in, 16)
                for dst, name in ((feats[:], "feats"), (w1[:], "filt_w1"), (w2[:], "filt_w2"),
                                  (mlp_col[:, 0:3], "filt_cols")):
                    sp.dma_start(dst, a[name]).then_inc(mlp_in, 16)
                w_src = a["w_mod"].rearrange("(p k) (n c) -> n p k c", k=KD, c=512)
                x_src, ctx_src = (a[n].rearrange("(t p) d -> p t d", p=P) for n in ("x", "ctx"))
                for n in range(NC):
                    if n >= 2:
                        sp.wait_ge(mod_done, n - 1)
                    sp.dma_start(w_mod[:, n % 2], w_src[n]).then_inc(w_in[n % 2], 16)
                    if n == 1:
                        for t in range(0, TT, 4):
                            sp.dma_start(x_raw[:, t:t + 4, :], x_src[:, t:t + 4, :]).then_inc(x_in[t // 4], 16)
                        sp.dma_start(x_raw[:, TT:NT, :], ctx_src).then_inc(x_in[2], 16)
                for u in range(2):
                    sp.dma_start(keep["w_in"][:, u], a["w_in"].rearrange("(k p) (u n) -> u p k n", p=P, n=UNIT)[u]
                                 ).then_inc(keep["w_in_sems"][u], 16)
                sp.wait_ge(mlp_sin, 2)
                sp.dma_start(a["hidden_d"], hidden[:]).then_inc(hidden_out, 16)
                sp.wait_ge(hidden_out, 16)

            @block.tensor
            def _(pe):
                pe.wait_ge(rows_in, 6 * 16)
                pe.transpose(ps_col[:, 0:N_PAR], par_rows[:], ident[0:N_PAR, 0:N_PAR]).then_inc(par_done, 1)

                def mlp(w, src):
                    for th in range(2):
                        pe.matmul(ps_x[0:FC, th, :], w, src[:, th * 512:(th + 1) * 512], start=True, stop=True
                                  ).then_inc(mlp_ps, 1)

                pe.wait_ge(mlp_in, 4 * 16)
                mlp(w1[:], feats)
                pe.wait_ge(silu_ready, 1)
                for n in range(NC):
                    pe.wait_ge(w_in[n % 2], 16 * (n // 2) + 16)
                    if n >= 2:
                        pe.wait_ge(mod_row_ready, n - 1)
                    for k in range(KD):
                        mm = pe.matmul(ps_mod[0:2, n % 2, :], c_silu[:, k, :], w_mod[:, n % 2, k, :],
                                       start=(k == 0), stop=(k == KD - 1))
                    mm.then_inc(mod_done, 1)
                    if n == 1:
                        pe.wait_ge(mlp_sin, 1)
                        mlp(w2[:], hidden)
                pe.wait_ge(mod_row_ready, NC)
                pe.wait_ge(cols_ready, 1)
                flat = mod_row[:].rearrange("j n c -> j (n c)")
                for k in range(2 * KD):
                    mm = pe.transpose(ps_col[:, 2 * k:2 * k + 2], flat[:, k * P:(k + 1) * P], ident[0:2, 0:2])
                mm.then_inc(col_done, 1)
                pe.wait_ge(mlp_arg, 2)
                pe.wait_ge(xn_ready, NT)
                for n, (k, g) in enumerate(fills):
                    t0, nt, _ = groups[g]
                    if n >= 4:
                        pe.wait_ge(full_ready, n - 3)
                    for t in range(nt):
                        mm = pe.transpose(ps_x[:, n % 4, t * P:(t + 1) * P],
                                          x_raw[:, t0 + t, k * P:(k + 1) * P], ident[:])
                    mm.then_inc(xt_done, 1)

            @block.scalar
            def _(act):
                act.wait_ge(c_in, 64)
                act.activation(c_silu[:].rearrange("p k j -> p j k"), c_col[:], ACT.Silu).then_inc(silu_ready, 1)
                act.wait_ge(mlp_arg, 1)
                act.activation(hidden[:], arg[:], ACT.Sin).then_inc(mlp_sin, 1)
                for t in range(NT):
                    if t % 4 == 0:
                        act.wait_ge(x_in[t // 4], 16)
                    if t:
                        act.wait_ge(sq_done, t)
                    act.activation(h_full[:].rearrange("p a b -> p (a b)"), x_raw[:, t, :], ACT.Square, accum_out=ss[:, t:t + 1]).then_inc(sq_done, 1)
                act.wait_ge(var_ready, 1)
                act.activation(root[:], var[:], ACT.Sqrt).then_inc(root_done, 1)
                act.wait_ge(mlp_arg, 2)
                act.activation(hidden[:], arg[:], ACT.Sin).then_inc(mlp_sin, 1)
                act.wait_ge(cols_ready, 2)
                for n, (k, g) in enumerate(fills):
                    t0, nt, j = groups[g]
                    cols = slice(t0 * P, (t0 + nt) * P)
                    sc, sh = scale_col[:, j, k:k + 1], shift_col[:, j, k:k + 1]
                    act.wait_ge(xt_done, n + 1)
                    act.activation(h_hi[:, k, cols], ps_x[:, n % 4, 0:nt * P], ACT.Identity, bias=sh, scale=sc)
                    if n >= 2:
                        act.wait_ge(lo_done, n - 1)
                    act.activation(h_full[:, n % 2, 0:nt * P], ps_x[:, n % 4, 0:nt * P], ACT.Identity,
                                   bias=sh, scale=sc).then_inc(full_ready, 1)

            @block.vector
            def _(dve):
                dt = Tally(dve, dve_step)
                dve.wait_ge(par_done, 1)
                dve.tensor_copy(par[:], ps_col[:, 0:N_PAR]).then_inc(cols_ready, 1)
                dve.wait_ge(mlp_in, 4 * 16)
                for layer in range(2):
                    dt.then_wait(dve.tensor_tensor(mlp_col[:, 3 + layer:4 + layer], mlp_col[:, 0:1],
                                                   mlp_col[:, 1 + layer:2 + layer], ALU.mult))

                def sine_argument(layer):
                    for th in range(2):
                        dve.wait_ge(mlp_ps, 2 * layer + th + 1)
                        if layer:
                            dve.wait_ge(mlp_sin, 1)
                        dt.inc(dve.tensor_scalar(arg[:, th * 512:(th + 1) * 512], ps_x[0:FC, th, :], mlp_col[:, 0:1],
                                                 mlp_col[:, 3 + layer:4 + layer], ALU.mult, ALU.add))
                    dt.wait()
                    dt.then_wait(dve.tensor_scalar(turns[:], arg[:], 1.0 / (2.0 * math.pi), ROUND, ALU.mult, ALU.add))
                    dt.then_wait(dve.tensor_scalar(turns[:], turns[:], -ROUND, None, ALU.add))
                    dt.then_wait(dve.scalar_tensor_tensor(out=arg[:], in0=turns[:], scalar=-TWO_PI_HI, in1=arg[:],
                                                          op0=ALU.mult, op1=ALU.add))
                    dt.then_wait(dve.scalar_tensor_tensor(out=arg[:], in0=turns[:], scalar=-TWO_PI_LO, in1=arg[:],
                                                          op0=ALU.mult, op1=ALU.add))
                    dve.tensor_scalar(arg[:], arg[:], 3.1415925, -3.1415925, ALU.min, ALU.max).then_inc(mlp_arg, 1)

                def mod_rows(n):
                    dve.wait_ge(mod_done, n + 1)
                    dve.tensor_tensor(mod_row[:, n, :], ps_mod[0:2, n % 2, :], mod_row[:, n, :], ALU.add
                                      ).then_inc(mod_row_ready, 1)

                sine_argument(0)
                dve.wait_ge(c_in, 64)
                mod_rows(0)
                mod_rows(1)
                dve.wait_ge(sq_done, NT)
                dve.tensor_scalar(var[:], ss[:], 1.0 / D, EPS, ALU.mult, ALU.add).then_inc(var_ready, 1)
                inverse_root(dve, dt, lambda: dve.wait_ge(root_done, 1), var[:], root[:], inv[:], tmp[:])
                sine_argument(1)
                for t in range(NT):
                    dve.tensor_scalar(x_raw[:, t, :], x_raw[:, t, :], inv[:, t:t + 1], None, ALU.mult
                                      ).then_inc(xn_ready, 1)
                    if t % 4 == 3:
                        mod_rows(2 + t // 4)
                dve.wait_ge(col_done, 1)
                dve.wait_ge(cols_ready, 1)
                col = ps_col[:, 0:4 * KD].rearrange("p (w k j) -> p w j k", w=2, j=2)
                dve.tensor_copy(shift_col[:], col[:, 0])
                for j in range(2):
                    ins = dve.scalar_tensor_tensor(out=scale_col[:, j, :], in0=col[:, 1, j, :], scalar=1.0,
                                                   in1=par[:, C_NORM1:C_BIN], op0=ALU.add, op1=ALU.mult)
                ins.then_inc(cols_ready, 1)
                for n, (k, g) in enumerate(fills):
                    t0, nt, _ = groups[g]
                    cols = slice(t0 * P, (t0 + nt) * P)
                    dve.wait_ge(full_ready, n + 1)
                    dve.tensor_tensor(h_lo[:, k, cols], h_full[:, n % 2, 0:nt * P], h_hi[:, k, cols].bitcast(F32),
                                      ALU.subtract).then_inc(lo_done, 1)


SEG_HY, SEG_Q, SEG_K, SEG_V, SEG_G = (0, 6), (6, 2), (8, 2), (10, 2), (12, 8)
N_UNITS = P_IN // UNIT


def project(nc, sems, a, keep, v_tok):
    h_hi, h_lo, par = keep["h_hi"], keep["h_lo"], keep["par"]
    with ExitStack() as ctx:
        m = Maker(nc, ctx, "proj_")
        w_raw, w_in = keep["w_in"], keep["w_in_sems"]
        w_hi = m.sb("w_hi", [P, 2, KD, UNIT], F32R)
        w_lo = m.sb("w_lo", [P, 2, KD, UNIT], F32R)
        z_pad = m.sb("z_pad", [P, 2, T + 2])
        conv = m.sb("conv", [P, 2, T])
        stage = m.sb("stage", [P, 2, W])
        q_bias = m.sb("q_bias", [P, 4])
        bias = m.sb("bias", [P, CH_UNIT])
        bv_row = m.sb("bv_row", [1, 512])
        ones = m.sb("ones", [1, P])
        ps = m.psum("ps", [P, 8, 512])

        hi_ready, lo_ready, z_done, evacuated, conv_ready = (
            sems(n) for n in ("w_hi_ready", "w_lo_ready", "z_done", "evacuated", "conv_ready"))
        stored = [sems(f"stored{s}") for s in range(2)]
        b_dve, bv_in, const_ready, bias_ready = (
            sems(n) for n in ("b_dve_step", "bv_in", "const_ready", "bias_ready"))

        n_q = 4 * SEG_HY[1]
        n_k = n_q + 4 * SEG_Q[1]
        n_v = n_k + 5 * SEG_K[1]
        n_g = n_v + 5 * SEG_V[1]

        with nc.Block() as block:

            @block.sync
            def _(sp):
                src = a["w_in"].rearrange("(k p) (u n) -> u p k n", p=P, n=UNIT)
                u_d = a["u_d"].rearrange("(c p) t -> c p t", p=P)
                qk_d = a["qk_d"].rearrange("(c p) t -> c p t", p=P)
                g_d = a["g_d"].rearrange("(c p) t -> c p t", p=P)

                def load(u, s):
                    sp.wait_ge(lo_ready, u + 1)
                    sp.dma_start(w_raw[:, s], src[u]).then_inc(w_in[s], 16)

                def store_conv(u):
                    for c in range(CH_UNIT):
                        sp.wait_ge(conv_ready, CH_UNIT * u + c + 3)
                        sp.dma_start(u_d[CH_UNIT * u + c], conv[:, c, :]).then_inc(stored[c], 16)

                def store_stage(n, dst, c0, cols):
                    for c in range(CH_UNIT):
                        sp.wait_ge(evacuated, n + (5 if cols == W else 2 * c + 2) + 8)
                        sp.dma_start(dst[c0 + c, :, 0:cols], stage[:, c, 0:cols]).then_inc(stored[c], 16)

                sp.sem_inc(stored[0], 16)
                sp.sem_inc(stored[1], 16)
                sp.dma_start(bv_row[:], a["b_in"].rearrange("(o r) c -> o (r c)", o=1)[:, 5 * 512:6 * 512]
                             ).then_inc(bv_in, 16)
                with sp.Fori(0, SEG_HY[1] // 2) as i:
                    for s in range(2):
                        load(2 * i + s + 2, s)
                        store_conv(2 * i + s)
                for s in range(2):
                    load(SEG_Q[0] + s + 2, s)
                    store_stage(n_q + 4 * s, qk_d, CH_UNIT * s, T)
                for s in range(2):
                    load(SEG_K[0] + s + 2, s)
                    store_stage(n_k + 5 * s, qk_d, 4 + CH_UNIT * s, W)
                for s in range(2):
                    load(SEG_V[0] + s + 2, s)
                with sp.Fori(0, SEG_G[1] // 2 - 1) as i:
                    for s in range(2):
                        load(SEG_G[0] + 2 * i + s + 2, s)
                        store_stage(n_g + 8 * i + 4 * s, g_d, 4 * i + CH_UNIT * s, T)
                for s in range(2):
                    store_stage(n_g + 24 + 4 * s, g_d, 12 + CH_UNIT * s, T)
                for s in range(2):
                    sp.wait_ge(stored[s], 16 * (6 + 2 + 2 + 8 + 1))

            @block.tensor
            def _(pe):
                pe.sem_inc(z_done, 4)

                def begin(u):
                    pe.wait_ge(lo_ready, u + 3)

                def latents(s, n, n8):
                    for c in range(CH_UNIT):
                        banks = [(n8 + 2 * c + th) % 8 for th in range(2)]
                        pe.wait_ge(evacuated, n + 2 * c + 2)
                        for k in range(KD):
                            hi, lo = (w[:, s, k, c * P:(c + 1) * P] for w in (w_hi, w_lo))
                            for w, h, first, last in ((hi, h_hi, True, False), (hi, h_lo, False, False),
                                                      (lo, h_hi, False, True)):
                                for th in range(2):
                                    mm = pe.matmul(ps[:, banks[th], :], w, h[:, k, th * 512:(th + 1) * 512],
                                                   start=(k == 0 and first), stop=(k == KD - 1 and last))
                                    if k == KD - 1 and last:
                                        mm.then_inc(z_done, 1)

                with pe.Fori(0, SEG_HY[1] // 2) as i:
                    for s in range(2):
                        begin(2 * i + s)
                        latents(s, 8 * i + 4 * s, 4 * s)
                for s in range(2):
                    begin(SEG_Q[0] + s)
                    latents(s, n_q + 4 * s, (n_q + 4 * s) % 8)
                for s in range(2):
                    n = n_k + 5 * s
                    begin(SEG_K[0] + s)
                    latents(s, n, n % 8)
                    n += 4
                    pe.wait_ge(evacuated, n + 1)
                    for c in range(CH_UNIT):
                        for k in range(KD):
                            for x, (w, h) in enumerate(((w_hi, h_hi), (w_hi, h_lo), (w_lo, h_hi))):
                                mm = pe.matmul(ps[:, n % 8, c * CTX:(c + 1) * CTX], w[:, s, k, c * P:(c + 1) * P],
                                               h[:, k, T:W], start=(k == 0 and x == 0), stop=(k == KD - 1 and x == 2))
                    mm.then_inc(z_done, 1)
                pe.wait_ge(bv_in, 16)
                pe.wait_ge(const_ready, 1)
                for s in range(2):
                    begin(SEG_V[0] + s)
                    for tp in range(NT // 2):
                        n = n_v + 5 * s + tp
                        pe.wait_ge(evacuated, n + 1)
                        for t in range(2):
                            o = ps[:, n % 8, t * UNIT:(t + 1) * UNIT]
                            tok = slice((2 * tp + t) * P, (2 * tp + t + 1) * P)
                            pe.matmul(o, ones[:], bv_row[:, s * UNIT:(s + 1) * UNIT], start=True, stop=False)
                            for k in range(KD):
                                for x, (w, h) in enumerate(((w_hi, h_hi), (w_lo, h_hi), (w_hi, h_lo))):
                                    mm = pe.matmul(o, h[:, k, tok], w[:, s, k, :], start=False,
                                                   stop=(k == KD - 1 and x == 2))
                        mm.then_inc(z_done, 1)
                with pe.Fori(0, SEG_G[1] // 2) as i:
                    for s in range(2):
                        begin(SEG_G[0] + 2 * i + s)
                        latents(s, n_g + 8 * i + 4 * s, (n_g + 4 * s) % 8)

            @block.scalar
            def _(act):
                act.sem_inc(evacuated, 8)

                def split(s, i, before):
                    act.wait_ge(w_in[s], 16 * i + 16)
                    if before is not None:
                        act.wait_ge(z_done, before + 4)
                    act.activation(w_hi[:, s], w_raw[:, s], ACT.Copy).then_inc(hi_ready, 1)

                def evacuate(n, bank, out, func, bias, scale=1.0):
                    act.wait_ge(z_done, n + 5)
                    act.activation(out, ps[:, bank, :], func, bias=bias, scale=scale).then_inc(evacuated, 1)

                def own_bias(c, ch, count):
                    act.activation(bias[:, c:c + 1], par[:, bass.ds(C_BIN + ch, 1)], ACT.Copy).then_inc(bias_ready, 1)
                    act.wait_ge(bias_ready, count)
                    return bias[:, c:c + 1]

                act.wait_ge(const_ready, 2)
                split(0, 0, None)
                with act.Fori(0, SEG_HY[1] // 2) as i:
                    for s in range(2):
                        split(1 - s, i + s, 8 * i + 4 * s)
                        for c in range(CH_UNIT):
                            ch = 4 * i + 2 * s + c
                            b = own_bias(c, ch, ch + 1)
                            act.wait_ge(conv_ready, ch + 1)
                            for th in range(2):
                                evacuate(8 * i + 4 * s + 2 * c + th, 4 * s + 2 * c + th,
                                         z_pad[:, c, 1 + th * 512:1 + (th + 1) * 512], ACT.Identity, b)
                for s in range(2):
                    n = n_q + 4 * s
                    split(1 - s, (SEG_Q[0] + s + 1) // 2, n)
                    for c in range(CH_UNIT):
                        ch = CH_UNIT * s + c
                        act.wait_ge(stored[c], 16 * (7 + s))
                        for th in range(2):
                            evacuate(n, n % 8, stage[:, c, th * 512:(th + 1) * 512], ACT.Identity,
                                     q_bias[:, ch:ch + 1], HD ** -0.5)
                            n += 1
                for s in range(2):
                    n = n_k + 5 * s
                    split(1 - s, (SEG_K[0] + s + 1) // 2, n)
                    biases = [par[:, b:b + 1] for b in range(C_BIN + 16 + CH_UNIT * s, C_BIN + 18 + CH_UNIT * s)]
                    for c in range(CH_UNIT):
                        act.wait_ge(stored[c], 16 * (9 + s))
                        for th in range(2):
                            evacuate(n, n % 8, stage[:, c, th * 512:(th + 1) * 512], ACT.Identity, biases[c])
                            n += 1
                    act.wait_ge(z_done, n + 5)
                    for c in range(CH_UNIT):
                        ins = act.activation(stage[:, c, T:W], ps[:, n % 8, c * CTX:(c + 1) * CTX],
                                             ACT.Identity, bias=biases[c])
                    ins.then_inc(evacuated, 1)
                for s in range(2):
                    split(1 - s, (SEG_V[0] + s + 1) // 2, n_v + 5 * s)
                    for tp in range(NT // 2):
                        n = n_v + 5 * s + tp
                        act.wait_ge(z_done, n + 5)
                        act.activation(v_tok[:, 2 * tp:2 * tp + 2, s * UNIT:(s + 1) * UNIT],
                                       ps[:, n % 8, :].rearrange("p (t c) -> p t c", t=2), ACT.Copy
                                       ).then_inc(evacuated, 1)

                def gates(i, s, last=False):
                    u = 2 * i + s
                    if not last:
                        split(1 - s, SEG_G[0] // 2 + i + s, n_g + 4 * u)
                    for c in range(CH_UNIT):
                        b = own_bias(c, 24 + 2 * u + c, 12 + 2 * u + c + 1)
                        act.wait_ge(stored[c], 16 * (11 + u))
                        for th in range(2):
                            evacuate(n_g + 4 * u + 2 * c + th, (n_g + 4 * s + 2 * c + th) % 8,
                                     stage[:, c, th * 512:(th + 1) * 512], ACT.Sigmoid, b)

                with act.Fori(0, SEG_G[1] // 2 - 1) as i:
                    for s in range(2):
                        gates(i, s)
                gates(SEG_G[1] // 2 - 1, 0)
                gates(SEG_G[1] // 2 - 1, 1, last=True)

            @block.vector
            def _(dve):
                dt = Tally(dve, b_dve)
                dve.sem_inc(lo_ready, 2)
                dve.sem_inc(conv_ready, 2)
                dt.inc(dve.memset(z_pad[:, :, 0:1], 0.0))
                dt.inc(dve.memset(z_pad[:, :, T + 1:T + 2], 0.0))
                dve.memset(ones[:], 1.0).then_inc(const_ready, 1)
                dve.tensor_scalar(q_bias[:], par[:, C_BIN + 12:C_BIN + 16], HD ** -0.5, None, ALU.mult
                                  ).then_inc(const_ready, 1)
                dt.wait()

                def split(u, s):
                    dve.wait_ge(hi_ready, u + 1)
                    dve.tensor_tensor(w_lo[:, s], w_raw[:, s], w_hi[:, s].bitcast(F32), ALU.subtract
                                      ).then_inc(lo_ready, 1)

                split(0, 0)
                with dve.Fori(0, SEG_HY[1] // 2) as i:
                    dt.enter(i, 8)
                    for s in range(2):
                        split(2 * i + s + 1, 1 - s)
                        for c in range(CH_UNIT):
                            ch = 4 * i + 2 * s + c

                            def w(j):
                                return par[:, bass.ds(C_SW + 12 * j + ch, 1)]

                            dve.wait_ge(evacuated, 2 * ch + 2 + 8)
                            dve.wait_ge(stored[c], 16 * (2 * i + s + 1))
                            dt.then_wait(dve.tensor_scalar(conv[:, c], z_pad[:, c, 1:T + 1], w(1),
                                                           par[:, bass.ds(C_SB + ch, 1)], ALU.mult, ALU.add))
                            dt.then_wait(dve.scalar_tensor_tensor(out=conv[:, c], in0=z_pad[:, c, 0:T], scalar=w(0),
                                                                  in1=conv[:, c], op0=ALU.mult, op1=ALU.add))
                            dve.scalar_tensor_tensor(out=conv[:, c], in0=z_pad[:, c, 2:T + 2], scalar=w(2),
                                                     in1=conv[:, c], op0=ALU.mult, op1=ALU.add
                                                     ).then_inc(conv_ready, 1)
                    dt.leave(SEG_HY[1] // 2)
                for u in range(SEG_Q[0] + 1, SEG_G[0] + 1):
                    split(u, u % 2)
                with dve.Fori(0, SEG_G[1] // 2 - 1) as i:
                    for s in range(2):
                        split(SEG_G[0] + 2 * i + s + 1, 1 - s)
                split(N_UNITS - 1, 1)



def key_rows(i):
    rs = [min(max(r - WIN_H // 2, 0), ROWS - WIN_H) for r in (2 * i, 2 * i + 1)]
    return rs[0], rs[1] + WIN_H - rs[0]


T_ROWS = 14
T_MIN = -6
HALF = P // 2
CTX0 = 5 * P


def attend(nc, sems, a, keep, v_tok, na_t):
    ident = keep["ident"]
    with ExitStack() as ctx:
        m = Maker(nc, ctx, "attn_")
        q_raw = m.sb("q_raw", [P, 2, T])
        k_raw = m.sb("k_raw", [P, 2, W])
        q_two = m.sb("q_two", [P, 2, T], F32R)
        k_hi, k_lo = m.sb("k_hi", [P, 2, W], F32R), m.sb("k_lo", [P, 2, W], F32R)
        t_raw = m.sb("t_raw", [P, 2, T_ROWS, GRID_W])
        table = m.sb("table", [P, 2, T_ROWS, GRID_W])
        edged = m.sb("edged", [P, 2, WIN_H + 1, GRID_W])
        mask = m.sb("mask", [P, GRID_W])
        score = m.sb("score", [P, 2, (WIN_H + 1) * GRID_W])
        prob = m.sb("prob", [P, 2, CTX0 + CTX])
        prob_t = m.sb("prob_t", [P, 2, 7, P])
        top = m.sb("top", [P, 2, 3])
        sums = m.sb("sums", [P, 4, 4])
        na = m.sb("na", [P, TT, P])
        ps_s = m.psum("ps_s", [P, 2, 1024])
        ps_t = m.psum("ps_t", [P, 2, 512])
        ps_o = m.psum("ps_o", [P, 2, 512])

        qk_in, t_in = ([sems(f"{n}{s}") for s in range(2)] for n in ("qk_in", "t_in"))
        mask_in = sems("mask_in")
        q_high, k_high, q_split, k_split, tables, scored, max_ready, exps, turned = (
            sems(n) for n in ("q_high", "k_high", "q_split", "k_split", "tables", "scored", "max_ready", "exps", "turned"))
        copied, filled, used, step, zeros = (
            sems(n) for n in ("probs_copied", "filled", "used", "c_dve_step", "zeros"))
        PAIRS, UNITS = HEADS // 2, 2 * TT

        FILLS = UNITS + TT

        def f_unit(n):
            return n + max(n - TT - 2, 0)

        def f_turn(i):
            return min(UNITS, i + TT + 3) + i

        def blocks(i):
            r0, n = key_rows(i)
            out = [(b, r0 // 2 + b) for b in range(n // 2)]
            if n % 2:
                out.append((4, r0 // 2 + 4))
            return out

        with nc.Block() as block:

            @block.sync
            def _(sp):
                qk = a["qk_d"].rearrange("(w g p) t -> w g p t", w=2, p=HD)
                sp.dma_start(mask[:], a["na_mask"]).then_inc(mask_in, 16)
                rpb = a["rpb"]
                for g in range(HEADS):
                    hh = g % 2
                    if g >= 2:
                        sp.wait_ge(k_split, 2 * g - 2)
                        sp.wait_ge(q_split, g - 1)
                    for half in range(2):
                        rows = slice(half * HALF, (half + 1) * HALF)
                        sp.dma_start(q_raw[rows, hh], qk[0, g][:, 0:T]).then_inc(qk_in[hh], 16)
                        sp.dma_start(k_raw[rows, hh], qk[1, g]).then_inc(qk_in[hh], 16)
                    if g >= 2:
                        sp.wait_ge(tables, g - 1)
                    for half in range(2):
                        src = bass.AP(rpb.tensor, (g * 15 + 1 - half) * P + 1, [[1, GRID_W], [P, T_ROWS], [1, GRID_W]])
                        sp.dma_start(t_raw[half * HALF:(half + 1) * HALF, hh], src).then_inc(t_in[hh], 16)
                for dst, name in ((keep["h2"][0:FC, :], "hidden_d"), (keep["w3"][0:FC, :], "filt_w3"),
                                  (keep["dft"][:], "dft"), (keep["idft"][:], "idft")):
                    sp.dma_start(dst, a[name]).then_inc(keep["hyena_in"], 16)
                sp.wait_ge(qk_in[0], 64 * PAIRS)
                sp.wait_ge(t_in[0], 32 * PAIRS)
                sp.sem_inc(qk_in[0], 64)
                sp.sem_inc(t_in[0], 32)

            @block.tensor
            def _(pe):
                pe.sem_inc(scored, 1)
                pe.sem_inc(turned, 2)
                pe.sem_inc(filled, 2)
                def turn_probs(j, n):
                    pe.wait_ge(exps, UNITS * j + n + 3)
                    pe.wait_ge(copied, UNITS * j + n + 1)
                    for b, _ in blocks(n % TT) + [(5, 0), (6, 0)]:
                        mm = pe.transpose(ps_t[:, b // 4, (b % 4) * P:(b % 4 + 1) * P],
                                          prob[:, n % 2, b * P:(b + 1) * P], ident[:])
                    mm.then_inc(turned, 1)

                def scores(j, s):
                    i, hh = s % TT, s // TT
                    r0, rows = key_rows(i)
                    if i == 0:
                        pe.wait_ge(k_split, 4 * j + 2 * hh + 2)
                        pe.wait_ge(q_split, 2 * j + hh + 1)
                    cols = [(0, r0 * GRID_W, 512), (512, T, CTX)]
                    if rows > WIN_H:
                        cols = [(0, r0 * GRID_W, 512), (512, r0 * GRID_W + 512, GRID_W), (576, T, CTX)]
                    pe.wait_ge(exps, UNITS * j + s + 1)
                    for o, c, w in cols:
                        for x, k in enumerate((k_hi, k_lo)):
                            mm = pe.matmul(ps_s[:, s % 2, o:o + w], q_two[:, hh, i * P:(i + 1) * P],
                                           k[:, hh, c:c + w], start=(x == 0), stop=(x == 1))
                    mm.then_inc(scored, 1)

                def head_cols(tile, j, hh):
                    at = j * P + hh * HD
                    return v_tok[:, tile, at:at + HD] if isinstance(at, int) else v_tok[:, tile, bass.ds(at, HD)]

                def product(j, n):
                    pe.wait_ge(copied, UNITS * j + n + 2)
                    f = f_unit(n)
                    pe.wait_ge(used, FILLS * j + f + 1)
                    todo = blocks(n % TT) + [(5, TT), (6, TT + 1)]
                    for x, (b, tile) in enumerate(todo):
                        mm = pe.matmul(ps_o[:, f % 2, 0:HD], prob_t[:, n % 2, b, :],
                                       head_cols(tile, j, n // TT),
                                       start=(x == 0), stop=(x == len(todo) - 1))
                    mm.then_inc(filled, 1)

                def turn_out(j, i):
                    f = f_turn(i)
                    pe.wait_ge(used, FILLS * j + max(f_unit(TT + i) + 3, f + 1))
                    pe.transpose(ps_o[:, f % 2, 0:P], na[:, i, :], ident[:]).then_inc(filled, 1)

                def at_step(j, s, now, before):
                    if s >= 2 and now:
                        turn_probs(j, s - 2)
                    elif s < 2 and before:
                        turn_probs(j - 1, UNITS + s - 2)
                    if now:
                        scores(j, s)
                    if s == 3 and before:
                        turn_out(j - 1, TT - 2)
                        turn_out(j - 1, TT - 1)
                    if s >= 3 and now:
                        product(j, s - 3)
                    elif s < 3 and before:
                        product(j - 1, UNITS + s - 3)
                        turn_out(j - 1, TT + s - 5)
                    if s >= TT + 5 and now:
                        turn_out(j, s - TT - 5)

                for s in range(UNITS):
                    at_step(0, s, True, False)
                with pe.Fori(1, PAIRS) as j:
                    for s in range(UNITS):
                        at_step(j, s, True, True)
                for s in range(4):
                    at_step(PAIRS, s, False, True)

            @block.scalar
            def _(act):
                act.sem_inc(exps, 2)
                act.sem_inc(copied, 1)
                act.wait_ge(zeros, 1)

                def high(hh, which):
                    if which:
                        cols = slice((which - 1) * W // 2, which * W // 2)
                        act.activation(k_hi[:, hh, cols], k_raw[:, hh, cols], ACT.Copy).then_inc(k_high, 1)
                    else:
                        act.activation(q_two[:, hh], q_raw[:, hh], ACT.Copy).then_inc(q_high, 1)

                act.wait_ge(qk_in[0], 64)
                high(0, 0)
                high(0, 1)
                high(0, 2)
                def copy_probs(j, n):
                    lo = 4 if key_rows(n % TT)[1] > WIN_H else 5
                    act.wait_ge(turned, UNITS * j + n + 3)
                    if n >= 2:
                        act.wait_ge(filled, FILLS * j + f_unit(n - 2) + 3)
                    elif not (isinstance(j, int) and j == 0):
                        act.wait_ge(filled, FILLS * (j - 1) + f_unit(UNITS + n - 2) + 3)
                    act.activation(prob_t[:, n % 2, 0:4, :], ps_t[:, 0, :].rearrange(
                        "p (b q) -> p b q", q=P), ACT.Copy)
                    act.activation(prob_t[:, n % 2, lo:7, :], ps_t[:, 1, (lo - 4) * P:3 * P].rearrange(
                        "p (b q) -> p b q", q=P), ACT.Copy).then_inc(copied, 1)

                def exponentials(j, s):
                    n, w = s, key_rows(s % TT)[1] * GRID_W
                    act.wait_ge(max_ready, UNITS * j + n + 1)
                    act.wait_ge(turned, UNITS * j + n + 1)
                    act.activation(prob[:, n % 2, 0:w], score[:, n % 2, 0:w], ACT.Exp,
                                   bias=top[:, n % 2, 2:3], accum_out=sums[:, n % 4, 0:1])
                    act.activation(prob[:, n % 2, CTX0:CTX0 + CTX], ps_s[:, n % 2, w:w + CTX], ACT.Exp,
                                   bias=top[:, n % 2, 2:3], accum_out=sums[:, n % 4, 1:2]).then_inc(exps, 1)

                def at_step(j, s, now, before):
                    if now:
                        if s in (1, TT + 1):
                            nh = s // TT
                            act.wait_ge(qk_in[1 - nh], 64 * (j + nh) + 64)
                            act.wait_ge(scored, UNITS * j + TT * nh + 1)
                            high(1 - nh, 0)
                        if s % TT in (2, 3):
                            high(1 - s // TT, s % TT - 1)
                    if s >= 2 and now:
                        copy_probs(j, s - 2)
                    elif s < 2 and before:
                        copy_probs(j - 1, UNITS + s - 2)
                    if now:
                        exponentials(j, s)

                for s in range(UNITS):
                    at_step(0, s, True, False)
                with act.Fori(1, PAIRS) as j:
                    for s in range(UNITS):
                        at_step(j, s, True, True)
                for s in range(2):
                    at_step(PAIRS, s, False, True)

            @block.vector
            def _(dve):
                dt = Tally(dve, step)
                dve.sem_inc(used, 2)
                dve.memset(prob[:, :, 9 * GRID_W:CTX0], 0.0).then_inc(zeros, 1)
                dve.memset(keep["w3"][FC:P, :], 0.0)
                dve.memset(keep["h2"][FC:P, :], 0.0)
                dve.memset(edged[0:HALF, :, WIN_H], NEG)
                dve.memset(edged[HALF:P, :, 0], NEG)
                dve.wait_ge(mask_in, 16)

                def low_q(turn, hh):
                    dve.wait_ge(q_high, 2 * turn + hh + 1)
                    dve.tensor_tensor(q_two[HALF:P, hh], q_raw[HALF:P, hh], q_two[HALF:P, hh].bitcast(F32),
                                      ALU.subtract).then_inc(q_split, 1)

                def low_k(turn, hh, half):
                    cols = slice(half * W // 2, (half + 1) * W // 2)
                    dve.wait_ge(k_high, 4 * turn + 2 * hh + half + 1)
                    dve.tensor_tensor(k_lo[:, hh, cols], k_raw[:, hh, cols], k_hi[:, hh, cols].bitcast(F32),
                                      ALU.subtract).then_inc(k_split, 1)

                def make_table(turn, hh):
                    dve.wait_ge(t_in[hh], 32 * turn + 32)
                    dt.then_wait(dve.tensor_tensor(table[:, hh], t_raw[:, hh, :, ::-1], mask[:].unsqueeze(1).broadcast_to(
                        [P, T_ROWS, GRID_W]), ALU.add))
                    for part, first in ((slice(0, HALF), 0), (slice(HALF, P), 1)):
                        src = table[part, hh, first - WIN_H // 2 - T_MIN:first + WIN_H // 2 - T_MIN]
                        dt.inc(dve.tensor_scalar(edged[part, hh, first:first + WIN_H], src, 1.0, None, ALU.mult))
                    dt.wait()
                    dve.sem_inc(tables, 1)

                low_q(0, 0)
                low_k(0, 0, 0)
                low_k(0, 0, 1)
                make_table(0, 0)
                def maxima(j, s):
                    n, i, hh = s, s % TT, s // TT
                    r0, rows = key_rows(i)
                    w = rows * GRID_W
                    first = r0 - 2 * i - T_MIN
                    bias = edged[:, hh] if rows > WIN_H else table[:, hh, first:first + WIN_H]
                    dve.wait_ge(scored, UNITS * j + n + 2)
                    dt.inc(dve.reduce_max(top[:, n % 2, 1:2], ps_s[:, n % 2, w:w + CTX], AX_X))
                    dt.then_wait(dve.tensor_tensor_reduce(score[:, n % 2, 0:w], ps_s[:, n % 2, 0:w],
                                                         bias.rearrange("p r c -> p (r c)"), 1.0, -3.0e38,
                                                         ALU.add, ALU.max, top[:, n % 2, 0:1]))
                    dve.tensor_scalar(top[:, n % 2, 2:3], top[:, n % 2, 0:1], top[:, n % 2, 1:2], -1.0,
                                      ALU.max, ALU.mult).then_inc(max_ready, 1)

                def keep_out(j, i):
                    f = f_turn(i)
                    dve.wait_ge(filled, FILLS * j + f + 3)
                    dve.tensor_scalar(na_t[:, j, i * P:(i + 1) * P], ps_o[:, f % 2, 0:P], 1.0, None,
                                      ALU.mult).then_inc(used, 1)

                def normalize(j, n):
                    i = n % TT
                    f = f_unit(n)
                    dt.then_wait(dve.tensor_tensor(sums[:, n % 4, 2:3], sums[:, n % 4, 0:1],
                                                   sums[:, n % 4, 1:2], ALU.add))
                    dt.then_wait(dve.reciprocal(sums[:, n % 4, 3:4], sums[:, n % 4, 2:3]))
                    dve.wait_ge(filled, FILLS * j + f + 3)
                    dve.tensor_scalar(na[:, i, n // TT * HD:(n // TT + 1) * HD], ps_o[:, f % 2, 0:HD],
                                      sums[:, n % 4, 3:4], None, ALU.mult).then_inc(used, 1)

                def at_step(j, s, now, before):
                    if now:
                        maxima(j, s)
                        if 2 <= s % TT <= 5:
                            at = (j + s // TT, 1 - s // TT)
                            if s % TT == 2:
                                low_q(*at)
                            elif s % TT == 5:
                                make_table(*at)
                            else:
                                low_k(*at, s % TT - 3)
                    if s <= 3 and before:
                        for i in [TT + s - 6] + [TT - 2, TT - 1] * (s == 3):
                            keep_out(j - 1, i)
                    if s >= TT + 6 and now:
                        keep_out(j, s - TT - 6)
                    if s >= 3 and now:
                        normalize(j, s - 3)
                    elif s < 3 and before:
                        normalize(j - 1, UNITS + s - 3)

                for s in range(UNITS):
                    at_step(0, s, True, False)
                with dve.Fori(0, PAIRS - 1) as turn:
                    dt.enter(turn, 6 + 4 * UNITS)
                    for s in range(UNITS):
                        at_step(turn + 1, s, True, True)
                    dt.leave(PAIRS - 1)
                for s in range(4):
                    at_step(PAIRS, s, False, True)


BLK = 256
NB = T // BLK

HALF_C = HY // 2
PASSES = 4


def hyena(nc, sems, a, keep, y_t):
    par, ident, c_silu = keep["par"], keep["ident"], keep["c_silu"]
    with ExitStack() as ctx:
        m = Maker(nc, ctx, "hyena_")
        h2, w3, dft, idft, consts_in = (keep[n] for n in ("h2", "w3", "dft", "idft", "hyena_in"))
        decay = m.sb("decay", [P, 2, 2, HALF_C])
        seg = m.sb("seg", [P, 2, 2, 2, HALF_C])
        win = m.sb("win", [P, 2, 2, NB, 4, HALF_C])
        u_tok = m.sb("u_tok", [P, TT, HALF_C])
        uf = m.sb("uf", [P, 2, NB, 4, HALF_C])
        yf = m.sb("yf", [P, 2, 4, HALF_C])
        cross = m.sb("cross", [P, 4, HALF_C])
        t1, t2 = m.sb("t1", [P, 4, HALF_C]), m.sb("t2", [P, 4, HALF_C])
        gate = m.sb("gate", [P, 2, 2, BLK])
        w_mod = m.sb("w_mod", [P, KD // 2, 512])
        mod_row = m.sb("mod_row", [2, 2, 512])
        A_BANKS = 3
        ps_a = m.psum("ps_a", [P, A_BANKS, 512])
        ps_mod = m.psum("ps_mod", [P, 512])
        ps_tap = m.psum("ps_tap", [P, 2, 512])
        ps_out = m.psum("ps_out", [P, 2, 512])

        v_in, w_mod_in, mod_done, mod_added, mod_out = (
            sems(n) for n in ("v_in", "mod_half_in", "mod_half_done", "mod_added", "mod_out"))
        b_in = [sems(f"b_mod_in{s}") for s in range(2)]
        a_done, a_used, tap_done, tap_used, out_done, out_used, y_ready = (
            sems(n) for n in ("a_done", "a_used", "tap_done", "tap_used", "out_done", "out_used", "yf_ready"))
        step = sems("d_dve_step")
        decay_in = [sems(f"decay_in{s}") for s in range(2)]
        gate_in = [sems(f"gate_in{s}") for s in range(2)]

        a_order = []
        for q in range(PASSES):
            for i in range(NB):
                a_order += [("seg", q, i, pl) for pl in range(4)]
                if i % 2 == 0:
                    a_order += [("turn", q, i), ("turn", q, i + 1)]
                a_order += [("input", q, i // 2, pl) for pl in (i % 2 * 2, i % 2 * 2 + 1)]
        a_at = {what: n for n, what in enumerate(a_order)}
        PER_A = len(a_order) // PASSES

        def split(p):
            return p // 2, p % 2

        with nc.Block() as block:

            @block.sync
            def _(sp):
                u_d = a["u_d"].rearrange("(o c p) t -> o p c t", c=4, p=P)
                sp.dma_start(y_t[:], u_d[0]).then_inc(v_in, 16)
                decays = a["decay"].rearrange("(b s p) c -> b p s c", s=2, p=P)
                w_src = a["w_mod"].rearrange("(p h k) (n c) -> n h p k c", h=2, k=KD // 2, c=512)
                mod_dst = a["mod_d"].rearrange("j (n c) -> n j c", c=512)
                for p in range(-1, PASSES):
                    q = p + 1
                    for i in range(NB):
                        if q < PASSES:
                            h = q % 2
                            if NB * q + i >= 2:
                                sp.wait_ge(tap_used, 2 * (NB * q + i) - 2)
                            sp.dma_start(decay[:, i % 2], decays[i][:, :, h * HALF_C:(h + 1) * HALF_C]
                                         ).then_inc(decay_in[i % 2], 16)
                        if p >= 0:
                            o, h = split(p)
                            if NB * p + i >= 2:
                                sp.wait_ge(out_used, NB * p + i - 1)
                            sp.dma_start(gate[:, i % 2], u_d[o + 1][:, 2 * h:2 * h + 2, i * BLK:(i + 1) * BLK]
                                         ).then_inc(gate_in[i % 2], 16)
                        if p >= 0:
                            n = NB * p + i
                            chunk = MOD_EARLY + n // 2
                            if n % 2 == 0:
                                if n:
                                    sp.wait_ge(mod_added, n // 2)
                                    sp.dma_start(mod_dst[chunk - 1], mod_row[:, (chunk - 1) % 2]).then_inc(mod_out, 16)
                                if n >= 4:
                                    sp.wait_ge(mod_out, 16 * (n // 2))
                                sp.dma_start(mod_row[:, chunk % 2], bass.AP(a["b_mod"].tensor, chunk * 512, [[0, 2], [1, 512]])
                                             ).then_inc(b_in[chunk % 2], 16)
                            if n:
                                sp.wait_ge(mod_done, n)
                            sp.dma_start(w_mod[:], w_src[chunk, n % 2]).then_inc(w_mod_in, 16)
                sp.wait_ge(mod_added, MOD_CHUNKS - MOD_EARLY)
                sp.dma_start(mod_dst[MOD_CHUNKS - 1], mod_row[:, (MOD_CHUNKS - 1) % 2]).then_inc(mod_out, 16)
                sp.wait_ge(mod_out, 16 * (MOD_CHUNKS - MOD_EARLY))

            @block.tensor
            def _(pe):
                pe.wait_ge(consts_in, 4 * 16)

                def bank(what):
                    n = a_at[what]
                    if n >= A_BANKS:
                        pe.wait_ge(a_used, n - A_BANKS + 1)
                    return ps_a[:, n % A_BANKS, :]

                def taps(q, i):
                    o, h = split(q)
                    for s in range(2):
                        n = 2 * (NB * q + i) + s
                        if n >= 2:
                            pe.wait_ge(tap_used, n - 1)
                        for d in range(2):
                            at = (2 * d + o) * HY + h * HALF_C
                            mm = pe.matmul(ps_tap[:, s, d * HALF_C:(d + 1) * HALF_C],
                                           h2[:, (2 * i + s) * P:(2 * i + s + 1) * P],
                                           w3[:, at:at + HALF_C], start=True, stop=True)
                        mm.then_inc(tap_done, 1)

                taps(0, 0)
                for p in range(-1, PASSES):
                    q = p + 1
                    for i in range(NB):
                        if q < PASSES:
                            pe.wait_ge(tap_used, 2 * (NB * q + i) + 2)
                            for pl in range(4):
                                to = bank(("seg", q, i, pl))
                                for s in range(2):
                                    mm = pe.matmul(to, dft[:, s, pl, :], seg[:, i % 2, s].rearrange("p d c -> p (d c)"),
                                                   start=(s == 0), stop=(s == 1))
                                mm.then_inc(a_done, 1)
                            if NB * q + i + 1 < NB * PASSES:
                                taps((NB * q + i + 1) // NB, (i + 1) % NB)
                            o, h = split(q)
                            if o and i == 0:
                                pe.wait_ge(out_used, NB * (q - 2) + NB)
                            if q == 0 and i == 0:
                                pe.wait_ge(v_in, 16)
                            if i % 2 == 0:
                                for b in (i, i + 1):
                                    to = bank(("turn", q, b))
                                    for t in range(2):
                                        for c in range(2):
                                            mm = pe.transpose(to[:, (2 * t + c) * P:(2 * t + c + 1) * P],
                                                              y_t[:, 2 * h + c, (2 * b + t) * P:(2 * b + t + 1) * P], ident[:])
                                    mm.then_inc(a_done, 1)
                        if p >= 0:
                            n = NB * p + i
                            half = n % 2
                            pe.wait_ge(w_mod_in, 16 * n + 16)
                            if half == 0 and n:
                                pe.wait_ge(mod_added, n // 2)
                            for k in range(KD // 2):
                                mm = pe.matmul(ps_mod[0:2, :], c_silu[:, half * KD // 2 + k, :], w_mod[:, k, :],
                                               start=(half == 0 and k == 0), stop=(half == 1 and k == KD // 2 - 1))
                            mm.then_inc(mod_done, 1)
                        if q < PASSES:
                            pe.wait_ge(a_used, a_at["turn", q, i // 2 * 2 + 1] + 1)
                            for pl in (i % 2 * 2, i % 2 * 2 + 1):
                                to = bank(("input", q, i // 2, pl)).rearrange("p (b c) -> p b c", b=2)
                                for s in range(2):
                                    b = i // 2 * 2
                                    mm = pe.matmul(to, dft[:, s, pl, :], u_tok[:, 2 * b + s:2 * b + 4:2, :],
                                                   start=(s == 0), stop=(s == 1))
                                mm.then_inc(a_done, 1)
                        if p >= 0:
                            n = NB * p + i
                            pe.wait_ge(y_ready, n + 1)
                            if n >= 2:
                                pe.wait_ge(out_used, n - 1)
                            for c in range(2):
                                for pl in range(4):
                                    mm = pe.matmul(ps_out[:, i % 2, c * BLK:(c + 1) * BLK],
                                                   yf[:, i % 2, pl, c * P:(c + 1) * P], idft[:, pl, :],
                                                   start=(pl == 0), stop=(pl == 3))
                            mm.then_inc(out_done, 1)

            @block.scalar
            def _(act):
                for n, what in enumerate(a_order):
                    kind, q, i = what[0:3]
                    h, src = q % 2, ps_a[:, n % A_BANKS, :].rearrange("p (x c) -> p x c", x=2)
                    if kind == "turn":
                        out = u_tok[:, 2 * i:2 * i + 2, :]
                    elif kind == "seg":
                        if q >= 2 and i == 0:
                            act.wait_ge(y_ready, NB * (q - 2) + NB)
                        out = win[:, h, :, i, what[3], :]
                    else:
                        out = uf[:, h, 2 * i:2 * i + 2, what[3], :]
                    act.wait_ge(a_done, n + 1)
                    act.activation(out, src, ACT.Copy).then_inc(a_used, 1)

            @block.vector
            def _(dve):
                dt = Tally(dve, step)

                def decayed(q, i):
                    dve.wait_ge(decay_in[i % 2], 16 * (NB // 2 * q + i // 2 + 1))
                    if NB * q + i >= 2:
                        before = NB * q + i - 2
                        dve.wait_ge(a_done, a_at["seg", before // NB, before % NB, 3] + 1)
                    for s in range(2):
                        dve.wait_ge(tap_done, 2 * (NB * q + i) + s + 1)
                        ins = dve.tensor_tensor(
                            seg[:, i % 2, s], ps_tap[:, s, :].rearrange("p (d c) -> p d c", d=2),
                            decay[:, i % 2, s, :].unsqueeze(1).broadcast_to([P, 2, HALF_C]), ALU.mult)
                        if i == 0 and s == 0:
                            dt.then_wait(ins)
                            ins = dve.memset(seg[0:1, 0, 0, 1, :], 0.0)
                        ins.then_inc(tap_used, 1)

                def products(p, i):
                    h, y = p % 2, yf[:, i % 2]
                    planes = "p (e r) c -> p e r c"
                    if NB * p + i >= 2:
                        dve.wait_ge(out_done, NB * p + i - 1)
                    for j in range(NB):
                        k = win[:, h, 0 if i >= j else 1, abs(i - j)].rearrange(planes, e=2)
                        re, im = (k[:, :, x, :].unsqueeze(2).broadcast_to([P, 2, 2, HALF_C]) for x in range(2))
                        u = uf[:, h, j].rearrange(planes, e=2)
                        if j == 0:
                            dt.inc(dve.tensor_tensor(y.rearrange(planes, e=2), re, u, ALU.mult))
                            dt.inc(dve.tensor_tensor(cross[:].rearrange(planes, e=2), im, u, ALU.mult))
                        else:
                            dt.wait(1)
                            dt.inc(dve.tensor_tensor(t1[:].rearrange(planes, e=2), re, u, ALU.mult))
                            dt.wait(1)
                            dt.inc(dve.tensor_tensor(t2[:].rearrange(planes, e=2), im, u, ALU.mult))
                            dt.wait(1)
                            dt.inc(dve.tensor_tensor(y, y, t1[:], ALU.add))
                            dt.wait(1)
                            dt.inc(dve.tensor_tensor(cross[:], cross[:], t2[:], ALU.add if i >= j else ALU.subtract))
                    dt.wait()
                    yv, cv = (x.rearrange(planes, e=2) for x in (y, cross[:]))
                    dt.inc(dve.tensor_tensor(yv[:, :, 0], yv[:, :, 0], cv[:, :, 1], ALU.subtract))
                    dt.inc(dve.tensor_tensor(yv[:, :, 1], yv[:, :, 1], cv[:, :, 0], ALU.add))
                    dt.wait()
                    dve.sem_inc(y_ready, 1)

                def gated(p, i):
                    o, h = split(p)
                    dve.wait_ge(out_done, NB * p + i + 1)
                    dve.wait_ge(gate_in[i % 2], 16 * (NB // 2 * p + i // 2 + 1))
                    for c in range(2):
                        ch, tok = 2 * h + c, slice(i * BLK, (i + 1) * BLK)
                        dt.inc(dve.scalar_tensor_tensor(
                            out=y_t[:, ch, tok], in0=y_t[:, ch, tok], scalar=par[:, C_SKIP + 4 * o + ch:C_SKIP + 4 * o + ch + 1],
                            in1=ps_out[:, i % 2, c * BLK:(c + 1) * BLK], op0=ALU.mult, op1=ALU.add))
                    dt.wait()
                    pair = y_t[:, 2 * h:2 * h + 2, i * BLK:(i + 1) * BLK]
                    dve.tensor_tensor(pair, pair, gate[:, i % 2], ALU.mult).then_inc(out_used, 1)

                for p in range(-1, PASSES):
                    q = p + 1
                    for i in range(NB):
                        if q < PASSES:
                            decayed(q, i)
                        if p >= 0:
                            products(p, i)
                            if i:
                                gated(p, i - 1)
                        if p >= 0 and i % 2:
                            n = (NB * p + i) // 2
                            dve.wait_ge(mod_done, 2 * n + 2)
                            dve.wait_ge(b_in[n % 2], 16 * (n // 2) + 16)
                            row = mod_row[:, (MOD_EARLY + n) % 2]
                            dve.tensor_tensor(row, ps_mod[0:2, :], row, ALU.add).then_inc(mod_added, 1)
                    if q < PASSES:
                        h = q % 2
                        dve.wait_ge(a_used, PER_A * (q + 1))
                        for b in range(NB - 1, 0, -1):
                            new, old = (win[:, h, :, x].rearrange("p d (e r) c -> p d e r c", e=2) for x in (b, b - 1))
                            for e, (re, im) in enumerate(((ALU.subtract, ALU.add), (ALU.add, ALU.subtract))):
                                dt.inc(dve.tensor_tensor(new[:, :, e, 0], new[:, :, e, 0], old[:, :, e, 1], re))
                                dt.inc(dve.tensor_tensor(new[:, :, e, 1], new[:, :, e, 1], old[:, :, e, 0], im))
                            dt.wait()
                        w0, f0 = (win[:, h, d, 0].rearrange("p (e r) c -> p e r c", e=2) for d in range(2))
                        dt.inc(dve.tensor_tensor(w0[:, :, 0], w0[:, :, 0], f0[:, :, 0], ALU.add))
                        dt.inc(dve.tensor_tensor(w0[:, :, 1], w0[:, :, 1], f0[:, :, 1], ALU.subtract))
                        dt.wait()
                    if p >= 0:
                        gated(p, NB - 1)


def merge(nc, sems, a, y_t, na_t, m_t):
    with ExitStack() as ctx:
        m = Maker(nc, ctx, "merge_")
        in_hi, in_lo = m.sb("in_hi", [P, 2, 4, T], F32R), m.sb("in_lo", [P, 2, 4, T], F32R)
        b_raw = m.sb("b_raw", [P, 2, 2, 4, P])
        b_hi, b_lo = m.sb("b_hi", [P, 2, 2, 4, P], F32R), m.sb("b_lo", [P, 2, 2, 4, P], F32R)
        gate = m.sb("gate", [P, 2, 2, T])
        part = m.sb("part", [P, 2, 2, 512])
        ps = m.psum("ps", [P, 4, 2, 512])

        w_in = [sems(f"branch_in{s}") for s in range(2)]
        g_in = [sems(f"gates_in{s}") for s in range(2)]
        in_hi_ready, in_lo_ready, bh_ready, bl_ready, branched, merged, step = (
            sems(n) for n in ("in_hi_ready", "in_lo_ready", "bh_ready", "bl_ready", "branched", "merged", "e_dve_step"))

        with nc.Block() as block:

            @block.sync
            def _(sp):
                w = [a[n].rearrange("(k p) (d c) -> d p k c", p=P, c=P) for n in ("w_branch_hy", "w_branch_na")]
                g = a["g_d"].rearrange("(b d p) t -> b d p t", b=2, p=P)
                with sp.Fori(0, KD // 2) as i:
                    for s in range(2):
                        d = 2 * i + s
                        sp.wait_ge(bl_ready, d + 1)
                        for b in range(2):
                            sp.dma_start(b_raw[:, s, b], w[b][d]).then_inc(w_in[s], 16)
                        sp.wait_ge(merged, 2 * d + 2)
                        for b in range(2):
                            sp.dma_start(gate[:, s, b], g[b, d]).then_inc(g_in[s], 16)

            @block.tensor
            def _(pe):
                pe.sem_inc(branched, 4)
                with pe.Fori(0, KD // 2) as i:
                    for s in range(2):
                        pe.wait_ge(bl_ready, 2 * i + s + 3)
                        for th in range(2):
                            n = 2 * s + th
                            pe.wait_ge(merged, 4 * i + n + 1)
                            for b in range(2):
                                for k in range(4):
                                    if n == 0:
                                        pe.wait_ge(in_lo_ready, 4 * b + k + 1)
                                    hi, lo = b_hi[:, s, b, k, :], b_lo[:, s, b, k, :]
                                    cols = slice(th * 512, (th + 1) * 512)
                                    for x, (w, h) in enumerate(((hi, in_hi), (hi, in_lo), (lo, in_hi))):
                                        mm = pe.matmul(ps[:, n, b, :], w, h[:, b, k, cols],
                                                       start=(k == 0 and x == 0), stop=(k == 3 and x == 2))
                            mm.then_inc(branched, 1)

            @block.scalar
            def _(act):
                def split(s, i, d):
                    act.wait_ge(w_in[s], 32 * i + 32)
                    act.wait_ge(branched, 2 * d + 2)
                    act.activation(b_hi[:, s], b_raw[:, s], ACT.Copy).then_inc(bh_ready, 1)

                split(0, 0, 0)
                for b, src in enumerate((y_t, na_t)):
                    for k in range(4):
                        act.activation(in_hi[:, b, k, :], src[:, k, :], ACT.Copy).then_inc(in_hi_ready, 1)
                with act.Fori(0, KD // 2 - 1) as i:
                    split(1, i, 2 * i + 1)
                    split(0, i + 1, 2 * i + 2)
                split(1, KD // 2 - 1, KD - 1)

            @block.vector
            def _(dve):
                dt = Tally(dve, step)
                dve.sem_inc(bl_ready, 2)
                dve.sem_inc(merged, 4)
                def split(d, s):
                    dve.wait_ge(bh_ready, d + 1)
                    dve.tensor_tensor(b_lo[:, s], b_raw[:, s], b_hi[:, s].bitcast(F32), ALU.subtract
                                      ).then_inc(bl_ready, 1)

                def gated(i, s):
                    for th in range(2):
                        n = 2 * s + th
                        cols = slice(th * 512, (th + 1) * 512)
                        dve.wait_ge(branched, 4 * i + n + 5)
                        dve.wait_ge(g_in[s], 32 * i + 32)
                        dve.wait_ge(merged, 4 * i + n + 3)
                        for b in range(2):
                            dt.inc(dve.tensor_tensor(part[:, th, b], ps[:, n, b, :], gate[:, s, b, cols], ALU.mult))
                        dt.wait()
                        dve.tensor_tensor(m_t[:, 2 * i + s, cols], part[:, th, 0], part[:, th, 1], ALU.add
                                          ).then_inc(merged, 1)

                split(0, 0)
                for b, src in enumerate((y_t, na_t)):
                    for k in range(4):
                        dve.wait_ge(in_hi_ready, 4 * b + k + 1)
                        dve.tensor_tensor(in_lo[:, b, k, :], src[:, k, :], in_hi[:, b, k, :].bitcast(F32),
                                          ALU.subtract).then_inc(in_lo_ready, 1)

                with dve.Fori(0, KD // 2 - 1) as i:
                    dt.enter(i, 8)
                    for s in range(2):
                        split(2 * i + s + 1, 1 - s)
                        gated(i, s)
                    dt.leave(KD // 2 - 1)
                split(KD - 1, 1)
                gated(KD // 2 - 1, 0)
                gated(KD // 2 - 1, 1)


def project_out(nc, sems, a, keep, m_t, logits):
    ident = keep["ident"]
    with ExitStack() as ctx:
        m = Maker(nc, ctx, "out_")
        w_raw = m.sb("w_raw", [P, KD, D])
        w_hi, w_lo = m.sb("w_hi", [P, KD, D], F32R), m.sb("w_lo", [P, KD, D], F32R)
        m_hi, m_lo = m.sb("m_hi", [P, 2, KD, P], F32R), m.sb("m_lo", [P, 2, KD, P], F32R)
        router = m.sb("router", [P, KD, E_N])
        g1_row, scale_row, shift_row, gain_row = (m.sb(n, [P, D]) for n in ("g1_row", "scale_row", "shift_row", "gain_row"))
        x_in = m.sb("x_in", [P, 2, D])
        x1 = m.sb("x1", [P, 2, D])
        h2 = m.sb("h2", [P, 2, D])
        h2_t = m.sb("h2_t", [P, 2, KD, P])
        squares = gain_row
        stat = m.sb("stat", [P, 2, 5])
        ps_o = m.psum("ps_o", [P, 2, D])
        ps_h = m.psum("ps_h", [P, D])

        rows_in = sems("rows_in")
        wo_in = [sems(f"w_out_in{s}") for s in range(2)]
        xt_in = [sems(f"x_tile_in{s}") for s in range(2)]
        stored = [sems(f"f_stored{s}") for s in range(2)]
        wo_hi, wo_lo, m_split, projected, x1_ready, squared, var_ready, rooted, normed, turned, copied, routed = (
            sems(n) for n in ("wo_hi", "wo_lo", "m_split", "projected", "x1_ready", "squared", "f_var_ready", "rooted",
                              "f_normed", "f_turned", "f_copied", "routed"))
        step, gain_used = sems("f_dve_step"), sems("gain_used")

        with nc.Block() as block:

            @block.sync
            def _(sp):
                w = a["w_out"].rearrange("(k p) n -> p k n", p=P)
                mod = a["mod_d"]
                for k in range(0, KD, 2):
                    sp.dma_start(w_raw[:, k:k + 2], w[:, k:k + 2]).then_inc(wo_in[k // 4], 16)
                for dst, at in ((g1_row, 2 * D), (shift_row, 3 * D), (scale_row, 4 * D)):
                    sp.dma_start(dst[:], bass.AP(mod.tensor, at, [[0, P], [1, D]])).then_inc(rows_in, 16)
                sp.dma_start(gain_row[:], bass.AP(a["norm2_g"].tensor, 0, [[0, P], [1, D]])).then_inc(rows_in, 16)
                sp.dma_start(router[:], a["w_router"].rearrange("(k p) e -> p k e", p=P)).then_inc(rows_in, 16)
                x_t, acc_t, h2_t_d = (a[n].rearrange("(t p) d -> t p d", p=P) for n in ("x", "acc_d", "h2_d"))
                sp.sem_inc(stored[0], 32)
                sp.sem_inc(stored[1], 32)

                def load(t, s):
                    sp.wait_ge(x1_ready, t + 1)
                    sp.dma_start(x_in[:, s], x_t[t]).then_inc(xt_in[s], 16)

                def store(t, s):
                    sp.wait_ge(x1_ready, t + 3)
                    sp.dma_start(acc_t[t], x1[:, s]).then_inc(stored[s], 16)
                    sp.wait_ge(normed, t + 3)
                    sp.dma_start(h2_t_d[t], h2[:, s]).then_inc(stored[s], 16)

                load(0, 0)
                load(1, 1)
                with sp.Fori(0, TT // 2 - 1) as i:
                    for s in range(2):
                        store(2 * i + s, s)
                        load(2 * i + s + 2, s)
                store(TT - 2, 0)
                store(TT - 1, 1)
                for s in range(2):
                    sp.wait_ge(stored[s], 32 * (TT // 2 + 1))

            @block.tensor
            def _(pe):
                pe.sem_inc(projected, 2)
                pe.sem_inc(turned, 2)
                pe.sem_inc(routed, 2)

                def out(t, s, first=False):
                    pe.wait_ge(m_split, t + 3)
                    pe.wait_ge(x1_ready, t + 1)
                    for k in range(KD):
                        if first:
                            pe.wait_ge(wo_lo, k + 1)
                        for x, (h, w) in enumerate(((m_hi, w_hi), (m_hi, w_lo), (m_lo, w_hi))):
                            for n in range(2):
                                mm = pe.matmul(ps_o[:, s, n * 512:(n + 1) * 512], h[:, s, k, :],
                                               w[:, k, n * 512:(n + 1) * 512], start=(k == 0 and x == 0),
                                               stop=(k == KD - 1 and x == 2))
                    mm.then_inc(projected, 1)

                def turn(t, s):
                    pe.wait_ge(normed, t + 3)
                    pe.wait_ge(copied, t + 1)
                    for k in range(KD):
                        mm = pe.transpose(ps_h[:, k * P:(k + 1) * P], h2[:, s, k * P:(k + 1) * P], ident[:])
                    mm.then_inc(turned, 1)

                def route(t, s):
                    pe.wait_ge(copied, t + 2)
                    for k in range(KD):
                        mm = pe.matmul(logits[:, bass.ds(t * E_N, E_N)] if not isinstance(t, int)
                                       else logits[:, t * E_N:(t + 1) * E_N], h2_t[:, s, k, :], router[:, k, :],
                                       start=(k == 0), stop=(k == KD - 1))
                    mm.then_inc(routed, 1)

                out(0, 0, first=True)
                pe.wait_ge(rows_in, 5 * 16)
                out(1, 1)
                turn(0, 0)
                with pe.Fori(0, TT // 2 - 1) as i:
                    for s in range(2):
                        out(2 * i + s + 2, s)
                        turn(2 * i + s + 1, 1 - s)
                        route(2 * i + s, s)
                turn(TT - 1, 1)
                route(TT - 2, 0)
                route(TT - 1, 1)

            @block.scalar
            def _(act):
                act.sem_inc(copied, 1)
                act.sem_inc(x1_ready, 2)
                for k in range(KD):
                    act.wait_ge(wo_in[k // 4], 32)
                    act.activation(w_hi[:, k, :], w_raw[:, k, :], ACT.Copy).then_inc(wo_hi, 1)
                act.wait_ge(gain_used, 1)
                with act.Fori(0, TT // 2) as i:
                    for s in range(2):
                        t = 2 * i + s
                        act.wait_ge(x1_ready, t + 3)
                        act.activation(squares[:], x1[:, s], ACT.Square, accum_out=stat[:, s, 0:1]
                                       ).then_inc(squared, 1)
                        act.wait_ge(var_ready, t + 1)
                        act.activation(stat[:, s, 2:3], stat[:, s, 1:2], ACT.Sqrt).then_inc(rooted, 1)
                        act.wait_ge(turned, t + 3)
                        act.wait_ge(routed, t + 1)
                        act.activation(h2_t[:, s].rearrange("p k q -> p (k q)"), ps_h[:], ACT.Copy).then_inc(copied, 1)

            @block.vector
            def _(dve):
                dt = Tally(dve, step)
                dve.sem_inc(m_split, 2)
                dve.sem_inc(normed, 2)

                def split(t, s):
                    src = m_t[:, :, bass.ds(t * P, P)] if not isinstance(t, int) else m_t[:, :, t * P:(t + 1) * P]
                    dve.wait_ge(projected, t + 1)
                    dt.then_wait(dve.tensor_scalar(m_hi[:, s], src, 1.0, None, ALU.mult))
                    dve.tensor_tensor(m_lo[:, s], src, m_hi[:, s].bitcast(F32), ALU.subtract).then_inc(m_split, 1)

                def residual(t, s, i):
                    dve.wait_ge(projected, t + 3)
                    dve.wait_ge(stored[s], 32 * i + 32)
                    dt.then_wait(dve.tensor_tensor(x1[:, s], ps_o[:, s], g1_row[:], ALU.mult))
                    dve.wait_ge(xt_in[s], 16 * i + 16)
                    dve.tensor_tensor(x1[:, s], x1[:, s], x_in[:, s], ALU.add).then_inc(x1_ready, 1)
                    dve.wait_ge(squared, t + 1)
                    st = [stat[:, s, x:x + 1] for x in range(5)]
                    dve.tensor_scalar(st[1], st[0], 1.0 / D, EPS, ALU.mult, ALU.add).then_inc(var_ready, 1)
                    inverse_root(dve, dt, lambda: dve.wait_ge(rooted, t + 1), st[1], st[2], st[3], st[4])
                    dve.wait_ge(turned, t + 1)
                    dt.then_wait(dve.scalar_tensor_tensor(out=h2[:, s], in0=x1[:, s], scalar=st[3], in1=scale_row[:],
                                                          op0=ALU.mult, op1=ALU.mult))
                    dve.tensor_tensor(h2[:, s], h2[:, s], shift_row[:], ALU.add).then_inc(normed, 1)

                split(0, 0)
                for k in range(KD):
                    dve.wait_ge(wo_hi, k + 1)
                    dve.tensor_tensor(w_lo[:, k, :], w_raw[:, k, :], w_hi[:, k, :].bitcast(F32), ALU.subtract
                                      ).then_inc(wo_lo, 1)
                dve.wait_ge(rows_in, 5 * 16)
                dt.then_wait(dve.scalar_tensor_tensor(out=scale_row[:], in0=scale_row[:], scalar=1.0, in1=gain_row[:],
                                                      op0=ALU.add, op1=ALU.mult))
                dve.sem_inc(gain_used, 1)
                with dve.Fori(0, TT // 2 - 1) as i:
                    dt.enter(i, 2 * 8)
                    for s in range(2):
                        split(2 * i + s + 1, 1 - s)
                        residual(2 * i + s, s, i)
                    dt.leave(TT // 2 - 1)
                split(TT - 1, 1)
                residual(TT - 2, 0, TT // 2 - 1)
                residual(TT - 1, 1, TT // 2 - 1)


CHUNKS = [(c, min(512, FF - c)) for c in range(0, FF, 512)]
UNITS = []
for _c, (_at, _w) in enumerate(CHUNKS):
    _parts = 2 * _w // 512
    UNITS += [(name, _c, q, _parts) for name in ("gate", "up") for q in range(_parts)]
    if _c:
        UNITS += [("down", _c - 1, q, 2) for q in range(2)]
UNITS += [("down", len(CHUNKS) - 1, q, _parts) for q in range(_parts)]
N_U = len(UNITS)
RAW = 11
PARTS = 3
assert N_U % RAW == 0 and N_U % PARTS == 0
LAST_OF = {(name, c): u for u, (name, c, q, parts) in enumerate(UNITS) if q == parts - 1}


def unit_source(a, e, u):
    name, c, q, parts = UNITS[u]
    at, w = CHUNKS[c]
    if name == "down":
        f = at // P + 2 * q
        return a["w_down"].rearrange("e (f p) n -> e p f n", p=P)[e][:, f:f + 2, :]
    rows = KD // parts
    return a["w_" + name].rearrange("e (k p) n -> e p k n", p=P)[e][:, rows * q:rows * (q + 1), at:at + w]


def unit_view(slot, u):
    name, c, _, parts = UNITS[u]
    return slot.rearrange("p (r n) -> p r n", r=2 if name == "down" else KD // parts)


def choose(nc, sems, a, keep, logits, raw, raw_in, gate_col, idx_col):
    ident = keep["ident"]
    with ExitStack() as ctx:
        m = Maker(nc, ctx, "choose_")
        lg = logits[:, 0:TT * E_N].rearrange("p (t e) -> p t e", e=E_N)
        top, total, inv = (m.sb(n, [P, TT]) for n in ("top", "total", "inv"))
        aff = m.sb("aff", [P, TT, E_N])
        rows = m.sb("rows", [E_N, T])
        best = m.sb("best", [E_N, CAP])
        where = m.sb("where", [E_N, CAP], U32)
        where_f = m.sb("where_f", [E_N, CAP])
        ps_r = m.psum("ps_r", [P, T])
        ps_c = m.psum("ps_c", [P, 2, 512])
        step, shifted, exped, aff_ready, aff_turned, best_ready, best_turned = (
            sems(n) for n in ("g_dve_step", "shifted", "exped", "aff_ready", "aff_turned", "best_ready", "best_turned"))

        with nc.Block() as block:

            @block.sync
            def _(sp):
                for u in range(RAW):
                    sp.dma_start(unit_view(raw[:, u], u), unit_source(a, 0, u)).then_inc(raw_in[u], 16)

            @block.scalar
            def _(act):
                act.wait_ge(shifted, 1)
                act.activation(aff[:], aff[:], ACT.Exp).then_inc(exped, 1)

            @block.tensor
            def _(pe):
                pe.wait_ge(aff_ready, 1)
                for t in range(TT):
                    mm = pe.transpose(ps_r[0:E_N, t * P:(t + 1) * P], aff[:, t, :], ident[:])
                mm.then_inc(aff_turned, 1)
                pe.wait_ge(best_ready, 1)
                pe.transpose(ps_c[:, 0, 0:E_N], best[:], ident[0:E_N, 0:E_N])
                pe.transpose(ps_c[:, 1, 0:E_N], where_f[:], ident[0:E_N, 0:E_N]).then_inc(best_turned, 1)

            @block.vector
            def _(dve):
                dt = Tally(dve, step)

                def wide(v):
                    return v[:].unsqueeze(2).broadcast_to([P, TT, E_N])

                dt.then_wait(dve.reduce_max(top[:], lg, AX_X))
                dve.tensor_tensor(aff[:], lg, wide(top), ALU.subtract).then_inc(shifted, 1)
                dve.wait_ge(exped, 1)
                dt.then_wait(dve.reduce_sum(total[:], aff[:], AX_X))
                dt.then_wait(dve.reciprocal(inv[:], total[:]))
                dve.tensor_tensor(aff[:], aff[:], wide(inv), ALU.mult).then_inc(aff_ready, 1)
                dve.wait_ge(aff_turned, 1)
                dt.then_wait(dve.tensor_copy(rows[:], ps_r[0:E_N, :]))
                for r in range(CAP // 8):
                    eight = slice(8 * r, 8 * r + 8)
                    dt.then_wait(dve.max(best[:, eight], rows[:]))
                    dt.inc(dve.max_index(where[:, eight], best[:, eight], rows[:]))
                    if r + 1 < CAP // 8:
                        dt.inc(dve.match_replace(rows[:], best[:, eight], rows[:], -1.0))
                    dt.wait()
                dve.tensor_copy(where_f[:], where[:]).then_inc(best_ready, 1)
                dve.wait_ge(best_turned, 1)
                dve.tensor_copy(gate_col[:], ps_c[:, 0, 0:E_N])
                dve.tensor_copy(idx_col[:], ps_c[:, 1, 0:E_N])


def experts(nc, sems, a, keep, raw, raw_in, gate_col, idx_col):
    ident = keep["ident"]
    with ExitStack() as ctx:
        m = Maker(nc, ctx, "moe_")
        w_hi, w_lo = m.sb("w_hi", [P, PARTS, 2048], F32R), m.sb("w_lo", [P, PARTS, 2048], F32R)
        xe = m.sb("xe", [P, D])
        xt_hi, xt_lo = m.sb("xt_hi", [P, KD, P], F32R), m.sb("xt_lo", [P, KD, P], F32R)
        sl = m.sb("sl", [P, 2, 512])
        h = m.sb("h", [P, 2, 512])
        ht_hi, ht_lo = m.sb("ht_hi", [P, 2, 4, P], F32R), m.sb("ht_lo", [P, 2, 4, P], F32R)
        y = m.sb("y", [P, D])
        g2_row = m.sb("g2_row", [P, D])
        ps_gate = m.psum("ps_gate", [P, 2, 512])
        ps_up = m.psum("ps_up", [P, 2, 512])
        ps_y = m.psum("ps_y", [P, D])
        ps_h = m.psum("ps_h", [P, 512])
        ps_x = m.psum("ps_x", [P, 512])

        hi_ready, lo_ready, used, silu_done, multiplied, turned_h, h_high, h_parts = (
            sems(n) for n in ("m_hi_ready", "m_lo_ready", "used_units", "silu_done", "multiplied", "turned_h", "h_high",
                              "h_parts"))
        turned_x, x_high, x_parts, gathered, y_ready, y_free, scattered, g2_in = (
            sems(n) for n in ("turned_x", "x_high", "x_parts", "gathered", "moe_y_ready", "y_free", "scattered", "g2_in"))
        N_C = len(CHUNKS)

        def after(u):
            out = []
            for c in range(N_C):
                if min(LAST_OF["gate", c] + 2, N_U - 1) == u:
                    out.append(("silu", c))
                if min(LAST_OF["up", c] + 2, N_U - 1) == u:
                    out.append(("multiply", c))
            for c in range(N_C - 1):
                if LAST_OF["gate", c + 1] + 2 == u:
                    out.append(("turned", c))
            if LAST_OF["up", N_C - 1] + 2 == u:
                out.append(("turned_x", 0))
            if u == N_U - 1:
                out += [("turned", N_C - 1), ("turned_x", 1)]
            return out

        with nc.Block() as block:

            @block.sync
            def _(sp):
                sp.dma_start(g2_row[:], bass.AP(a["mod_d"].tensor, 5 * D, [[0, P], [1, D]])).then_inc(g2_in, 16)

                def load(e, e_of, u):
                    sp.wait_ge(lo_ready, N_U * e_of + u + 1)
                    sp.dma_start(unit_view(raw[:, u % RAW], u), unit_source(a, e_of, u)).then_inc(raw_in[u % RAW], 16)

                with sp.Fori(0, E_N - 1) as e:
                    for u in range(RAW, N_U):
                        load(e, e, u)
                    for u in range(RAW):
                        load(e, e + 1, u)
                for u in range(RAW, N_U):
                    load(E_N - 1, E_N - 1, u)

            @block.gpsimd
            def _(pool):
                h2, acc = a["h2_d"], a["acc_d"]

                def gather(e):
                    if e:
                        pool.wait_ge(turned_x, 2 * e)
                    pool.indirect_dma_start(xe[:], None, h2, bass.IndirectOffsetOnAxis(ap=idx_col[:, min(e, E_N - 1):min(e, E_N - 1) + 1], axis=0)
                                            ).then_inc(gathered, 16)

                pool.sem_inc(y_free, 1)
                gather(0)
                for e in range(E_N):
                    gather(e + 1)
                    pool.wait_ge(y_ready, e + 2)
                    pool.indirect_dma_start(acc, bass.IndirectOffsetOnAxis(ap=idx_col[:, e:e + 1], axis=0), y[:], None,
                                            compute_op=ALU.add).then_inc(scattered, 16)
                    pool.wait_ge(scattered, 16 * e + 16)
                    pool.sem_inc(y_free, 1)

            @block.tensor
            def _(pe):
                pe.sem_inc(used, 3)
                pe.sem_inc(turned_h, 1)

                def turn_x(half, count):
                    pe.wait_ge(x_parts, count + 1)
                    for k in range(4):
                        at = (4 * half + k) * P
                        mm = pe.transpose(ps_x[:, k * P:(k + 1) * P], xe[:, at:at + P], ident[:])
                    mm.then_inc(turned_x, 1)

                def turn_h(e, c):
                    pe.wait_ge(multiplied, N_C * e + c + 3)
                    pe.wait_ge(h_parts, N_C * e + c + 1)
                    for b in range(CHUNKS[c][1] // P):
                        mm = pe.transpose(ps_h[:, b * P:(b + 1) * P], h[:, c % 2, b * P:(b + 1) * P], ident[:])
                    mm.then_inc(turned_h, 1)

                def unit(e, u):
                    name, c, q, parts = UNITS[u]
                    w = CHUNKS[c][1]
                    hi, lo = (unit_view(x[:, u % PARTS], u) for x in (w_hi, w_lo))
                    pe.wait_ge(lo_ready, N_U * e + u + 1 + RAW)
                    if name == "down":
                        if q == 0:
                            pe.wait_ge(h_parts, N_C * e + c + 2)
                        if q == 0 and c == 0:
                            pe.wait_ge(y_ready, e + 1)
                        for r in range(2):
                            f = 2 * q + r
                            ht = [x[:, c % 2, f, :] for x in (ht_hi, ht_lo)]
                            first, last = c == 0 and f == 0, c == N_C - 1 and f == w // P - 1
                            for x, (hp, wp) in enumerate(((ht[0], hi), (ht[0], lo), (ht[1], hi))):
                                for n in range(2):
                                    mm = pe.matmul(ps_y[:, n * 512:(n + 1) * 512], hp, wp[:, r, n * 512:(n + 1) * 512],
                                                   start=(first and x == 0), stop=(last and x == 2))
                    else:
                        ps = (ps_gate if name == "gate" else ps_up)[:, c % 2, 0:w]
                        if q == 0:
                            pe.wait_ge(multiplied, N_C * e + c + 1)
                        rows = KD // parts
                        for r in range(rows):
                            k = rows * q + r
                            for x, (hp, wp) in enumerate(((xt_hi, hi), (xt_hi, lo), (xt_lo, hi))):
                                mm = pe.matmul(ps, hp[:, k, :], wp[:, r, :], start=(k == 0 and x == 0),
                                               stop=(k == KD - 1 and x == 2))
                    mm.then_inc(used, 1)

                pe.wait_ge(gathered, 16)
                turn_x(0, 0)
                turn_x(1, 1)
                with pe.Fori(0, E_N) as e:
                    pe.wait_ge(x_parts, 2 * e + 3)
                    for u in range(N_U):
                        unit(e, u)
                        for c in range(N_C - 1):
                            if LAST_OF["gate", c + 1] == u:
                                turn_h(e, c)
                        if LAST_OF["up", N_C - 1] == u:
                            pe.wait_ge(gathered, 16 * e + 32)
                            turn_x(0, 2 * e + 2)
                        if LAST_OF["down", N_C - 2] == u:
                            turn_h(e, N_C - 1)
                            turn_x(1, 2 * e + 3)

            @block.scalar
            def _(act):
                act.sem_inc(silu_done, 2)

                def high_x(count):
                    half = count[1]
                    act.wait_ge(turned_x, count[0] + 1)
                    act.activation(xt_hi[:, 4 * half:4 * half + 4, :], ps_x[:].rearrange("p (k q) -> p k q", q=P),
                                   ACT.Copy).then_inc(x_high, 1)

                high_x((0, 0))
                high_x((1, 1))
                with act.Fori(0, E_N) as e:
                    for u in range(N_U):
                        act.wait_ge(raw_in[u % RAW], 48 * e + 16 * (u // RAW) + 16)
                        act.wait_ge(used, N_U * e + u + 1)
                        act.activation(w_hi[:, u % PARTS], raw[:, u % RAW], ACT.Copy).then_inc(hi_ready, 1)
                        for what, c in after(u):
                            if what == "silu":
                                w = CHUNKS[c][1]
                                act.wait_ge(used, N_U * e + LAST_OF["gate", c] + 1 + 3)
                                act.activation(sl[:, c % 2, 0:w], ps_gate[:, c % 2, 0:w], ACT.Silu
                                               ).then_inc(silu_done, 1)
                            elif what == "turned":
                                n = CHUNKS[c][1] // P
                                act.wait_ge(turned_h, N_C * e + c + 2)
                                act.activation(ht_hi[:, c % 2, 0:n], ps_h[:, 0:n * P].rearrange(
                                    "p (k q) -> p k q", q=P), ACT.Copy).then_inc(h_high, 1)
                            elif what == "turned_x":
                                high_x((2 * e + 2 + c, c))

            @block.vector
            def _(dve):
                dve.sem_inc(lo_ready, RAW)
                dve.sem_inc(h_parts, 1)
                dve.sem_inc(x_parts, 1)
                dve.sem_inc(multiplied, 2)
                dve.sem_inc(y_ready, 1)

                def low_x(count, half):
                    dve.wait_ge(x_high, count + 1)
                    view = xt_lo[:, 4 * half:4 * half + 4, :]
                    dve.tensor_tensor(view, ps_x[:].rearrange("p (k q) -> p k q", q=P),
                                      xt_hi[:, 4 * half:4 * half + 4, :].bitcast(F32), ALU.subtract
                                      ).then_inc(x_parts, 1)

                low_x(0, 0)
                low_x(1, 1)
                dve.wait_ge(g2_in, 16)
                with dve.Fori(0, E_N) as e:
                    for u in range(N_U):
                        dve.wait_ge(hi_ready, N_U * e + u + 1)
                        dve.tensor_tensor(w_lo[:, u % PARTS], raw[:, u % RAW], w_hi[:, u % PARTS].bitcast(F32),
                                          ALU.subtract).then_inc(lo_ready, 1)
                        for what, c in after(u):
                            if what == "multiply":
                                w = CHUNKS[c][1]
                                dve.wait_ge(silu_done, N_C * e + c + 3)
                                dve.wait_ge(used, N_U * e + LAST_OF["up", c] + 1 + 3)
                                dve.tensor_tensor(h[:, c % 2, 0:w], sl[:, c % 2, 0:w], ps_up[:, c % 2, 0:w], ALU.mult
                                                  ).then_inc(multiplied, 1)
                            elif what == "turned":
                                n = CHUNKS[c][1] // P
                                dve.wait_ge(h_high, N_C * e + c + 1)
                                dve.tensor_tensor(ht_lo[:, c % 2, 0:n], ps_h[:, 0:n * P].rearrange(
                                    "p (k q) -> p k q", q=P), ht_hi[:, c % 2, 0:n].bitcast(F32), ALU.subtract
                                    ).then_inc(h_parts, 1)
                            elif what == "turned_x":
                                low_x(2 * e + 2 + c, c)
                    dve.wait_ge(used, N_U * e + N_U + 3)
                    dve.wait_ge(y_free, e + 1)
                    dve.scalar_tensor_tensor(out=y[:], in0=ps_y[:], scalar=gate_col[:, bass.ds(e, 1)], in1=g2_row[:],
                                             op0=ALU.mult, op1=ALU.mult).then_inc(y_ready, 1)


def last_norm(nc, sems, a, out):
    with ExitStack() as ctx:
        m = Maker(nc, ctx, "last_")
        x = m.sb("x", [P, TT, D])
        o = m.sb("o", [P, TT, D])
        gain = m.sb("gain", [P, D])
        squares = m.sb("squares", [P, D])
        ss, var, root, inv, tmp = (m.sb(n, [P, TT]) for n in ("ss", "var", "root", "inv", "tmp"))
        GROUP = TT // 2
        x_in = [sems(f"acc_in{g}") for g in range(2)]
        gain_in, squared, var_ready, rooted, step, out_ready, stored = (
            sems(n) for n in ("gain_in", "h_squared", "h_var_ready", "h_rooted", "h_dve_step", "out_ready", "out_stored"))

        with nc.Block() as block:

            @block.sync
            def _(sp):
                src, dst = a["acc_d"].rearrange("(t p) d -> p t d", p=P), out[0].rearrange("(t p) d -> t p d", p=P)
                for g in range(2):
                    for t in range(g * GROUP, (g + 1) * GROUP, 2):
                        sp.dma_start(x[:, t:t + 2], src[:, t:t + 2]).then_inc(x_in[g], 16)
                sp.dma_start(gain[:], bass.AP(a["final_g"].tensor, 0, [[0, P], [1, D]])).then_inc(gain_in, 16)
                for t in range(TT):
                    sp.wait_ge(out_ready, t + 1)
                    sp.dma_start(dst[t], o[:, t]).then_inc(stored, 16)
                sp.wait_ge(stored, 16 * TT)

            @block.scalar
            def _(act):
                for g in range(2):
                    tiles = slice(g * GROUP, (g + 1) * GROUP)
                    act.wait_ge(x_in[g], 16 * GROUP // 2)
                    for t in range(g * GROUP, (g + 1) * GROUP):
                        if t:
                            act.wait_ge(squared, t)
                        act.activation(squares[:], x[:, t], ACT.Square, accum_out=ss[:, t:t + 1]).then_inc(squared, 1)
                    act.wait_ge(var_ready, g + 1)
                    act.activation(root[:, tiles], var[:, tiles], ACT.Sqrt).then_inc(rooted, 1)

            @block.vector
            def _(dve):
                dt = Tally(dve, step)
                for g in range(2):
                    tiles = slice(g * GROUP, (g + 1) * GROUP)
                    dve.wait_ge(squared, (g + 1) * GROUP)
                    dve.tensor_scalar(var[:, tiles], ss[:, tiles], 1.0 / D, EPS, ALU.mult, ALU.add).then_inc(var_ready, 1)
                    inverse_root(dve, dt, lambda: dve.wait_ge(rooted, g + 1), var[:, tiles], root[:, tiles],
                                 inv[:, tiles], tmp[:, tiles])
                    dve.wait_ge(gain_in, 16)
                    for t in range(g * GROUP, (g + 1) * GROUP):
                        dve.scalar_tensor_tensor(out=o[:, t], in0=x[:, t], scalar=inv[:, t:t + 1], in1=gain[:],
                                                 op0=ALU.mult, op1=ALU.mult).then_inc(out_ready, 1)


def program(nc, a, out):
    with ExitStack() as ctx:
        m = Maker(nc, ctx)
        sems = m.sem
        for name, shape in (("mod_d", (2, 6 * D)), ("hidden_d", (FC, T)), ("u_d", (3 * HY, T)), ("qk_d", (2 * HY, W)), ("g_d", (2 * D, T)),
                            ("acc_d", (T, D)), ("h2_d", (T, D))):
            a[name] = nc.dram_tensor(name, shape, F32, kind="Internal").ap()
        keep = {"ident": m.sb("identity", [P, P]), "par": m.sb("par", [P, N_PAR]),
                "c_silu": m.sb("c_silu", [P, KD, 2])}
        with ExitStack() as mixer:
            with ExitStack() as values:
                with ExitStack() as projection:
                    n = Maker(nc, projection)
                    keep["h_hi"] = n.sb("h_hi", [P, KD, W], F32R)
                    keep["h_lo"] = n.sb("h_lo", [P, KD, W], F32R)
                    keep["w_in"] = n.sb("w_in", [P, 2, KD, UNIT])
                    keep["w_in_sems"] = [sems(f"w_in{s}") for s in range(2)]
                    modulate_and_norm(nc, sems, a, keep)
                    v_tok = Maker(nc, values).sb("v_tok", [P, NT, 512], side="right")
                    project(nc, sems, a, keep, v_tok)
                n = Maker(nc, mixer)
                na_t = n.sb("na_t", [P, 4, T])
                keep["w3"] = n.sb("w3", [P, 4 * HY])
                keep["h2"] = n.sb("h2", [P, T])
                keep["dft"] = n.sb("dft", [P, 2, 4, P])
                keep["idft"] = n.sb("idft", [P, 4, BLK])
                keep["hyena_in"] = sems("hyena_in")
                attend(nc, sems, a, keep, v_tok, na_t)
            y_t = n.sb("y_t", [P, 4, T])
            hyena(nc, sems, a, keep, y_t)
            merged = ExitStack()
            m_t = Maker(nc, merged).sb("m_t", [P, KD, T], side="right")
            merge(nc, sems, a, y_t, na_t, m_t)
        with ExitStack() as routing:
            logits = Maker(nc, routing).psum("logits", [P, 512])
            with merged:
                project_out(nc, sems, a, keep, m_t, logits)
            n = Maker(nc, ctx)
            gate_col = n.sb("gate_col", [P, E_N])
            idx_col = n.sb("idx_col", [P, E_N], U32)
            raw = n.sb("raw", [P, RAW, 2048])
            raw_in = [sems(f"raw_in{s}") for s in range(RAW)]
            choose(nc, sems, a, keep, logits, raw, raw_in, gate_col, idx_col)
        experts(nc, sems, a, keep, raw, raw_in, gate_col, idx_col)
        last_norm(nc, sems, a, out)


def laid_out(inputs):
    x = {k: np.asarray(v) for k, v in inputs.items()}
    arrays = {
        "x": x["x"][0], "ctx": x["ctx"][0], "c": x["c"][0], "c_ctx": x["c_ctx"],
        "w_mod": x["w_mod"][0], "b_mod": x["b_mod"][0], "norm1_g": x["norm1_g"].reshape(-1, P),
        "w_in": x["w_in"][0], "b_in": x["b_in"].reshape(-1, P),
        "hy_short_w": x["hy_short_w"].reshape(-1, P), "hy_short_b": x["hy_short_b"].reshape(-1, P),
        "hy_skip": x["hy_skip"].reshape(-1, P),
    }
    rpb = np.pad(x["na_rpb"][0], ((0, 0), (0, 0), (48, P - 48 - (2 * WIN_W - 1))))
    arrays["rpb"] = rpb[:, :, ::-1]
    col = np.arange(GRID_W)
    start = np.clip(col - WIN_W // 2, 0, GRID_W - WIN_W)[:, None]
    seen = (col[None, :] >= start) & (col[None, :] < start + WIN_W)
    arrays["na_mask"] = np.tile(np.where(seen, 0.0, NEG).astype(np.float32), (2, 1))
    arrays["filt_w1"], arrays["filt_w2"], arrays["filt_w3"] = (x["filt_w" + n][0] for n in "123")
    arrays["filt_cols"] = np.stack([x[n][0] for n in ("filt_freq", "filt_b1", "filt_b2")], axis=1)
    pos = np.arange(T, dtype=np.float32)
    t = pos / np.float32(T - 1)
    bands = np.linspace(1e-4, (FEMB - 1) // 2 - 1, (FEMB - 1) // 2, dtype=np.float32)
    ang = (np.float32(2.0 * math.pi) * pos / np.float32(T))[:, None] * bands[None, :]
    arrays["feats"] = np.concatenate([t[:, None], np.cos(ang), -np.sin(ang)], axis=1).astype(np.float32).T
    deltas = np.linspace(math.log(1e-2) / 1.5, math.log(1e-2) / 0.3, HY, dtype=np.float32)
    arrays["decay"] = np.exp(-t[:, None] * np.abs(deltas)[None, :]).astype(np.float32)
    f = 2 * np.arange(P)[None, :] + np.arange(2)[:, None]
    turn = np.arange(BLK)[:, None, None] * (f[None] + 0.5) * (2.0 * math.pi / (2 * BLK))
    planes = np.stack([np.cos(turn), -np.sin(turn)], axis=2)
    arrays["dft"] = planes.reshape(2, P, 4, P).transpose(1, 0, 2, 3).astype(np.float32)
    arrays["idft"] = (planes.reshape(BLK, 4, P).transpose(2, 1, 0) / BLK).astype(np.float32)
    arrays.update({k: x[k][0] for k in ("w_branch_hy", "w_branch_na", "w_out", "w_router", "w_gate", "w_up", "w_down")})
    arrays["norm2_g"], arrays["final_g"] = x["norm2_g"], x["final_g"].reshape(1, -1)
    arrays["ident"] = np.eye(P, dtype=np.float32)
    return {k: np.ascontiguousarray(v) for k, v in arrays.items()}


def kernel(**inputs):
    import concourse.bacc as bacc
    from concourse.bass_utils import run_bass_kernel_spmd as run

    nc = bacc.Bacc("TRN2", target_bir_lowering=False, num_devices=1)
    arrays = {"in_" + k: v for k, v in laid_out(inputs).items()}
    a = {k[3:]: nc.dram_tensor(k, v.shape, mybir.dt.from_np(v.dtype), kind="ExternalInput").ap()
         for k, v in arrays.items()}
    out = nc.dram_tensor("out", (1, T, D), F32, kind="ExternalOutput").ap()
    program(nc, a, out)
    return run(nc, [arrays], core_ids=[0]).results[0]["out"]
```
